# Optimizing a Trainium2 kernel written in Bass

```python
import math
import jax
import jax.numpy as jnp
from jax import lax
import numpy as np

D_MODEL = 1024
BATCH = 1
SEQ = 128
DEPTH = 2
DEC_BATCH = 1
DEC_SEQ = 512
PAST_LEN = 128

GRID_W = 64
HEAD_DIM = 64
N_DIR = 2
ATT_WIDTH = 3 * D_MODEL // 8
ATT_HEADS = ATT_WIDTH // HEAD_DIM
ATT_KV_HEADS = 2
ATT_GROUP = ATT_HEADS // ATT_KV_HEADS
KV_WIDTH = ATT_KV_HEADS * HEAD_DIM
WINDOW = 128
ATT_BLOCK = 128
ATT_SCALE = HEAD_DIM ** -0.5
ROPE_BASE = 10000.0
SSD_WIDTH = 3 * D_MODEL // 8
SSD_HEADS = SSD_WIDTH // HEAD_DIM
SSD_STATE = 64
SSD_GROUPS = 2
SSD_CONV = 5
SSD_CHUNK = 128
SSD_CONV_CH = SSD_WIDTH + 2 * SSD_GROUPS * SSD_STATE
RWKV_WIDTH = D_MODEL // 4
RWKV_HEADS = RWKV_WIDTH // HEAD_DIM
RWKV_W_RANK = 64
RWKV_A_RANK = 64
RWKV_G_RANK = 128
RWKV_COLS = 3 * RWKV_WIDTH + RWKV_W_RANK + RWKV_A_RANK + RWKV_G_RANK
RWKV_GN_EPS = 64e-5
RWKV_SPLITS = (RWKV_WIDTH, 2 * RWKV_WIDTH, 3 * RWKV_WIDTH, 3 * RWKV_WIDTH + RWKV_W_RANK, 3 * RWKV_WIDTH + RWKV_W_RANK + RWKV_A_RANK)
IN_SIZES = (ATT_WIDTH, KV_WIDTH, KV_WIDTH, SSD_WIDTH, SSD_CONV_CH, N_DIR * SSD_HEADS, RWKV_COLS)
IN_COLS = sum(IN_SIZES)
IN_SPLITS = tuple(sum(IN_SIZES[:i + 1]) for i in range(len(IN_SIZES) - 1))
FFN_HIDDEN = -(-8 * D_MODEL // (3 * 256)) * 256
DEEPNORM_ALPHA = (2 * DEPTH) ** 0.25
DEEPNORM_BETA = (8 * DEPTH) ** -0.25
LN_EPS = 1e-5

kernel_name = 'hybrid_flow_backbone_step'

def layer_norm(x, w, b):
    xf = x.astype(jnp.float32)
    mu = jnp.mean(xf, -1, keepdims=True)
    var = jnp.mean(jnp.square(xf - mu), -1, keepdims=True)
    return ((xf - mu) * lax.rsqrt(var + LN_EPS)).astype(x.dtype) * w + b

def adaln_modulation(cond, w_mod, b_mod):
    return (jax.nn.silu(cond) @ w_mod + b_mod)[:, None, :]

def two_way(t):
    return jnp.stack([t, t[:, ::-1]])

def orient(t):
    return jnp.stack([t[0], t[1][:, ::-1]])

def axial_rope(x):
    T = x.shape[1]
    rows = T // GRID_W
    row = jnp.repeat(jnp.arange(rows), GRID_W).astype(jnp.float32)
    col = jnp.tile(jnp.arange(GRID_W), rows).astype(jnp.float32)
    half = HEAD_DIM // 2
    inv_freq = 1.0 / (ROPE_BASE ** (jnp.arange(0, half, 2, dtype=jnp.float32) / half))

    def rotate(xa, pos):
        ang = pos[:, None] * inv_freq[None, :]
        cos = jnp.cos(ang)[None, :, None, :].astype(x.dtype)
        sin = jnp.sin(ang)[None, :, None, :].astype(x.dtype)
        x1, x2 = xa[..., : half // 2], xa[..., half // 2:]
        return jnp.concatenate([x1 * cos - x2 * sin, x2 * cos + x1 * sin], axis=-1)

    return jnp.concatenate([rotate(x[..., :half], row), rotate(x[..., half:], col)], axis=-1)

def context_attention(q, k, v, sink):
    B, S = q.shape[:2]
    nb = S // ATT_BLOCK
    qb = jnp.moveaxis(q.reshape(B, nb, ATT_BLOCK, ATT_KV_HEADS, ATT_GROUP, HEAD_DIM), 1, 0)
    sink_f = sink.astype(jnp.float32).reshape(1, ATT_KV_HEADS, ATT_GROUP, 1)
    vf = v.astype(jnp.float32)

    def one_block(qblk):
        s = jnp.einsum('bqhgd,bkhd->bhgqk', qblk, k, preferred_element_type=jnp.float32) * ATT_SCALE
        m = jnp.maximum(jnp.max(s, -1), sink_f)
        p = jnp.exp(s - m[..., None])
        den = jnp.sum(p, -1) + jnp.exp(sink_f - m)
        o = jnp.einsum('bhgqk,bkhd->bhgqd', p, vf) / den[..., None]
        return o.transpose(0, 3, 1, 2, 4)

    o = lax.map(one_block, qb)
    return jnp.moveaxis(o, 0, 1).reshape(B, S, ATT_WIDTH).astype(q.dtype)

def latent_attention(q, k, v, k_ctx, v_ctx, sink):
    B, T = q.shape[:2]
    nb = T // ATT_BLOCK
    qb = q.reshape(B, nb, ATT_BLOCK, ATT_KV_HEADS, ATT_GROUP, HEAD_DIM)

    def band(t):
        tp = jnp.pad(t, ((0, 0), (ATT_BLOCK, ATT_BLOCK), (0, 0), (0, 0)))
        tp = tp.reshape(B, nb + 2, ATT_BLOCK, ATT_KV_HEADS, HEAD_DIM)
        return jnp.concatenate([tp[:, :-2], tp[:, 1:-1], tp[:, 2:]], axis=2)

    kb, vb = band(k), band(v)
    blk = jnp.arange(nb)[:, None] * ATT_BLOCK
    q_pos = blk + jnp.arange(ATT_BLOCK)[None, :]
    k_pos = blk - ATT_BLOCK + jnp.arange(3 * ATT_BLOCK)[None, :]
    kp = k_pos[:, None, :]
    valid = (jnp.abs(q_pos[:, :, None] - kp) <= WINDOW) & (kp >= 0) & (kp < T)
    s_loc = jnp.einsum('bnqhgd,bnkhd->bnhgqk', qb, kb, preferred_element_type=jnp.float32) * ATT_SCALE
    s_loc = jnp.where(valid[None, :, None, None], s_loc, -jnp.inf)
    s_ctx = jnp.einsum('bnqhgd,bkhd->bnhgqk', qb, k_ctx, preferred_element_type=jnp.float32) * ATT_SCALE
    sink_f = sink.astype(jnp.float32).reshape(1, 1, ATT_KV_HEADS, ATT_GROUP, 1)
    m = jnp.maximum(jnp.maximum(jnp.max(s_loc, -1), jnp.max(s_ctx, -1)), sink_f)
    p_loc = jnp.exp(s_loc - m[..., None])
    p_ctx = jnp.exp(s_ctx - m[..., None])
    den = jnp.sum(p_loc, -1) + jnp.sum(p_ctx, -1) + jnp.exp(sink_f - m)
    o = (jnp.einsum('bnhgqk,bnkhd->bnhgqd', p_loc, vb.astype(jnp.float32))
         + jnp.einsum('bnhgqk,bkhd->bnhgqd', p_ctx, v_ctx.astype(jnp.float32))) / den[..., None]
    return o.transpose(0, 1, 4, 2, 3, 5).reshape(B, T, ATT_WIDTH).astype(q.dtype)

def centred_depthwise_conv(x, w, b):
    y = lax.conv_general_dilated(x, w[:, None, :].astype(x.dtype), window_strides=(1,),
                                 padding=[(SSD_CONV // 2, SSD_CONV // 2)],
                                 dimension_numbers=('NWC', 'WIO', 'NWC'),
                                 feature_group_count=x.shape[-1])
    return y + b

def segsum(a):
    L = a.shape[-1]
    cs = jnp.cumsum(a, axis=-1)
    diff = cs[..., :, None] - cs[..., None, :]
    return jnp.where(jnp.tril(jnp.ones((L, L), dtype=bool)), diff, -jnp.inf)

def ssd_chunked_scan(x, a, b, c, state0):
    B, T, H, P = x.shape
    nc = T // SSD_CHUNK
    x = x.reshape(B, nc, SSD_CHUNK, H, P)
    b = b.reshape(B, nc, SSD_CHUNK, H, -1)
    c = c.reshape(B, nc, SSD_CHUNK, H, -1)
    a = a.reshape(B, nc, SSD_CHUNK, H).transpose(0, 3, 1, 2)
    a_cum = jnp.cumsum(a, axis=-1)
    decay_in = jnp.exp(segsum(a))
    cb = jnp.einsum('bclhn,bcshn->bhcls', c, b)
    y_diag = jnp.einsum('bhcls,bcshp->bclhp', cb * decay_in, x)
    decay_to_end = jnp.exp(a_cum[..., -1:] - a_cum)
    chunk_states = jnp.einsum('bclhn,bhcl,bclhp->bchpn', b, decay_to_end, x)
    states = jnp.concatenate([state0[:, None], chunk_states], axis=1)
    chunk_decay = jnp.exp(segsum(jnp.pad(a_cum[..., -1], ((0, 0), (0, 0), (1, 0)))))
    states = jnp.einsum('bhzc,bchpn->bzhpn', chunk_decay, states)
    y_off = jnp.einsum('bclhn,bchpn,bhcl->bclhp', c, states[:, :-1], jnp.exp(a_cum))
    return (y_diag + y_off).reshape(B, T, H, P), states[:, -1]

def ssd_mixer(z, xbc, dt_raw, lp, state0):
    B, T, _ = z.shape
    f32 = jnp.float32
    xbc = jax.nn.silu(centred_depthwise_conv(xbc, lp['ssd_conv_w'], lp['ssd_conv_b'])).astype(f32)
    xs, bm, cm = jnp.split(xbc, [SSD_WIDTH, SSD_WIDTH + SSD_GROUPS * SSD_STATE], axis=-1)
    rep = SSD_HEADS // SSD_GROUPS
    xs = xs.reshape(B, T, SSD_HEADS, HEAD_DIM)
    bm = jnp.repeat(bm.reshape(B, T, SSD_GROUPS, SSD_STATE), rep, axis=2)
    cm = jnp.repeat(cm.reshape(B, T, SSD_GROUPS, SSD_STATE), rep, axis=2)
    dt = jnp.moveaxis(dt_raw.reshape(B, T, N_DIR, SSD_HEADS), 2, 0).astype(f32)
    dt = orient(jax.nn.softplus(dt + lp['ssd_dt_bias'][:, None, None, :].astype(f32)))
    a = -jnp.exp(lp['ssd_a_log'].astype(f32))
    x_s = two_way(xs) * dt[..., None]
    a_s = dt * a[:, None, None, :]
    y_s, fin = jax.vmap(ssd_chunked_scan)(x_s, a_s, two_way(bm), two_way(cm), state0.astype(f32))
    y = y_s[0] + y_s[1][:, ::-1] + lp['ssd_d'][:, None].astype(f32) * xs
    y = y.reshape(B, T, SSD_WIDTH) * jax.nn.silu(z.astype(f32))
    y = y * lax.rsqrt(jnp.mean(jnp.square(y), -1, keepdims=True) + LN_EPS) * lp['ssd_norm_w']
    return y.astype(z.dtype), fin

def bidir_token_shift(p):
    prev = jnp.pad(p, ((0, 0), (1, 0), (0, 0)))[:, :-1]
    nxt = jnp.pad(p, ((0, 0), (0, 1), (0, 0)))[:, 1:]
    return 0.5 * (prev + nxt)

def rwkv_mixer(p, lp, state0):
    B, T, _ = p.shape
    f32 = jnp.float32
    pf = p.astype(f32)
    pf = pf + lp['rwkv_mu'] * (bidir_token_shift(pf) - pf)
    r, k, v, wd, ad, gd = jnp.split(pf, RWKV_SPLITS, axis=-1)
    w_raw = lp['rwkv_w0'][:, None, None, :] + jnp.einsum('btr,drc->dbtc', jnp.tanh(wd), lp['rwkv_w_up'])
    decay = jnp.exp(-jnp.exp(-jax.nn.softplus(-w_raw) - 0.5))
    a = jax.nn.sigmoid(lp['rwkv_a0'][:, None, None, :] + jnp.einsum('btr,drc->dbtc', ad, lp['rwkv_a_up']))
    g = jax.nn.sigmoid(gd) @ lp['rwkv_g_up']

    def heads(t):
        return t.reshape(t.shape[:-1] + (RWKV_HEADS, HEAD_DIM))

    kk = heads(k * lp['rwkv_k_k'])
    kk = kk * lax.rsqrt(jnp.sum(kk * kk, -1, keepdims=True) + 1e-12)
    k_d = heads(k[None] * (1.0 + (a - 1.0) * lp['rwkv_k_a']))
    r_h, v_h = heads(r), heads(v)
    seq = (two_way(r_h), orient(heads(decay)), orient(k_d), two_way(v_h), two_way(kk), orient(heads(a)))
    seq = tuple(jnp.moveaxis(t, 2, 0) for t in seq)

    def step(S, inp):
        r_t, w_t, k_t, v_t, kk_t, a_t = inp
        sk = jnp.einsum('dbhvk,dbhk->dbhv', S, kk_t)
        S = (S * w_t[..., None, :] - sk[..., :, None] * (kk_t * a_t)[..., None, :]
             + v_t[..., :, None] * k_t[..., None, :])
        return S, jnp.einsum('dbhvk,dbhk->dbhv', S, r_t)

    fin, o = lax.scan(step, state0.astype(f32), seq)
    o = jnp.moveaxis(o, 0, 2)
    o = o[0] + o[1][:, ::-1]
    mu = jnp.mean(o, -1, keepdims=True)
    var = jnp.mean(jnp.square(o - mu), -1, keepdims=True)
    o = ((o - mu) * lax.rsqrt(var + RWKV_GN_EPS)).reshape(B, T, RWKV_WIDTH) * lp['rwkv_gn_w'] + lp['rwkv_gn_b']
    bonus = jnp.sum(jnp.sum(r_h[None] * k_d * lp['rwkv_r_k'], -1, keepdims=True), 0) * v_h
    y = (o + bonus.reshape(B, T, RWKV_WIDTH)) * g
    return y.astype(p.dtype), fin

def mixer_forward(h, lp, ctx_cache):
    B, T, _ = h.shape
    q, k, v, z, xbc, dt_raw, rw = jnp.split(h @ lp['w_in'], IN_SPLITS, axis=-1)
    q = q.reshape(B, T, ATT_HEADS, HEAD_DIM)
    k = k.reshape(B, T, ATT_KV_HEADS, HEAD_DIM)
    v = v.reshape(B, T, ATT_KV_HEADS, HEAD_DIM)
    if ctx_cache is None:
        att = context_attention(q, k, v, lp['attn_sink'])
        ssd0 = jnp.zeros((N_DIR, B, SSD_HEADS, HEAD_DIM, SSD_STATE), jnp.float32)
        rwkv0 = jnp.zeros((N_DIR, B, RWKV_HEADS, HEAD_DIM, HEAD_DIM), jnp.float32)
    else:
        k_ctx, v_ctx, ssd_ctx, rwkv_ctx = ctx_cache
        att = latent_attention(axial_rope(q), axial_rope(k), v, k_ctx, v_ctx, lp['attn_sink'])
        ssd0 = jnp.moveaxis(ssd_ctx, 1, 0)
        rwkv0 = jnp.moveaxis(rwkv_ctx, 1, 0)
    y_ssd, ssd_fin = ssd_mixer(z, xbc, dt_raw, lp, ssd0)
    y_rwkv, rwkv_fin = rwkv_mixer(rw, lp, rwkv0)
    out = jnp.concatenate([att, y_ssd, y_rwkv], axis=-1) @ lp['w_out']
    if ctx_cache is None:
        return out, (k, v, jnp.moveaxis(ssd_fin, 0, 1), jnp.moveaxis(rwkv_fin, 0, 1))
    return out, None

def swiglu_ffn(h, w_in, w_out):
    gate, up = jnp.split(h @ w_in, 2, axis=-1)
    return (jax.nn.silu(gate) * up) @ w_out

def trunk_layer(x, mod, lp, ctx_cache):
    shift1, scale1, gate1, shift2, scale2, gate2 = jnp.split(mod, 6, axis=-1)
    mix, ctx_tensors = mixer_forward(x * (1.0 + scale1) + shift1, lp, ctx_cache)
    x = layer_norm(DEEPNORM_ALPHA * x + gate1 * mix, lp['ln1_w'], lp['ln1_b'])
    ffn = swiglu_ffn(x * (1.0 + scale2) + shift2, lp['ffn_w_in'], lp['ffn_w_out'])
    x = layer_norm(DEEPNORM_ALPHA * x + gate2 * ffn, lp['ln2_w'], lp['ln2_b'])
    return x, ctx_tensors

def setup_inputs(seed: int = 0) -> dict:
    key = jax.random.key(seed)
    keys = iter(jax.random.split(key, 48))
    f32 = jnp.float32
    L = DEPTH

    def normal(shape, scale):
        return jax.random.normal(next(keys), shape, f32) * scale

    def uniform(shape, lo, hi):
        return jax.random.uniform(next(keys), shape, f32, lo, hi)

    dt0 = jnp.exp(uniform((L, N_DIR, SSD_HEADS), math.log(1e-3), math.log(1e-1)))
    return {
        'x_prompt': normal((BATCH, SEQ, D_MODEL), 1.0),
        'x_sample': normal((DEC_BATCH, DEC_SEQ, D_MODEL), 1.0),
        'cache_k': normal((DEC_BATCH, DEPTH, PAST_LEN, ATT_KV_HEADS, HEAD_DIM), 1.0),
        'cache_v': normal((DEC_BATCH, DEPTH, PAST_LEN, ATT_KV_HEADS, HEAD_DIM), 1.0),
        'state_ssd': normal((DEC_BATCH, DEPTH, N_DIR, SSD_HEADS, HEAD_DIM, SSD_STATE), 0.3),
        'state_rwkv': normal((DEC_BATCH, DEPTH, N_DIR, RWKV_HEADS, HEAD_DIM, HEAD_DIM), 0.3),
        'c': normal((DEC_BATCH, D_MODEL), 1.0),
        'c_ctx': normal((D_MODEL,), 1.0),
        'w_mod': normal((L, D_MODEL, 6 * D_MODEL), 0.5 * D_MODEL ** -0.5),
        'b_mod': normal((L, 6 * D_MODEL), 0.02),
        'w_in': normal((L, D_MODEL, IN_COLS), D_MODEL ** -0.5),
        'w_out': normal((L, D_MODEL, D_MODEL), DEEPNORM_BETA * D_MODEL ** -0.5),
        'attn_sink': normal((L, ATT_HEADS), 1.0),
        'ssd_conv_w': normal((L, SSD_CONV, SSD_CONV_CH), SSD_CONV ** -0.5),
        'ssd_conv_b': normal((L, SSD_CONV_CH), 0.02),
        'ssd_dt_bias': dt0 + jnp.log(-jnp.expm1(-dt0)),
        'ssd_a_log': jnp.log(uniform((L, N_DIR, SSD_HEADS), 1.0, 16.0)),
        'ssd_d': 1.0 + normal((L, SSD_HEADS), 0.1),
        'ssd_norm_w': 1.0 + normal((L, SSD_WIDTH), 0.02),
        'rwkv_mu': uniform((L, RWKV_COLS), 0.0, 1.0),
        'rwkv_w0': uniform((L, N_DIR, RWKV_WIDTH), -6.0, -1.0),
        'rwkv_w_up': normal((L, N_DIR, RWKV_W_RANK, RWKV_WIDTH), 0.1),
        'rwkv_a0': normal((L, N_DIR, RWKV_WIDTH), 0.1),
        'rwkv_a_up': normal((L, N_DIR, RWKV_A_RANK, RWKV_WIDTH), RWKV_A_RANK ** -0.5),
        'rwkv_g_up': normal((L, RWKV_G_RANK, RWKV_WIDTH), RWKV_G_RANK ** -0.5),
        'rwkv_k_k': 0.85 + normal((L, RWKV_WIDTH), 0.05),
        'rwkv_k_a': 1.0 + normal((L, RWKV_WIDTH), 0.05),
        'rwkv_r_k': normal((L, RWKV_HEADS, HEAD_DIM), 0.1),
        'rwkv_gn_w': 1.0 + normal((L, RWKV_WIDTH), 0.02),
        'rwkv_gn_b': normal((L, RWKV_WIDTH), 0.02),
        'ln1_w': 1.0 + normal((L, D_MODEL), 0.02),
        'ln1_b': normal((L, D_MODEL), 0.02),
        'ln2_w': 1.0 + normal((L, D_MODEL), 0.02),
        'ln2_b': normal((L, D_MODEL), 0.02),
        'ffn_w_in': normal((L, D_MODEL, 2 * FFN_HIDDEN), D_MODEL ** -0.5),
        'ffn_w_out': normal((L, FFN_HIDDEN, D_MODEL), DEEPNORM_BETA * FFN_HIDDEN ** -0.5),
    }

def reference(x_prompt, x_sample, cache_k, cache_v, state_ssd, state_rwkv, c, c_ctx,
              w_mod, b_mod, w_in, w_out, attn_sink, ssd_conv_w, ssd_conv_b, ssd_dt_bias,
              ssd_a_log, ssd_d, ssd_norm_w, rwkv_mu, rwkv_w0, rwkv_w_up, rwkv_a0, rwkv_a_up,
              rwkv_g_up, rwkv_k_k, rwkv_k_a, rwkv_r_k, rwkv_gn_w, rwkv_gn_b,
              ln1_w, ln1_b, ln2_w, ln2_b, ffn_w_in, ffn_w_out):
    xp, xs = x_prompt, x_sample
    k_list, v_list, ssd_list, rwkv_list = [], [], [], []
    for l in range(DEPTH):
        lp = {
            'w_in': w_in[l], 'w_out': w_out[l], 'attn_sink': attn_sink[l],
            'ssd_conv_w': ssd_conv_w[l], 'ssd_conv_b': ssd_conv_b[l], 'ssd_dt_bias': ssd_dt_bias[l],
            'ssd_a_log': ssd_a_log[l], 'ssd_d': ssd_d[l], 'ssd_norm_w': ssd_norm_w[l],
            'rwkv_mu': rwkv_mu[l], 'rwkv_w0': rwkv_w0[l], 'rwkv_w_up': rwkv_w_up[l],
            'rwkv_a0': rwkv_a0[l], 'rwkv_a_up': rwkv_a_up[l], 'rwkv_g_up': rwkv_g_up[l],
            'rwkv_k_k': rwkv_k_k[l], 'rwkv_k_a': rwkv_k_a[l], 'rwkv_r_k': rwkv_r_k[l],
            'rwkv_gn_w': rwkv_gn_w[l], 'rwkv_gn_b': rwkv_gn_b[l],
            'ln1_w': ln1_w[l], 'ln1_b': ln1_b[l], 'ln2_w': ln2_w[l], 'ln2_b': ln2_b[l],
            'ffn_w_in': ffn_w_in[l], 'ffn_w_out': ffn_w_out[l],
        }
        mod_ctx = adaln_modulation(c_ctx[None, :], w_mod[l], b_mod[l])
        xp, (k_c, v_c, s_ssd, s_rwkv) = trunk_layer(xp, mod_ctx, lp, None)
        k_list.append(k_c)
        v_list.append(v_c)
        ssd_list.append(s_ssd)
        rwkv_list.append(s_rwkv)
        mod_lat = adaln_modulation(c, w_mod[l], b_mod[l])
        xs, _ = trunk_layer(xs, mod_lat, lp, (cache_k[:, l], cache_v[:, l], state_ssd[:, l], state_rwkv[:, l]))
    new_cache_k = jnp.stack(k_list, axis=1)
    new_cache_v = jnp.stack(v_list, axis=1)
    new_state_ssd = jnp.stack(ssd_list, axis=1)
    new_state_rwkv = jnp.stack(rwkv_list, axis=1)
    return (xp, xs, new_cache_k, new_cache_v, new_state_ssd, new_state_rwkv)


_drawn_inputs = setup_inputs


def setup_inputs(seed=0):
    import zlib

    import numpy as np

    out = dict(_drawn_inputs(seed))
    spreads = {}
    factors = {'cache_k': 8.0,
     'cache_v': 8.0,
     'state_rwkv': 8.0,
     'attn_sink': 35.603,
     'ssd_d': 8.0,
     'ssd_norm_w': 32.542,
     'rwkv_r_k': 3.903,
     'rwkv_gn_w': 64.0,
     'rwkv_gn_b': 64.0}
    for name, (base, spread) in spreads.items():
        noise = np.random.default_rng([zlib.crc32(name.encode()), seed]).standard_normal(out[name].shape)
        drawn = base * np.exp(spread * noise) if base else spread * noise
        out[name] = jnp.asarray(drawn.astype(out[name].dtype))
    for name, factor in factors.items():
        out[name] = (out[name] * factor).astype(out[name].dtype)
    return out
```

```python
from contextlib import ExitStack

import numpy as np

import concourse.bass as bass
import concourse.mybir as mybir

ALU = mybir.AluOpType
ACT = mybir.ActivationFunctionType
F32 = mybir.dt.float32
AX = mybir.AxisListType

P = 128
D = 1024
KT = D // P
DEPTH = 2
CTX = 128
LAT = 512
TOK = CTX + LAT
NCH = TOK // P
GRID_W = 64
HD = 64
ROPE_BASE = 10000.0
ATT_H = 6
ATT_T = 3
SSD_H = 6
RW_H = 4
CONV = 5
FFN_T = 22
ALPHA = (2 * DEPTH) ** 0.25
LN_EPS = 1e-5
GN_EPS = 64e-5
SCALE = HD ** -0.5
NEG_BIG = -1e30
DECAY = float(np.exp(np.float32(-0.5)))

TQ, TK_, TV, TZ, TX, TB, TC, TR, TKK, TVV, TWA, TG = 0, 3, 4, 5, 8, 11, 12, 13, 15, 17, 19, 20
N_IN = 21
PW = TOK + 6
CTX0, LAT0 = 2, CTX + 4

SLOT = 8 * 256
RING = 4
MOD_T = 48
MOD_SLOTS = 24
MOD_FIRST = 8
IN_SLOTS, OUT_SLOTS, UP_SLOTS, DOWN_PAIRS, DOWN_PARTS = 11, 4, FFN_T, 4, 3
MOD_AFTER_IN = [2, 2, 2, 2, 2, 1, 1, 1, 1, 1, 1]
assert sum(MOD_AFTER_IN) == MOD_SLOTS - MOD_FIRST

VEC = {}
_n = 0
for _name, _cols in (("convw", CONV * 5), ("convb", 5), ("d", 3), ("normw", 3), ("mu", 8),
                     ("w0", 4), ("a0", 4), ("kk", 2), ("ka", 2), ("rk", 2), ("gnw", 2), ("gnb", 2),
                     ("ln1w", 8), ("ln1b", 8), ("ln2w", 8), ("ln2b", 8)):
    VEC[_name] = _n
    _n += _cols
NVEC = _n

CON = {}
_n = 0
for _name, _cols in (("ident", P), ("ones", P), ("blk", P), ("perm", P), ("incf", P), ("incb", P),
                     ("strf", P), ("strb", P), ("lvl", 7 * P), ("gmf", 2 * P), ("gmb", 2 * P),
                     ("bprev", P), ("bnext", P), ("cos", LAT), ("sin", LAT), ("reset", TOK), ("eps", 4)):
    CON[_name] = _n
    _n += _cols
NCON = _n

NROW = ATT_H + 4 * SSD_H
N_SMALL = 7


def stream_order():
    order = [("mod", 0, i) for i in range(MOD_FIRST)]
    for l in range(DEPTH):
        m = MOD_FIRST
        for i in range(IN_SLOTS):
            order.append(("in", l, i))
            for _ in range(MOD_AFTER_IN[i]):
                order.append(("mod", l, m))
                m += 1
        order += [("out", l, i) for i in range(OUT_SLOTS)]
        for i in range(UP_SLOTS):
            order.append(("up", l, i))
            if l + 1 < DEPTH and i % 2 == 0 and i // 2 < MOD_FIRST:
                order.append(("mod", l + 1, i // 2))
        order += [("down", l, i) for i in range(DOWN_PAIRS * DOWN_PARTS)]
    return order


SCR_SIZE = 12200


def place(*sizes):
    at, out = 0, {}
    for name, size in sizes:
        out[name] = at
        at += size
    assert at <= SCR_SIZE, at
    return out


SA_ = place(("vt", 640), ("e", 2048), ("et", 2048), ("osb", 384), ("rot", 1024), ("nm", 30), ("mx", 30),
            ("sum", 30), ("es", 30), ("den", 30), ("nms", 30))
SS_ = place(("xb", 2560), ("cs0", 384), ("cs", 1536), ("sp", 1920), ("ea", 768), ("g", 1536), ("cbm", 512),
            ("xd", 768), ("t1", 768), ("y", 384), ("small", 900))
SR_ = place(("ar", 2560), ("gb", 2048), ("gk", 2048), ("m", 1024), ("mt", 1024), ("x", 1024),
            ("tok", 1024), ("s", 256), ("s0", 256), ("small", 160))
ST_ = place(("ar", 2560), ("sw", 2560), ("sa", 2560), ("kk", 1280), ("l", 640), ("t1", 640), ("t2", 640),
            ("kd", 1280))


class Track:

    def __init__(self, eng, own):
        self.eng, self.own_sem, self.count, self.last = eng, own, {}, None

    def sig(self, ins, sem):
        ins.then_inc(sem, 1)
        self.count[id(sem)] = self.count.get(id(sem), 0) + 1
        self.last = (sem, self.count[id(sem)])

    def own(self, ins):
        self.sig(ins, self.own_sem)

    def hold(self):
        self.eng.wait_ge(*self.last)


def build(nc, stream, xin, consts, conds, bmods, vecs, rows, kctx, vctx, lora, gup, ssd0, rwkv0,
          y_out, k_out, v_out, ssd_out, rwkv_out):
    ctx = ExitStack()
    with ctx:
        def sb(name, shape):
            return ctx.enter_context(nc.sbuf_tensor(name, shape, F32))

        def sem(name):
            return ctx.enter_context(nc.semaphore(name))

        xt = sb("xt", [P, KT, TOK])
        h = sb("h", [P, KT, TOK])
        mix = h
        proj = sb("proj", [P, N_IN + 1, PW])
        ring = sb("ring", [P, RING, KT, 256])
        con = sb("con", [P, NCON])
        vc = sb("vc", [P, NVEC])
        bm = sb("bm", [P, DEPTH, MOD_T])
        row = sb("row", [P, NROW + ATT_H])
        kc = sb("kc", [P, CTX])
        vcx = sb("vcx", [P, P])
        lo = sb("lo", [P, 2, 256])
        gu = sb("gu", [P, 256])
        mod = sb("mod", [P, MOD_T, 2])
        cond = sb("cond", [P, KT, 2])
        dtr = sb("dtr", [P, NCH, 12])
        t2 = sb("t2", [P, 2, TOK])
        rstd = sb("rstd", [P, TOK])
        mus = sb("mus", [P, 24])
        dec = sb("dec", [P, 2, 4, NCH])
        init_rw = sb("init_rw", [P, 256])
        fin_rw = sb("fin_rw", [P, 256])
        scr = sb("scr", [P, SCR_SIZE])
        ps = ctx.enter_context(nc.psum_tensor("ps", [P, 8, 512], F32))
        psf = ps[:].rearrange("p b n -> p (b n)")
        pflat = proj[:].rearrange("p t n -> p (t n)")

        def C(name, n=P, j=0):
            a = CON[name] + j * n
            return con[:, a:a + n]

        def V(name, j=0, n=1):
            return vc[:, VEC[name] + j:VEC[name] + j + n]

        def pair(i):
            return psf[:, 1024 * i + 384:1024 * i + 1024]

        def bank(i, n=512, a=0):
            return ps[:, i, a:a + n]

        def S(where, name, n, a=0):
            a = where[name] + a
            return scr[:, a:a + n]

        def T(t):
            return proj[:, t, 0:TOK]

        def ch(t, c):
            return proj[:, t, P * c:P * c + P]

        s_const = sem("s_const")
        s_x = sem("s_x")
        s_small = sem("s_small")
        s_slot = [sem(f"s_slot{i}") for i in range(RING)]
        s_init = sem("s_init")
        s_out = sem("s_out")
        s_y = sem("s_y")
        s_pe = sem("s_pe")
        s_act = sem("s_act")
        s_dve = sem("s_dve")
        s_pool = sem("s_pool")
        s_bar = sem("s_bar")
        s_dense = sem("s_dense")
        s_free = [sem("s_free_a"), sem("s_free_a2"), sem("s_free_v")]
        s_cond = sem("s_cond")
        s_modps = sem("s_modps")
        s_mod = sem("s_mod")
        s_h = sem("s_h")
        s_res = sem("s_res")
        s_mu = sem("s_mu")
        s_cen = sem("s_cen")
        s_sq = sem("s_sq")
        s_var = sem("s_var")
        s_std = sem("s_std")
        s_ln = sem("s_ln")
        a_v = sem("a_v")
        a_vt = sem("a_vt")
        a_rot = sem("a_rot")
        a_rope = sem("a_rope")
        a_score = sem("a_score")
        a_max = sem("a_max")
        a_exp = sem("a_exp")
        a_tr = sem("a_tr")
        a_trsb = sem("a_trsb")
        a_pv = sem("a_pv")
        a_nms = sem("a_nms")
        a_es = sem("a_es")
        a_on = sem("a_on")
        a_ot = sem("a_ot")
        a_out = sem("a_out")
        c_conv = sem("c_conv")
        c_silu = sem("c_silu")
        c_dtx = sem("c_dtx")
        c_dte = sem("c_dte")
        c_a = sem("c_a")
        c_cum = sem("c_cum")
        c_ecum = sem("c_ecum")
        c_dtend = sem("c_dtend")
        c_tr = sem("c_tr")
        c_xb = sem("c_xb")
        c_xe = sem("c_xe")
        c_st = sem("c_st")
        c_cs = sem("c_cs")
        c_sp = sem("c_sp")
        c_cb = sem("c_cb")
        c_cbm = sem("c_cbm")
        c_rh = sem("c_rh")
        c_arg = sem("c_arg")
        c_ea = sem("c_ea")
        c_g = sem("c_g")
        c_xd = sem("c_xd")
        c_y = sem("c_y")
        c_ytok = sem("c_ytok")
        c_yt = sem("c_yt")
        c_yf = sem("c_yf")
        c_gate = sem("c_gate")
        c_sq = sem("c_sq")
        c_var = sem("c_var")
        c_std = sem("c_std")
        r_mu = sem("r_mu")
        r_sum = sem("r_sum")
        r_scl = sem("r_scl")
        r_shift = sem("r_shift")
        r_act = sem("r_act")
        r_wps = sem("r_wps")
        r_sig = sem("r_sig")
        r_gps = sem("r_gps")
        r_g = sem("r_g")
        r_ksq = sem("r_ksq")
        r_kps = sem("r_kps")
        r_kstd = sem("r_kstd")
        r_kk = sem("r_kk")
        r_cum = sem("r_cum")
        r_exp = sem("r_exp")
        r_kd = sem("r_kd")
        r_ops = sem("r_ops")
        r_bon = sem("r_bon")
        r_bps = sem("r_bps")
        r_bv = sem("r_bv")
        r_v = sem("r_v")
        r_vt = sem("r_vt")
        r_gmat = sem("r_gmat")
        r_gsb = sem("r_gsb")
        r_lvl = sem("r_lvl")
        r_mt0 = sem("r_mt0")
        r_m0ps = sem("r_m0ps")
        r_m0 = sem("r_m0")
        r_xps = sem("r_xps")
        r_xsb = sem("r_xsb")
        r_mps = sem("r_mps")
        r_msb = sem("r_msb")
        r_tkps = sem("r_tkps")
        r_tk = sem("r_tk")
        r_s0 = sem("r_s0")
        r_rps = sem("r_rps")
        r_rsb = sem("r_rsb")
        r_ups = sem("r_ups")
        r_nu = sem("r_nu")
        r_ops2 = sem("r_ops2")
        r_sps = sem("r_sps")
        r_osb = sem("r_osb")
        r_st = sem("r_st")
        r_osq = sem("r_osq")
        r_ovar = sem("r_ovar")
        r_ostd = sem("r_ostd")
        r_on = sem("r_on")
        r_otps = sem("r_otps")
        r_y = sem("r_y")

        order = stream_order()
        NS = len(order)
        D_IN, D_OUT, D_UP, D_DOWN = 0, 22, 30, 74
        N_DENSE = 82
        N_BAR = 6

        def barrier(eng, tr, n):
            tr.hold()
            eng.sem_inc(s_bar, 1)
            eng.wait_ge(s_bar, 4 * (n + 1))

        def freed(n):
            l, i = divmod(n, N_DENSE)
            if n % 2 == 0:
                return s_free[0], n // 2 + 1
            if D_UP <= i < D_DOWN:
                return s_free[2], l * FFN_T + (i - D_UP) // 2 + 1
            return s_free[1], (N_DENSE // 2 - FFN_T) * l + (i // 2 if i < D_UP else i // 2 - FFN_T) + 1

        def wait_pair_free(eng, n):
            if n >= 2:
                eng.wait_ge(*freed(n - 2))

        def padded(i):
            return TX <= i < N_IN

        RW_UNITS = [(d, hp) for d in range(2) for hp in range(2)]

        def op_blocks(which, d, hp):
            i = (4 if which else 0) + 2 * d + hp
            if i < 6:
                a = pflat[:, 1280 * i:1280 * i + 1280]
            else:
                a = S(SR_, "ar", 1280, 1280 * (i - 6))
            return a.rearrange("p (c n) -> p c n", c=NCH)

        VTOK = pflat[:, TKK * PW:TKK * PW + 1280].rearrange("p (c n) -> p c n", c=NCH)
        OTOK = pflat[:, TR * PW:TR * PW + 1280].rearrange("p (c n) -> p c n", c=NCH)

        def s0(d, hp):
            return S(SR_, "s0", HD, HD * (2 * d + hp))

        def lv_(d):
            return t2[:, d, 0:512]

        def xs(which, n, a):
            return S(SR_, "x", n, 512 * which + a)

        def lvl_count(l, i, d, j):
            return 14 * (NCH * l + i) + 2 * j + d + 1

        def x_count(l, i, d, j):
            return 12 * (NCH * l + i) + 2 * (j - 1) + d + 1

        def inv_count(l, i, d, j, turned):
            base = 22 * (NCH * l + i)
            return base + (20 + d + 1 if j == 6 else 4 * (j - 1) + 2 * d + turned + 1)

        used_by, tiles, mods, parts = [], 0, 0, 0
        for kind, l, i in order:
            if kind == "mod":
                mods += 1
                used_by.append((s_modps, mods))
            elif kind == "down":
                used_by.append((s_dense, N_DENSE * l + D_DOWN + 2 * (i // DOWN_PARTS) + 2))
            else:
                first = {"in": D_IN, "out": D_OUT, "up": D_UP}[kind]
                used_by.append((s_dense, N_DENSE * l + first + 2 * i + 2))

        block = ctx.enter_context(nc.Block())

        @block.sync
        def _(sp):
            sp.dma_start(con[:], consts).then_inc(s_const, 16)
            sp.dma_start(cond[:], conds).then_inc(s_const, 16)
            sp.dma_start(bm[:], bmods).then_inc(s_const, 16)
            for n in range(NS):
                if n == MOD_FIRST // 2:
                    sp.dma_start(xt[:], xin).then_inc(s_x, 16)
                if n >= RING:
                    sp.wait_ge(*used_by[n - RING])
                sp.dma_start(ring[:, n % RING].rearrange("p k n -> p (k n)"), stream[n])\
                  .then_inc(s_slot[n % RING], 16)
            for k in range(KT):
                sp.wait_ge(s_ln, 8 * (2 * DEPTH - 1) + k + 1)
                sp.dma_start(y_out[:, k], xt[:, k]).then_inc(s_y, 16)
            sp.wait_ge(s_y, 16 * KT)
            sp.wait_ge(s_out, 64 * DEPTH)

        @block.tensor
        def _(pe):
            tr = Track(pe, s_pe)
            mm = nc.tensor.matmul
            slot = [0]
            nbar = [0]

            def bar():
                barrier(pe, tr, nbar[0])
                nbar[0] += 1

            def take():
                n = slot[0]
                slot[0] += 1
                pe.wait_ge(s_slot[n % RING], 16 * (n // RING + 1))
                return ring[:, n % RING]

            def tp(out, in_):
                return nc.tensor.transpose(out, in_, C("ident"))

            def mod_slot(l, i):
                w = take()
                if i == 0:
                    if l:
                        pe.wait_ge(s_mod, 2 * l)
                for j in range(2):
                    for k in range(KT):
                        a = 2 * (2 * i + j)
                        ins = mm(bank(4, 2, a), w[:, k, P * j:P * j + P], cond[:, k, :],
                                 start=(k == 0), stop=(k == KT - 1))
                tr.sig(ins, s_modps)

            def dense(n, parts, rhs, first=None, used=()):
                wait_pair_free(pe, n)
                acc = pair(n % 2)
                ks = [(w, col, k, kk) for w, col, k0, kn in parts for k, kk in
                      ((k0 + q, q) for q in range(kn))]
                for i, (w, col, k, kk) in enumerate(ks):
                    if first is not None:
                        pe.wait_ge(s_h, first + k + 1)
                    for a, b in ((CTX, TOK), (0, CTX)):
                        ins = mm(acc[:, a:b], w[:, kk, col:col + P], rhs(k)[:, a:b],
                                 start=(i == 0), stop=(i == len(ks) - 1))
                tr.sig(ins, s_dense)

            pe.wait_ge(s_const, 48)
            pe.wait_ge(s_cond, 1)
            for i in range(MOD_FIRST):
                mod_slot(0, i)

            def norm(n):
                for k in range(KT):
                    pe.wait_ge(s_res, KT * n + k + 1)
                    for a, b in ((CTX, TOK), (0, CTX)):
                        ins = mm(pair(2)[:, a:b], C("ones"), xt[:, k, a:b], start=(k == 0),
                                 stop=(k == KT - 1))
                tr.sig(ins, s_mu)
                for k in range(KT):
                    pe.wait_ge(s_sq, KT * n + k + 1)
                    for a, b in ((CTX, TOK), (0, CTX)):
                        ins = mm(pair(3)[:, a:b], C("ones"), t2[:, k % 2, a:b], start=(k == 0),
                                 stop=(k == KT - 1))
                    tr.sig(ins, s_var)

            def attention(l):
                for c in range(NCH):
                    ins = tp(psf[:, P * c:P * c + P], ch(TV, c))
                tr.sig(ins, a_v)
                for t in range(4):
                    if t >= 2:
                        pe.wait_ge(a_rope, 4 * l + t - 1)
                    tr.sig(mm(bank(2 + t % 2), C("perm"), proj[:, TQ + t, CTX:TOK], start=True, stop=True),
                           a_rot)

                def keys(qb):
                    if qb == 0:
                        return []
                    n = qb - 1
                    return list(range(max(n - 1, 0), min(n + 1, 3) + 1))

                def scores(u):
                    qb, t = divmod(u, ATT_T)
                    if u == 0:
                        pe.wait_ge(a_vt, l + 1)
                        pe.wait_ge(a_rope, 4 * l + 4)
                    if u >= 2:
                        pe.wait_ge(a_exp, 15 * l + u - 1)
                    blocks = keys(qb)
                    for hh in range(2):
                        r = slice(HD * hh, HD * hh + HD)
                        b = 2 * (u % 2) + hh
                        q = ch(TQ + t, qb)[r]
                        own = kc[r, :] if qb else ch(TK_, 0)[r]
                        ins = mm(ps[:, b, 0:CTX], q, own, start=True, stop=True)
                        if blocks:
                            a = CTX + P * blocks[0]
                            ins = mm(ps[:, b, P:P + P * len(blocks)], q,
                                     proj[r, TK_, a:a + P * len(blocks)], start=True, stop=True)
                    tr.sig(ins, a_score)

                def turn(u):
                    qb, t = divmod(u, ATT_T)
                    pe.wait_ge(a_exp, 15 * l + u + 1)
                    if u:
                        pe.wait_ge(a_trsb, 15 * l + u)
                    for hh in range(2):
                        for j in range(1 + len(keys(qb))):
                            ins = tp(ps[:, 4 + hh, P * j:P * j + P],
                                     S(SA_, "e", P, 1024 * (u % 2) + 512 * hh + P * j))
                    tr.sig(ins, a_tr)

                def values(u):
                    qb, t = divmod(u, ATT_T)
                    pe.wait_ge(a_trsb, 15 * l + u + 1)
                    if t == 0 and qb:
                        pe.wait_ge(a_on, 5 * l + qb)
                    blocks = keys(qb)
                    for hh in range(2):
                        for j in range(1 + len(blocks)):
                            if j == 0:
                                v = vcx[:, HD * hh:HD * hh + HD] if qb else S(SA_, "vt", HD, HD * hh)
                            else:
                                v = S(SA_, "vt", HD, P * (1 + blocks[j - 1]) + HD * hh)
                            ins = mm(bank(6, HD, P * t + HD * hh),
                                     S(SA_, "et", P, 1024 * (u % 2) + 512 * hh + P * j), v,
                                     start=(j == 0), stop=(j == len(blocks)))
                    tr.sig(ins, a_pv)

                def out(qb):
                    pe.wait_ge(a_on, 5 * l + qb + 1)
                    if qb:
                        pe.wait_ge(a_out, 5 * l + qb)
                    for t in range(ATT_T):
                        ins = tp(bank(7, P, P * t), S(SA_, "osb", P, P * t))
                    tr.sig(ins, a_ot)

                scores(0)
                for u in range(15):
                    if u + 1 < 15:
                        scores(u + 1)
                    turn(u)
                    values(u)
                    if u % 3 == 0 and u:
                        out(u // 3 - 1)
                out(4)

            def ssd(l):
                pe.wait_ge(c_a, l + 1)
                sm = SS_["small"]
                af, ab = scr[:, sm:sm + 30], scr[:, sm + 30:sm + 60]
                mm(bank(4, 30, 0), C("incf"), af, start=True, stop=True)
                mm(bank(4, 30, 30), C("incb"), ab, start=True, stop=True)
                mm(bank(4, 30, 60), C("strb"), af, start=True, stop=True)
                mm(bank(4, 30, 90), C("strf"), ab, start=True, stop=True)
                ins = mm(bank(4, 60, 120), C("ones"), scr[:, sm:sm + 60], start=True, stop=True)
                tr.sig(ins, c_cum)
                for c in range(NCH):
                    if c == 0:
                        pe.wait_ge(c_silu, 5 * l + 5)
                    if c >= 2:
                        pe.wait_ge(c_xb, 5 * l + c - 1)
                    for i, t in enumerate((TX, TX + 1, TX + 2, TB)):
                        ins = tp(bank(c % 2, P, P * i), ch(t, c))
                    tr.sig(ins, c_tr)
                    if c:
                        states(l, c - 1)
                states(l, NCH - 1)
                for c in range(NCH):
                    pe.wait_ge(c_xb, 5 * l + 5)
                    if c:
                        pe.wait_ge(c_cbm, 5 * l + c)
                    for g in range(2):
                        r = slice(HD * g, HD * g + HD)
                        ins = mm(bank(g, P), ch(TB, c)[r], ch(TC, c)[r], start=True, stop=True)
                    tr.sig(ins, c_cb)
                    pe.wait_ge(c_rh, 5 * l + c + 1)
                    pe.wait_ge(c_cs, 5 * l + 5)
                    if c:
                        pe.wait_ge(c_ea, 5 * l + c)
                    for g in range(2):
                        mm(bank(2 + g, 384), C("strb"), S(SS_, "cs", 384, 384 * g), start=True, stop=False)
                        ins = mm(bank(2 + g, 384), C("strf"), S(SS_, "cs", 384, 768 + 384 * g),
                                 start=False, stop=True)
                    tr.sig(ins, c_arg)
                    if c == 1:
                        pe.wait_ge(c_sp, l + 1)
                    pe.wait_ge(c_ecum, l + 1)
                    if c:
                        pe.wait_ge(c_ytok, 5 * l + c)
                        for g in range(2):
                            r = slice(HD * g, HD * g + HD)
                            for d in range(2):
                                mm(bank(5 + g, 192, 192 * d), ch(TC, c)[r],
                                   scr[r, SS_["sp"] + 960 * d + 192 * c:SS_["sp"] + 960 * d + 192 * c + 192],
                                   start=True, stop=True)
                    pe.wait_ge(c_g, 5 * l + c + 1)
                    pe.wait_ge(c_xd, 5 * l + c + 1)
                    for hh in range(SSD_H):
                        for d in range(2):
                            ins = mm(bank(4, HD, HD * hh), S(SS_, "g", P, 768 * d + P * hh),
                                     S(SS_, "xd", HD, 384 * d + HD * hh), start=(d == 0), stop=(d == 1))
                    tr.sig(ins, c_y)
                    pe.wait_ge(c_ytok, 5 * l + c + 1)
                    if c:
                        pe.wait_ge(c_yf, 5 * l + c)
                    for t in range(3):
                        ins = tp(bank(7, P, P * t), S(SS_, "y", P, P * t))
                    tr.sig(ins, c_yt)
                for t in range(3):
                    pe.wait_ge(c_sq, 3 * l + t + 1)
                    for a, b in ((CTX, TOK), (0, CTX)):
                        ins = mm(pair(0)[:, a:b], C("ones"), t2[:, t % 2, a:b], start=(t == 0), stop=(t == 2))
                    tr.sig(ins, c_var)

            def states(l, c):
                pe.wait_ge(c_xb, 5 * l + c + 1)
                pe.wait_ge(c_xe, 5 * l + c + 1)
                if c >= 2:
                    pe.wait_ge(c_cs, 5 * l + c - 1)
                for g in range(2):
                    for d in range(2):
                        ins = mm(ps[HD * g:HD * g + HD, 2 + c % 2, 192 * d:192 * d + 192],
                                 S(SS_, "xb", HD, 512 * c + 384 + HD * g),
                                 S(SS_, "xd", 192, 384 * d + 192 * g), start=True, stop=True)
                tr.sig(ins, c_st)

            def rwkv_features(l):
                pe.wait_ge(r_act, 2 * l + 2)
                for hp in range(2):
                    if hp:
                        pe.wait_ge(r_g, 2 * l + 1)
                    for a, b in ((CTX, TOK), (0, CTX)):
                        ins = mm(pair(2)[:, a:b], gu[:, P * hp:P * hp + P], T(TG)[:, a:b], start=True, stop=True)
                    tr.sig(ins, r_gps)
                    pe.wait_ge(r_ksq, 2 * l + hp + 1)
                    if hp:
                        pe.wait_ge(r_kstd, 2 * l + 1)
                    for a, b in ((CTX, TOK), (0, CTX)):
                        ins = mm(pair(3)[:, a:b], C("blk"), t2[:, hp, a:b], start=True, stop=True)
                    tr.sig(ins, r_kps)
                for i, (d, hp) in enumerate(RW_UNITS):
                    for w in range(2):
                        if i:
                            pe.wait_ge(r_sig, 8 * l + 2 * (i - 1) + w + 1)
                        r = slice(HD * w, HD * w + HD)
                        for a, b in ((CTX, TOK), (0, CTX)):
                            ins = mm(pair(w)[:, a:b], lo[r, d, P * hp:P * hp + P], T(TWA)[r, a:b],
                                     start=True, stop=True)
                        tr.sig(ins, r_wps)
                for hp in range(2):
                    pe.wait_ge(r_bon, 2 * l + hp + 1)
                    for a, b in ((CTX, TOK), (0, CTX)):
                        ins = mm(pair(2 + hp)[:, a:b], C("blk"), T(TWA + hp)[:, a:b], start=True, stop=True)
                    tr.sig(ins, r_bps)

            def rwkv_scan(l):
                for c in range(NCH):
                    for hp in range(2):
                        ins = tp(psf[:, 256 * c + P * hp:256 * c + P * hp + P], ch(TVV + hp, c))
                tr.sig(ins, r_v)
                for i in range(NCH):
                    cs = (0, 0) if i == 0 else (i, NCH - i)
                    for d in range(2):
                        n = 10 * l + 2 * i + d
                        if n % 10 == 0:
                            pe.wait_ge(r_vt, l + 1)
                        if d:
                            pe.wait_ge(r_gsb, 2 * n)
                        if d == 0 and i:
                            pe.wait_ge(r_osb, 5 * l + i)
                            pe.wait_ge(r_st, 5 * l + i)
                        for w in range(2):
                            for hp in range(2):
                                for par in range(2):
                                    r = slice(HD * par, HD * par + HD)
                                    ins = mm(bank(2 * w + par, 256, 256 * hp),
                                             op_blocks(0, d, hp)[r, cs[d], P * w:P * w + P],
                                             op_blocks(1, d, hp)[r, cs[d], :], start=True, stop=True)
                            tr.sig(ins, r_gmat)
                    for d in range(2):
                        n = 10 * l + 2 * i + d
                        pe.wait_ge(r_mt0, n + 1)
                        for q in range(4):
                            ins = tp(bank(5 + 2 * d, P, P * q), S(SR_, "mt", P, 512 * d + P * q))
                        tr.sig(ins, r_m0ps)
                    for j in range(1, 7):
                        for d in range(2):
                            n = 10 * l + 2 * i + d
                            k = 6 * n + j - 1
                            if j == 1:
                                pe.wait_ge(r_m0, n + 1)
                            else:
                                pe.wait_ge(r_msb, inv_count(l, i, d, j - 1, 1))
                            pe.wait_ge(r_lvl, lvl_count(l, i, d, j))
                            for q in range(4):
                                ins = mm(bank(4 + 2 * d, P, P * q), lv_(d)[:, P * q:P * q + P],
                                         S(SR_, "m", P, 512 * d + P * q), start=True, stop=True)
                            tr.sig(ins, r_xps)
                        for d in range(2):
                            n = 10 * l + 2 * i + d
                            pe.wait_ge(r_xsb, x_count(l, i, d, j))
                            if j < 6:
                                for q in range(4):
                                    ins = mm(bank(5 + 2 * d, P, P * q), S(SR_, "mt", P, 512 * d + P * q),
                                             S(SR_, "x", P, 512 * d + P * q), start=True, stop=True)
                                tr.sig(ins, r_mps)
                            for q in range(4):
                                ins = mm(bank(4 + 2 * d, P, P * q), S(SR_, "x", P, 512 * d + P * q),
                                         S(SR_, "mt", P, 512 * d + P * q), start=True, stop=True)
                            tr.sig(ins, r_mps)
                    for d in range(2):
                        pe.wait_ge(r_gsb, 4 * (5 * l + i + 1))
                        for w in range(2):
                            for hp in range(2):
                                ins = tp(bank(d, P, 256 * w + P * hp),
                                         op_blocks(0, d, hp)[:, cs[d], P * w:P * w + P])
                    tr.sig(ins, r_tkps)
                    if i:
                        pe.wait_ge(r_s0, 4 * l + i)
                    for par in range(2):
                        r = slice(HD * par, HD * par + HD)
                        for d in range(2):
                            for hp in range(2):
                                o = bank(2 + par, HD, HD * (2 * d + hp))
                                if i:
                                    mm(o, op_blocks(1, d, hp)[r, cs[d], 0:P],
                                       s0(d, hp)[r], start=True, stop=False)
                                ins = mm(o, S(SR_, "gk", P, 1024 * d + 512 * par + 256 * hp),
                                         VTOK[:, cs[d], HD * (2 * hp + par):HD * (2 * hp + par) + HD],
                                         start=(i == 0), stop=True)
                    tr.sig(ins, r_rps)
                    pe.wait_ge(r_tk, 5 * l + i + 1)
                    pe.wait_ge(r_rsb, 5 * l + i + 1)
                    pe.wait_ge(r_msb, inv_count(l, i, 1, 6, 1))
                    for par in range(2):
                        for d in range(2):
                            for hp in range(2):
                                k = 4 * par + 2 * d + hp
                                ins = mm(bank(0, HD, HD * k),
                                         S(SR_, "mt", P, 512 * d + 256 * par + P * hp), xs(0, HD, HD * k),
                                         start=True, stop=True)
                    tr.sig(ins, r_ups)
                    pe.wait_ge(r_nu, 5 * l + i + 1)
                    for par in range(2):
                        for d in range(2):
                            for hp in range(2):
                                k = 4 * par + 2 * d + hp
                                o = ps[HD * par:HD * par + HD, 1, HD * (2 * d + hp):HD * (2 * d + hp) + HD]
                                a = 512 * d + P * hp + HD * par
                                mm(o, S(SR_, "tok", HD, a + 256),
                                   VTOK[:, cs[d], HD * (2 * hp + par):HD * (2 * hp + par) + HD],
                                   start=True, stop=False)
                                ins = mm(o, S(SR_, "tok", HD, a), xs(1, HD, HD * k), start=False, stop=True)
                    tr.sig(ins, r_sps)
                    for par in range(2):
                        r = slice(HD * par, HD * par + HD)
                        for d in range(2):
                            for hp in range(2):
                                k = 4 * par + 2 * d + hp
                                o = bank(2 + par, HD, HD * (2 * d + hp))
                                a = 1024 * d + 512 * par + 256 * hp + P
                                if i:
                                    mm(o, op_blocks(1, d, hp)[r, cs[d], P:2 * P], s0(d, hp)[r],
                                       start=True, stop=False)
                                mm(o, S(SR_, "gk", P, a),
                                   VTOK[:, cs[d], HD * (2 * hp + par):HD * (2 * hp + par) + HD],
                                   start=(i == 0), stop=False)
                                ins = mm(o, S(SR_, "gb", P, a), xs(1, HD, HD * k), start=False, stop=True)
                    tr.sig(ins, r_ops2)
                pe.wait_ge(r_on, l + 1)
                for c in range(NCH):
                    for hp in range(2):
                        ins = tp(pair(hp)[:, P * c:P * c + P], OTOK[:, c, P * hp:P * hp + P])
                tr.sig(ins, r_otps)

            for l in range(DEPTH):
                base = N_DENSE * l
                m = MOD_FIRST
                for i in range(IN_SLOTS):
                    w = take()
                    for j in range(2):
                        t = 2 * i + j
                        if t < N_IN:
                            dense(base + t, [(w, P * j, 0, KT)], lambda k: h[:, k, :],
                                  first=(2 * l * KT if t == 0 else None))
                        else:
                            wait_pair_free(pe, base + t)
                            for c in range(NCH):
                                for k in range(KT):
                                    ins = mm(psf[:, 1024 + 12 * c:1024 + 12 * c + 12],
                                             h[:, k, P * c:P * c + P], w[:, k, P:P + 12],
                                             start=(k == 0), stop=(k == KT - 1))
                            tr.sig(ins, s_dense)
                    for _ in range(MOD_AFTER_IN[i]):
                        mod_slot(l, m)
                        m += 1
                bar()
                attention(l)
                bar()
                ssd(l)
                bar()
                rwkv_features(l)
                bar()
                rwkv_scan(l)
                bar()
                for i in range(OUT_SLOTS):
                    w = take()
                    for j in range(2):
                        dense(base + D_OUT + 2 * i + j, [(w, P * j, 0, KT)], lambda k: mix[:, k, :])
                norm(2 * l)
                for i in range(UP_SLOTS):
                    w = take()
                    for j in range(2):
                        dense(base + D_UP + 2 * i + j, [(w, P * j, 0, KT)], lambda k: h[:, k, :],
                              first=((2 * l + 1) * KT if i == 0 and j == 0 else None))
                    if l + 1 < DEPTH and i % 2 == 0 and i // 2 < MOD_FIRST:
                        mod_slot(l + 1, i // 2)
                pe.wait_ge(s_free[2], FFN_T * (l + 1))
                for i in range(DOWN_PAIRS):
                    ws = [take() for _ in range(DOWN_PARTS)]
                    for j in range(2):
                        parts = [(w, P * j, 8 * q, min(8, FFN_T - 8 * q)) for q, w in enumerate(ws)]
                        dense(base + D_DOWN + 2 * i + j, parts, lambda k: T(k))
                norm(2 * l + 1)
                bar()

        @block.scalar
        def _(act):
            tr = Track(act, s_act)
            nbar = [0]

            def bar():
                barrier(act, tr, nbar[0])
                nbar[0] += 1

            def A(out, in_, f, bias=0.0, scale=1.0, **kw):
                return nc.scalar.activation(out, in_, f, bias=bias, scale=scale, **kw)

            def evict(n, out):
                act.wait_ge(s_dense, n + 1)
                acc = pair(n % 2)
                if out is None:
                    return acc
                i = n % N_DENSE
                if padded(i):
                    tr.own(nc.scalar.copy(proj[:, i, CTX0:CTX0 + CTX], acc[:, 0:CTX]))
                    ins = nc.scalar.copy(proj[:, i, LAT0:LAT0 + LAT], acc[:, CTX:TOK])
                else:
                    ins = nc.scalar.copy(out, acc)
                tr.sig(ins, s_free[n % 2])

            def modulate(group, k, which):
                sh, sc = (0, 8) if which == 0 else (24, 32)
                for c, (a, b) in enumerate(((CTX, TOK), (0, CTX))):
                    cc = 1 - c
                    ins = A(h[:, k, a:b], xt[:, k, a:b], ACT.Identity, bias=mod[:, sh + k, cc:cc + 1],
                            scale=mod[:, sc + k, cc:cc + 1])
                    if c == 0:
                        tr.own(ins)
                tr.sig(ins, s_h)

            def gated(n, k, gate, group):
                act.wait_ge(s_dense, n + 1)
                g = KT * group + k
                if g >= 2:
                    act.wait_ge(s_res, g - 1)
                if k < 2 and group:
                    act.wait_ge(s_var, KT * group)
                acc = pair(n % 2)
                tr.own(A(t2[:, k % 2, CTX:TOK], acc[:, CTX:TOK], ACT.Copy, scale=mod[:, gate + k, 1:2]))
                tr.sig(A(t2[:, k % 2, 0:CTX], acc[:, 0:CTX], ACT.Copy, scale=mod[:, gate + k, 0:1]),
                       s_free[n % 2])

            def norm(group, modulate_next):
                for k in range(KT):
                    act.wait_ge(s_cen, KT * group + k + 1)
                    if k >= 2:
                        act.wait_ge(s_var, KT * group + k - 1)
                    tr.sig(A(t2[:, k % 2], xt[:, k], ACT.Square), s_sq)
                act.wait_ge(s_var, KT * group + KT)
                tr.sig(A(rstd[:], pair(3), ACT.Sqrt, bias=C("eps", 1)), s_std)
                if modulate_next is not None:
                    for k in range(KT):
                        act.wait_ge(s_ln, KT * group + k + 1)
                        modulate(group, k, modulate_next)

            act.wait_ge(s_const, 48)
            tr.sig(A(cond[:], cond[:], ACT.Silu), s_cond)
            act.wait_ge(s_x, 16)
            act.wait_ge(s_mod, 1)
            for k in range(KT):
                modulate(0, k, 0)

            def attention(l):
                act.wait_ge(a_v, l + 1)
                tr.sig(nc.scalar.copy(S(SA_, "vt", 640), psf[:, 0:640]), a_vt)

                def nk(u):
                    qb = u // 3
                    if qb == 0:
                        return CTX
                    n = qb - 1
                    return P * (2 + min(n + 1, 3) - max(n - 1, 0))

                def exps(u):
                    qb, t = divmod(u, ATT_T)
                    act.wait_ge(a_max, 15 * l + u + 1)
                    if u >= 2:
                        act.wait_ge(a_tr, 15 * l + u - 1)
                    for hh in range(2):
                        k = 6 * qb + 2 * t + hh
                        ins = A(S(SA_, "e", nk(u), 1024 * (u % 2) + 512 * hh), ps[:, 2 * (u % 2) + hh, 0:nk(u)],
                                ACT.Exp, bias=S(SA_, "nm", 1, k), scale=SCALE, accum_out=S(SA_, "sum", 1, k))
                        if hh == 0:
                            tr.own(ins)
                    tr.sig(ins, a_exp)

                exps(0)
                for u in range(15):
                    qb, t = divmod(u, ATT_T)
                    if u + 1 < 15:
                        exps(u + 1)
                    act.wait_ge(a_tr, 15 * l + u + 1)
                    if u >= 2:
                        act.wait_ge(a_pv, 15 * l + u - 1)
                    n = nk(u)
                    et = S(SA_, "et", 1024, 1024 * (u % 2)).rearrange("p (a n) -> p a n", a=2)[:, :, 0:n]
                    tr.sig(nc.scalar.copy(et, ps[:, 4:6, 0:n]), a_trsb)
                    if t == 2:
                        act.wait_ge(a_nms, 5 * l + qb + 1)
                        tr.sig(A(S(SA_, "es", 6, 6 * qb), S(SA_, "nms", 6, 6 * qb), ACT.Exp), a_es)
                    if t == 0 and qb:
                        out(l, qb - 1)
                out(l, 4)

            def out(l, qb):
                act.wait_ge(a_ot, 5 * l + qb + 1)
                tr.sig(nc.scalar.copy(mix[:, 0:ATT_T, P * qb:P * qb + P],
                                      bank(7, 384).rearrange("p (t n) -> p t n", t=3)), a_out)

            def ssd(l):
                for t in range(5):
                    act.wait_ge(c_conv, 5 * l + t + 1)
                    cv = S(SS_, "ea", 646, 646 * (t % 2))
                    tr.own(A(T(TX + t)[:, 0:CTX], cv[:, CTX0:CTX0 + CTX], ACT.Silu))
                    tr.sig(A(T(TX + t)[:, CTX:TOK], cv[:, LAT0:LAT0 + LAT], ACT.Silu), c_silu)
                for t in range(3):
                    tr.own(A(T(TZ + t), T(TZ + t), ACT.Silu))
                sm = SS_["small"]
                act.wait_ge(c_dtx, l + 1)
                tr.own(A(scr[:, sm + 120:sm + 180], scr[:, sm + 120:sm + 180], ACT.Exp))
                tr.sig(A(row[:, 18:30], row[:, 18:30], ACT.Exp), c_dte)
                act.wait_ge(c_cum, l + 1)
                tr.own(A(S(SS_, "small", 120, 240), bank(4, 120), ACT.Exp))
                tr.sig(A(S(SS_, "small", 60, 360), bank(4, 60, 120), ACT.Exp, scale=float(D)), c_ecum)

                def added(c):
                    act.wait_ge(c_st, 5 * l + c + 1)
                    tr.sig(nc.scalar.copy(S(SS_, "cs0", 384, 384 * c), bank(2 + c % 2, 384)), c_cs)

                for c in range(NCH):
                    act.wait_ge(c_tr, 5 * l + c + 1)
                    tr.sig(nc.scalar.copy(S(SS_, "xb", 512, 512 * c), bank(c % 2)), c_xb)
                    if c:
                        added(c - 1)
                added(NCH - 1)
                for c in range(NCH):
                    act.wait_ge(c_arg, 5 * l + c + 1)
                    if c:
                        act.wait_ge(c_g, 5 * l + c)
                    tr.sig(A(S(SS_, "ea", 768).rearrange("p (g n) -> p g n", g=2), ps[:, 2:4, 0:384],
                             ACT.Exp), c_ea)
                for t in range(3):
                    act.wait_ge(c_gate, 3 * l + t + 1)
                    if t >= 2:
                        act.wait_ge(c_var, 3 * l + t - 1)
                    tr.sig(A(t2[:, t % 2], mix[:, 3 + t], ACT.Square), c_sq)
                act.wait_ge(c_var, 3 * l + 3)
                tr.sig(A(rstd[:], pair(0), ACT.Sqrt, bias=C("eps", 1), scale=D / 384.0), c_std)

            def rwkv_features(l):
                act.wait_ge(r_mu, l + 1)
                for t in range(8):
                    if t >= 2:
                        act.wait_ge(r_shift, 8 * l + t - 1)
                    tr.sig(A(S(ST_, "kk", 642, 642 * (t % 2)), proj[:, TR + t, 2:644], ACT.Copy,
                             scale=mus[:, t:t + 1]), r_scl)
                act.wait_ge(r_shift, 8 * l + 8)
                tr.sig(A(T(TWA)[0:HD], T(TWA)[0:HD], ACT.Tanh), r_act)
                tr.sig(A(T(TG), T(TG), ACT.Sigmoid), r_act)
                for hp in range(2):
                    act.wait_ge(r_gps, 2 * l + hp + 1)
                    tr.sig(nc.scalar.copy(mix[:, 6 + hp], pair(2)), r_g)
                    act.wait_ge(r_kps, 2 * l + hp + 1)
                    tr.sig(A(t2[:, hp], pair(3), ACT.Sqrt, bias=C("eps", 1, 1)), r_kstd)
                for i, (d, hp) in enumerate(RW_UNITS):
                    for w, name in enumerate(("w0", "a0")):
                        act.wait_ge(r_wps, 8 * l + 2 * i + w + 1)
                        tr.sig(A(S(ST_, "sw" if w == 0 else "sa", TOK, TOK * i), pair(w), ACT.Sigmoid,
                                 bias=V(name, i)), r_sig)
                for u, (hp, d) in enumerate((hp, d) for hp in range(2) for d in range(2)):
                    i = 2 * d + hp
                    act.wait_ge(r_cum, 4 * l + u + 1)
                    lcol = S(ST_, "l", TOK).rearrange("p (c n) -> p c n", c=NCH)
                    t1 = S(ST_, "t1", TOK).rearrange("p (c n) -> p c n", c=NCH)
                    tt2 = S(ST_, "t2", TOK).rearrange("p (c n) -> p c n", c=NCH)
                    end = P - 1 if d == 0 else 0
                    tr.own(A(dec[:, 0, i], lcol[:, :, HD], ACT.Exp, scale=-DECAY))
                    tr.own(A(dec[:, 1, i], t1[:, :, end], ACT.Exp, scale=-DECAY))
                    tr.own(A(op_blocks(1, d, hp)[:, :, P:2 * P], t1, ACT.Exp, scale=-DECAY))
                    tr.own(A(op_blocks(1, d, hp)[:, :, 0:P], tt2, ACT.Exp, scale=-DECAY))
                    tr.sig(A(op_blocks(0, d, hp)[:, :, P:2 * P], t1, ACT.Exp, scale=DECAY), r_exp)

            def rwkv_scan(l):
                act.wait_ge(r_v, l + 1)
                tr.sig(nc.scalar.copy(VTOK.rearrange("p c n -> p (c n)"), psf[:, 0:1280]), r_vt)
                for i in range(NCH):
                    for j in range(1, 7):
                        for d in range(2):
                            act.wait_ge(r_xps, x_count(l, i, d, j))
                            tr.sig(nc.scalar.copy(S(SR_, "x", 512, 512 * d), bank(4 + 2 * d)), r_xsb)
                    act.wait_ge(r_tkps, 5 * l + i + 1)
                    tr.sig(nc.scalar.copy(S(SR_, "tok", 1024), psf[:, 0:1024]), r_tk)
                    act.wait_ge(r_rps, 5 * l + i + 1)
                    tr.sig(nc.scalar.copy(xs(0, 512, 0).rearrange("p (a n) -> p a n", a=2), ps[:, 2:4, 0:256]),
                           r_rsb)
                sq = S(SR_, "gb", 1280)
                act.wait_ge(r_osq, 2 * l + 1)
                tr.sig(A(sq, OTOK.rearrange("p c n -> p (c n)"), ACT.Square), r_ovar)
                act.wait_ge(r_osq, 2 * l + 2)
                sm = S(SR_, "small", 20, 20)
                tr.sig(A(sm, sm, ACT.Sqrt, bias=C("eps", 1, 2), scale=1.0 / HD), r_ostd)

            for l in range(DEPTH):
                base = N_DENSE * l
                for t in range(N_IN):
                    evict(base + t, T(t))
                n = base + N_IN
                act.wait_ge(s_dense, n + 1)
                tr.sig(nc.scalar.copy(dtr[:].rearrange("p c n -> p (c n)"), psf[:, 1024:1084]), s_free[1])
                bar()
                attention(l)
                bar()
                act.wait_ge(s_small, 16 * N_SMALL * (l + 1))
                ssd(l)
                bar()
                rwkv_features(l)
                bar()
                rwkv_scan(l)
                bar()
                act.wait_ge(s_mod, 2 * l + 2)
                for k in range(KT):
                    gated(base + D_OUT + k, k, 16, 2 * l)
                norm(2 * l, 1)
                for i in range(FFN_T):
                    n = base + D_UP + 2 * i
                    act.wait_ge(s_dense, n + 1)
                    tr.sig(A(T(i), pair(0), ACT.Silu), s_free[0])
                for k in range(KT):
                    gated(base + D_DOWN + k, k, 40, 2 * l + 1)
                if l + 1 < DEPTH:
                    act.wait_ge(s_mod, 2 * (l + 1) + 1)
                norm(2 * l + 1, 0 if l + 1 < DEPTH else None)
                bar()

        @block.vector
        def _(dve):
            tr = Track(dve, s_dve)
            nbar = [0]
            v = nc.vector

            def bar():
                barrier(dve, tr, nbar[0])
                nbar[0] += 1

            def own(ins):
                tr.own(ins)
                tr.hold()

            def modulation(l, a, b):
                first = a == 0
                dve.wait_ge(s_modps, MOD_SLOTS * l + (MOD_FIRST if first else MOD_SLOTS))
                own(v.tensor_tensor(mod[:, a:b, :], bank(4, 2 * (b - a), 2 * a).rearrange("p (t c) -> p t c", c=2),
                                    bm[:, l, a:b].unsqueeze(2).broadcast_to([P, b - a, 2]), ALU.add))
                s = (8, 16) if first else (32, 40)
                tr.sig(v.tensor_scalar(mod[:, s[0]:s[1], :], mod[:, s[0]:s[1], :], 1.0, None, ALU.add), s_mod)

            def norm(group, first, w, b):
                for k in range(KT):
                    dve.wait_ge(*freed(first + k))
                    tr.sig(v.scalar_tensor_tensor(xt[:, k], xt[:, k], ALPHA, t2[:, k % 2], ALU.mult, ALU.add),
                           s_res)
                dve.wait_ge(s_mu, group + 1)
                for k in range(KT):
                    tr.sig(v.tensor_tensor(xt[:, k], xt[:, k], pair(2), ALU.subtract), s_cen)
                dve.wait_ge(s_std, group + 1)
                own(v.reciprocal(rstd[:], rstd[:]))
                for k in range(KT):
                    own(v.tensor_tensor(xt[:, k], xt[:, k], rstd[:], ALU.mult))
                    tr.sig(v.tensor_scalar(xt[:, k], xt[:, k], V(w, k), V(b, k), ALU.mult, ALU.add), s_ln)

            def attention(l):
                for t in range(4):
                    x = proj[:, TQ + t, CTX:TOK]
                    rot = S(SA_, "rot", LAT, LAT * (t % 2))
                    dve.wait_ge(a_rot, 4 * l + t + 1)
                    tr.own(v.tensor_tensor(rot, bank(2 + t % 2), C("sin", LAT), ALU.mult))
                    own(v.tensor_tensor(x, x, C("cos", LAT), ALU.mult))
                    tr.sig(v.tensor_tensor(x, x, rot, ALU.add), a_rope)
                own(v.tensor_scalar(row[:, 30:36], row[:, 0:6], -1.0, None, ALU.mult))

                def maxima(u):
                    qb, t = divmod(u, ATT_T)
                    dve.wait_ge(a_score, 15 * l + u + 1)
                    b = 2 * (u % 2)
                    nk = CTX
                    if qb:
                        n = qb - 1
                        lo_, hi = max(n - 1, 0), min(n + 1, 3)
                        nk = P * (2 + hi - lo_)
                        for there, at, name in ((n > 0, P, "bprev"), (n < 3, nk - P, "bnext")):
                            if there:
                                o = ps[:, b:b + 2, at:at + P]
                                own(v.tensor_tensor(o, o, C(name).unsqueeze(1).broadcast_to([P, 2, P]), ALU.add))
                    k = 6 * qb + 2 * t
                    own(v.tensor_reduce(S(SA_, "mx", 2, k), ps[:, b:b + 2, 0:nk], AX.X, ALU.max))
                    tr.sig(v.scalar_tensor_tensor(S(SA_, "nm", 2, k), S(SA_, "mx", 2, k), -SCALE,
                                                  row[:, 30 + 2 * t:32 + 2 * t], ALU.mult, ALU.min), a_max)
                    if t == 2:
                        k = 6 * qb
                        tr.hold()
                        tr.sig(v.tensor_tensor(S(SA_, "nms", 6, k), S(SA_, "nm", 6, k), row[:, 0:6], ALU.add), a_nms)

                def normalise(qb):
                    k = 6 * qb
                    dve.wait_ge(a_es, 5 * l + qb + 1)
                    own(v.tensor_tensor(S(SA_, "den", 6, k), S(SA_, "sum", 6, k), S(SA_, "es", 6, k), ALU.add))
                    own(v.reciprocal(S(SA_, "den", 6, k), S(SA_, "den", 6, k)))
                    dve.wait_ge(a_pv, 15 * l + 3 * qb + 3)
                    if qb:
                        dve.wait_ge(a_ot, 5 * l + qb)
                    tr.sig(v.tensor_tensor(S(SA_, "osb", 384).rearrange("p (h n) -> p h n", h=6),
                                           bank(6, 384).rearrange("p (h n) -> p h n", h=6),
                                           S(SA_, "den", 6, k).unsqueeze(2).broadcast_to([P, 6, HD]), ALU.mult),
                           a_on)

                maxima(0)
                for u in range(15):
                    if u + 1 < 15:
                        maxima(u + 1)
                    if u % 3 == 2:
                        normalise(u // 3)

            def ssd(l):
                for t in range(5):
                    cv = S(SS_, "ea", 642, 646 * (t % 2) + 2)
                    if t >= 2:
                        dve.wait_ge(c_silu, 5 * l + t - 1)
                    x = proj[:, TX + t]
                    own(v.tensor_scalar(cv, x[:, 0:642], V("convw", t), V("convb", t), ALU.mult, ALU.add))
                    for k in range(1, CONV):
                        ins = v.scalar_tensor_tensor(cv, x[:, k:k + 642], V("convw", 5 * k + t), cv,
                                                     ALU.mult, ALU.add)
                        if k < CONV - 1:
                            own(ins)
                    tr.sig(ins, c_conv)
                sm = SS_["small"]

                def X(a, n=60):
                    return scr[:, sm + a:sm + a + n]

                x, e, dt_, z, q = X(60), X(120), X(180), X(420), X(480)
                x5 = x.rearrange("p (c n) -> p c n", c=NCH)
                own(v.tensor_tensor(x5, dtr[:], row[:, 6:18].unsqueeze(1).broadcast_to([P, NCH, 12]), ALU.add))
                tr.sig(v.scalar_tensor_tensor(e, x, -1.0, x, ALU.mult, ALU.min), c_dtx)
                own(v.tensor_scalar(x, x, 0.0, None, ALU.max))
                dve.wait_ge(c_dte, l + 1)
                own(v.tensor_scalar(z, e, 2.0, None, ALU.add))
                own(v.reciprocal(z, z))
                own(v.tensor_tensor(e, e, z, ALU.mult))
                own(v.tensor_tensor(z, e, e, ALU.mult))
                own(v.tensor_scalar(q, z, 1.0 / 17, None, ALU.mult))
                for c in (15, 13, 11, 9, 7, 5, 3):
                    own(v.scalar_tensor_tensor(q, q, 1.0 / c, z, ALU.add, ALU.mult))
                own(v.scalar_tensor_tensor(q, q, 1.0, e, ALU.add, ALU.mult))
                own(v.scalar_tensor_tensor(dt_, q, 2.0, x, ALU.mult, ALU.add))
                d5 = dt_.rearrange("p (c n) -> p c n", c=NCH)
                for d in range(2):
                    ins = v.scalar_tensor_tensor(scr[:, sm + 30 * d:sm + 30 * d + 30].rearrange("p (c n) -> p c n", c=NCH),
                                                 d5[:, :, 6 * d:6 * d + 6], -1.0,
                                                 row[:, 18 + 6 * d:24 + 6 * d].unsqueeze(1).broadcast_to([P, NCH, 6]),
                                                 ALU.mult, ALU.mult)
                    if d == 0:
                        tr.own(ins)
                tr.sig(ins, c_a)
                dve.wait_ge(c_ecum, l + 1)
                for d in range(2):
                    ins = v.tensor_tensor(X(540 + 30 * d, 30).rearrange("p (c n) -> p c n", c=NCH),
                                          d5[:, :, 6 * d:6 * d + 6],
                                          X(300 + 30 * d, 30).rearrange("p (c n) -> p c n", c=NCH), ALU.mult)
                    if d == 0:
                        tr.own(ins)
                tr.sig(ins, c_dtend)
                for g in range(2):
                    own(v.tensor_copy(scr[HD * g:HD * g + HD, sm + 600:sm + 630].rearrange("p (a n) -> p a n", n=3),
                                      scr[HD * g:HD * g + HD, sm + 360:sm + 420]
                                      .rearrange("p (a n) -> p a n", n=6)[:, :, 3 * g:3 * g + 3]))
                dve.wait_ge(c_cs, 5 * l + 5)
                dve.wait_ge(s_init, 32 * (l + 1))
                for step in range(3):
                    for d in range(2):
                        c = 1 + step if d == 0 else 4 - step
                        nxt = c + 1 if d == 0 else c - 1
                        old = S(SS_, "sp", 192, 960 * d + 192 * c).rearrange("p (h n) -> p h n", h=3)
                        new = S(SS_, "sp", 192, 960 * d + 192 * nxt)
                        own(v.tensor_tensor(new.rearrange("p (h n) -> p h n", h=3), old,
                                            X(600 + 15 * d + 3 * c, 3).unsqueeze(2).broadcast_to([P, 3, HD]),
                                            ALU.mult))
                        own(v.tensor_tensor(new, new, S(SS_, "cs0", 192, 384 * c + 192 * d), ALU.add))
                tr.sig(v.tensor_copy(X(630, 1), X(600, 1)), c_sp)
                for c in range(NCH):
                    dve.wait_ge(c_cb, 5 * l + c + 1)
                    cbm = S(SS_, "cbm", 512).rearrange("p (g d n) -> p g d n", g=2, d=2)
                    for d, name in enumerate(("incf", "incb")):
                        ins = v.tensor_tensor(cbm[:, :, d], ps[:, 0:2, 0:P],
                                              C(name).unsqueeze(1).broadcast_to([P, 2, P]), ALU.mult)
                        if d == 0:
                            tr.own(ins)
                    tr.sig(ins, c_cbm)
                    tr.hold()
                    dve.wait_ge(c_ea, 5 * l + c + 1)
                    if c:
                        dve.wait_ge(c_y, 5 * l + c)
                    for d in range(2):
                        for g in range(2):
                            ins = v.tensor_tensor(
                                S(SS_, "g", 384, 768 * d + 384 * g).rearrange("p (h n) -> p h n", h=3),
                                S(SS_, "ea", 384, 384 * g).rearrange("p (h n) -> p h n", h=3),
                                cbm[:, g, d].unsqueeze(1).broadcast_to([P, 3, P]), ALU.mult)
                            if d == 0 or g == 0:
                                tr.own(ins)
                    tr.sig(ins, c_g)
                    dve.wait_ge(c_y, 5 * l + c + 1)
                    y = S(SS_, "y", 384)
                    if c:
                        dve.wait_ge(c_yt, 5 * l + c)
                        for d in range(2):
                            t1 = S(SS_, "t1", 384, 384 * d).rearrange("p (g h n) -> p g h n", g=2, h=3)
                            ec = X(240 + 30 * d + 6 * c, 6).rearrange("p (g h) -> p g h", g=2)
                            for g in range(2):
                                tr.own(v.tensor_tensor(t1[:, g], bank(5 + g, 192, 192 * d)
                                                       .rearrange("p (h n) -> p h n", h=3),
                                                       ec[:, g].unsqueeze(2).broadcast_to([P, 3, HD]), ALU.mult))
                        tr.hold()
                        own(v.tensor_tensor(y, S(SS_, "t1", 384), S(SS_, "t1", 384, 384), ALU.add))
                        tr.sig(v.tensor_tensor(y, y, bank(4, 384), ALU.add), c_ytok)
                    else:
                        tr.sig(v.tensor_copy(y, bank(4, 384)), c_ytok)
                    dve.wait_ge(c_yt, 5 * l + c + 1)
                    for t in range(3):
                        ins = v.scalar_tensor_tensor(mix[:, 3 + t, P * c:P * c + P], ch(TX + t, c), V("d", t),
                                                     bank(7, P, P * t), ALU.mult, ALU.add)
                        if t < 2:
                            tr.own(ins)
                    tr.sig(ins, c_yf)
                tr.hold()
                for t in range(3):
                    tr.sig(v.tensor_tensor(mix[:, 3 + t], mix[:, 3 + t], T(TZ + t), ALU.mult), c_gate)
                dve.wait_ge(c_std, l + 1)
                own(v.reciprocal(rstd[:], rstd[:]))
                for t in range(3):
                    own(v.scalar_tensor_tensor(mix[:, 3 + t], mix[:, 3 + t], V("normw", t), rstd[:],
                                               ALU.mult, ALU.mult))

            def rwkv_features(l):
                tr.own(v.tensor_scalar(mus[:, 8:16], V("mu", 0, 8), 0.5, None, ALU.mult))
                tr.own(v.tensor_scalar(mus[:, 16:18], V("ka", 0, 2), -1.0, 1.0, ALU.mult, ALU.add))
                tr.sig(v.tensor_scalar(mus[:, 0:8], V("mu", 0, 8), -1.0, 1.0, ALU.mult, ALU.add), r_mu)
                tr.hold()
                for t in range(8):
                    dve.wait_ge(r_sum, 8 * l + t + 1)
                    dve.wait_ge(r_scl, 8 * l + t + 1)
                    a = 642 * (t % 2)
                    for i, (o, n, f) in enumerate(((0, CTX, 0), (CTX, LAT, LAT0 - CTX0))):
                        ins = v.scalar_tensor_tensor(T(TR + t)[:, o:o + n], S(ST_, "sw", n, a + f),
                                                     mus[:, 8 + t:9 + t], S(ST_, "kk", n, a + f),
                                                     ALU.mult, ALU.add)
                        if i == 0:
                            tr.own(ins)
                    tr.sig(ins, r_shift)
                tr.hold()
                kk = S(ST_, "kk", 1280).rearrange("p (a n) -> p a n", a=2)
                for hp in range(2):
                    own(v.tensor_scalar(kk[:, hp], T(TKK + hp), V("kk", hp), None, ALU.mult))
                    tr.sig(v.tensor_tensor(t2[:, hp], kk[:, hp], kk[:, hp], ALU.mult), r_ksq)
                for hp in range(2):
                    dve.wait_ge(r_kstd, 2 * l + hp + 1)
                    own(v.reciprocal(t2[:, hp], t2[:, hp]))
                    tr.sig(v.tensor_tensor(kk[:, hp], kk[:, hp], t2[:, hp], ALU.mult), r_kk)
                for u, (hp, d) in enumerate((hp, d) for hp in range(2) for d in range(2)):
                    i = 2 * d + hp
                    dve.wait_ge(r_sig, 8 * l + 8)
                    if u:
                        dve.wait_ge(r_exp, 4 * l + u)
                    L, t1, tt2 = (S(ST_, n, TOK) for n in ("l", "t1", "t2"))
                    sw = S(ST_, "sw", TOK, TOK * i)
                    if d == 0:
                        own(v.tensor_tensor_scan(L, C("reset", TOK), sw, 0.0, ALU.mult, ALU.add))
                    else:
                        own(v.tensor_tensor_scan(L[:, ::-1], C("reset", TOK), sw[:, ::-1], 0.0, ALU.mult, ALU.add))
                    L5, t15 = (x.rearrange("p (c n) -> p c n", c=NCH) for x in (L, t1))
                    own(v.tensor_tensor(t15, L5, L5[:, :, HD:HD + 1].broadcast_to([P, NCH, P]), ALU.subtract))
                    tr.sig(v.tensor_tensor(tt2, t1, sw, ALU.subtract), r_cum)
                    dve.wait_ge(r_exp, 4 * l + u + 1)
                    dve.wait_ge(r_kd, 8 * l + 2 * u + 2)
                    al, rho = op_blocks(1, d, hp)[:, :, 0:P], op_blocks(1, d, hp)[:, :, P:2 * P]
                    be, ka = op_blocks(0, d, hp)[:, :, 0:P], op_blocks(0, d, hp)[:, :, P:2 * P]

                    def c5(x):
                        return x.rearrange("p (c n) -> p c n", c=NCH)

                    tr.own(v.tensor_tensor(rho, rho, c5(T(TR + hp)), ALU.mult))
                    tr.own(v.tensor_tensor(al, al, c5(kk[:, hp]), ALU.mult))
                    own(v.tensor_tensor(be, ka, c5(S(ST_, "sa", TOK, TOK * i)), ALU.mult))
                    own(v.tensor_tensor(ka, ka, c5(S(ST_, "kd", TOK, TOK * d)), ALU.mult))
                    if d == 1:
                        kd0, kd1 = S(ST_, "kd", TOK), S(ST_, "kd", TOK, TOK)
                        dve.wait_ge(r_wps, 8 * l + 8)
                        dve.wait_ge(r_gps, 2 * l + 2)
                        own(v.tensor_tensor(kd0, kd0, kd1, ALU.add))
                        tr.sig(v.scalar_tensor_tensor(T(TWA + hp), kd0, V("rk", hp), T(TR + hp),
                                                      ALU.mult, ALU.mult), r_bon)
                for hp in range(2):
                    dve.wait_ge(r_bps, 2 * l + hp + 1)
                    tr.sig(v.tensor_tensor(T(TWA + hp), pair(2 + hp), T(TVV + hp), ALU.mult), r_bv)

            def rwkv_scan(l):
                own(v.memset(OTOK, 0.0))
                sx, s0x = S(SR_, "s", 256), S(SR_, "s0", 256)
                for i in range(NCH):
                    cs = (0, 0) if i == 0 else (i, NCH - i)
                    if i:
                        dve.wait_ge(r_lvl, 14 * (NCH * l + i))
                    for d in range(2):
                        n = 10 * l + 2 * i + d
                        for w, name in enumerate(("gb", "gk")):
                            dve.wait_ge(r_gmat, 2 * n + w + 1)
                            tr.sig(v.tensor_tensor(
                                S(SR_, name, 1024, 1024 * d).rearrange("p (q n) -> p q n", q=4),
                                ps[:, 2 * w:2 * w + 2, :].rearrange("p b (h n) -> p (b h) n", h=2),
                                C("gmf" if d == 0 else "gmb", 256).unsqueeze(1).broadcast_to([P, 4, 256]),
                                ALU.mult), r_gsb)
                    for d in range(2):
                        n = 10 * l + 2 * i + d
                        dve.wait_ge(r_m0ps, n + 1)
                        tr.sig(v.tensor_copy(S(SR_, "m", 512, 512 * d), bank(5 + 2 * d)), r_m0)
                    if i:
                        for d in range(2):
                            src = (init_rw[:] if i == 1 else sx)
                            ins = v.tensor_tensor(s0x[:, 128 * d:128 * d + 128].rearrange("p (h n) -> p h n", h=2),
                                                  src[:, 128 * d:128 * d + 128].rearrange("p (h n) -> p h n", h=2),
                                                  dec[:, 0, 2 * d:2 * d + 2, cs[d]:cs[d] + 1].broadcast_to([P, 2, HD]),
                                                  ALU.mult)
                            if d == 0:
                                tr.own(ins)
                        tr.sig(ins, r_s0)
                    for j in range(1, 7):
                        for d in range(2):
                            for turned in range(2):
                                if j == 6 and not turned:
                                    continue
                                dve.wait_ge(r_mps, inv_count(l, i, d, j, turned))
                                m = S(SR_, "mt" if turned else "m", 512, 512 * d)
                                tr.sig(v.tensor_tensor(m, m, bank((4 if turned else 5) + 2 * d), ALU.subtract), r_msb)
                    dve.wait_ge(r_ups, 5 * l + i + 1)
                    tr.sig(v.tensor_scalar(xs(1, 512, 0), bank(0), -1.0, None, ALU.mult), r_nu)
                    dve.wait_ge(r_sps, 5 * l + i + 1)
                    if i:
                        own(v.tensor_tensor(sx, s0x, bank(1, 256), ALU.add))
                    else:
                        own(v.tensor_copy(sx, bank(1, 256)))
                    for d in range(2):
                        o = (fin_rw[:] if i == 0 else sx)[:, 128 * d:128 * d + 128]
                        ins = v.tensor_tensor(o.rearrange("p (h n) -> p h n", h=2),
                                              sx[:, 128 * d:128 * d + 128].rearrange("p (h n) -> p h n", h=2),
                                              dec[:, 1, 2 * d:2 * d + 2, cs[d]:cs[d] + 1].broadcast_to([P, 2, HD]),
                                              ALU.mult)
                        if d == 0:
                            tr.own(ins)
                    tr.sig(ins, r_st)
                    dve.wait_ge(r_ops2, 5 * l + i + 1)
                    for d in range(2):
                        o = OTOK[:, cs[d]].rearrange("p (h a n) -> p a h n", h=2, a=2)
                        for par in range(2):
                            ins = v.tensor_tensor(o[:, par], o[:, par],
                                                  bank(2 + par, P, P * d).rearrange("p (h n) -> p h n", h=2),
                                                  ALU.add)
                            if d == 0 or par == 0:
                                own(ins)
                    tr.sig(ins, r_osb)
                tr.hold()
                o20 = OTOK.rearrange("p c (h n) -> p (c h) n", h=4)
                mu, var = S(SR_, "small", 20), S(SR_, "small", 20, 20)
                own(v.tensor_reduce(mu, o20, AX.X, ALU.add))
                own(v.tensor_scalar(mu, mu, 1.0 / HD, None, ALU.mult))
                tr.sig(v.tensor_tensor(o20, o20, mu.unsqueeze(2).broadcast_to([P, 20, HD]), ALU.subtract), r_osq)
                dve.wait_ge(r_ovar, l + 1)
                tr.sig(v.tensor_reduce(var, S(SR_, "gb", 1280).rearrange("p (a n) -> p a n", a=20), AX.X, ALU.add),
                       r_osq)
                dve.wait_ge(r_ostd, l + 1)
                own(v.reciprocal(var, var))
                tr.sig(v.tensor_tensor(o20, o20, var.unsqueeze(2).broadcast_to([P, 20, HD]), ALU.mult), r_on)
                dve.wait_ge(r_otps, l + 1)
                for hp in range(2):
                    y = S(SR_, "gb", TOK, TOK * hp)
                    own(v.tensor_scalar(y, pair(hp), V("gnw", hp), V("gnb", hp), ALU.mult, ALU.add))
                    own(v.tensor_tensor(y, y, T(TWA + hp), ALU.add))
                    own(v.tensor_tensor(mix[:, 6 + hp], mix[:, 6 + hp], y, ALU.mult))

            dve.wait_ge(s_const, 48)
            modulation(0, 0, 16)
            for l in range(DEPTH):
                modulation(l, 16, MOD_T)
                bar()
                dve.wait_ge(s_small, 16 * N_SMALL * (l + 1))
                attention(l)
                bar()
                ssd(l)
                bar()
                rwkv_features(l)
                bar()
                rwkv_scan(l)
                bar()
                norm(2 * l, N_DENSE * l + D_OUT, "ln1w", "ln1b")
                for i in range(FFN_T):
                    n = N_DENSE * l + D_UP + 2 * i
                    dve.wait_ge(s_dense, n + 2)
                    dve.wait_ge(s_free[0], n // 2 + 1)
                    tr.sig(v.tensor_tensor(T(i), T(i), pair(1), ALU.mult), s_free[2])
                if l + 1 < DEPTH:
                    modulation(l + 1, 0, 16)
                norm(2 * l + 1, N_DENSE * l + D_DOWN, "ln2w", "ln2b")
                bar()

        @block.gpsimd
        def _(pool):
            tr = Track(pool, s_pool)
            nbar = [0]
            g_ = nc.gpsimd

            def bar():
                barrier(pool, tr, nbar[0])
                nbar[0] += 1

            def own(ins):
                tr.own(ins)
                tr.hold()

            def small_loads(l):
                for dst, src in ((vc[:], vecs), (row[:, 0:NROW], rows), (kc[:], kctx), (vcx[:], vctx), (lo[:], lora),
                                 (gu[:], gup)):
                    pool.dma_start(dst, src[l]).then_inc(s_small, 16)
                pool.dma_start(init_rw[:], rwkv0[l]).then_inc(s_small, 16)

            def pads():
                for a in (0, CTX0 + CTX, LAT0 + LAT):
                    own(g_.memset(proj[:, TX:N_IN, a:a + 2], 0.0))

            def ssd(l):
                sm = SS_["small"]
                pool.dma_start(S(SS_, "sp", 192, 192 * 1), ssd0[l, :, 0]).then_inc(s_init, 16)
                pool.dma_start(S(SS_, "sp", 192, 960 + 192 * 4), ssd0[l, :, 1]).then_inc(s_init, 16)
                pool.wait_ge(c_dtend, l + 1)
                for c in range(NCH):
                    pool.wait_ge(c_xb, 5 * l + c + 1)
                    if c:
                        pool.wait_ge(c_st, 5 * l + c)
                    scaled_x(l, c, 540, c_xe)
                for c in range(NCH):
                    if c == 0:
                        pool.wait_ge(c_sp, l + 1)
                    else:
                        pool.wait_ge(c_arg, 5 * l + c)
                    for d, name in enumerate(("incf", "incb")):
                        ins = g_.tensor_tensor(S(SS_, "cs", 768, 768 * d).rearrange("p (h n) -> p h n", h=6),
                                               C(name).unsqueeze(1).broadcast_to([P, 6, P]),
                                               scr[:, sm + 30 * d + 6 * c:sm + 30 * d + 6 * c + 6]
                                               .unsqueeze(2).broadcast_to([P, 6, P]), ALU.mult)
                        if d == 0:
                            tr.own(ins)
                    tr.sig(ins, c_rh)
                    if c == 0:
                        pool.wait_ge(c_st, 5 * l + 5)
                    else:
                        pool.wait_ge(c_y, 5 * l + c)
                    scaled_x(l, c, None, c_xd)
                pool.wait_ge(c_cs, 5 * l + 1)
                pool.dma_start(ssd_out[l], S(SS_, "cs0", 384)).then_inc(s_out, 16)

            def scaled_x(l, c, at, sig):
                sm = SS_["small"]
                for d in range(2):
                    a = sm + (180 + 12 * c + 6 * d if at is None else at + 30 * d + 6 * c)
                    ins = g_.tensor_tensor(S(SS_, "xd", 384, 384 * d).rearrange("p (h n) -> p h n", h=6),
                                           S(SS_, "xb", 384, 512 * c).rearrange("p (h n) -> p h n", h=6),
                                           scr[:, a:a + 6].unsqueeze(2).broadcast_to([P, 6, HD]), ALU.mult)
                    if d == 0:
                        tr.own(ins)
                tr.sig(ins, sig)

            def rwkv_features(l):
                for t in range(8):
                    if t >= 2:
                        pool.wait_ge(r_shift, 8 * l + t - 1)
                    tr.sig(g_.tensor_tensor(S(ST_, "sw", 642, 642 * (t % 2)), proj[:, TR + t, 1:643],
                                            proj[:, TR + t, 3:645], ALU.add), r_sum)
                pool.wait_ge(r_kk, 2 * l + 2)
                for u, (hp, d) in enumerate((hp, d) for hp in range(2) for d in range(2)):
                    i = 2 * d + hp
                    kd, sa = S(ST_, "kd", TOK, TOK * d), S(ST_, "sa", TOK, TOK * i)
                    if u == 0:
                        pool.wait_ge(r_sig, 8 * l + 8)
                    if u >= 2:
                        pool.wait_ge(r_bon, 2 * l + 1)
                    own(g_.tensor_scalar(kd, sa, V("ka", hp), mus[:, 16 + hp:17 + hp], ALU.mult, ALU.add))
                    tr.sig(g_.tensor_tensor(kd, kd, T(TKK + hp), ALU.mult), r_kd)
                    tr.hold()
                    tr.sig(g_.tensor_tensor(sa, sa, S(ST_, "kk", TOK, TOK * hp), ALU.mult), r_kd)

            def rwkv_scan(l):
                for i in range(NCH):
                    for j in range(7):
                        for d in range(2):
                            if j == 0:
                                pool.wait_ge(r_gsb, 4 * (NCH * l + i) + 2 * d + 1)
                            if j == 0 and i:
                                pool.wait_ge(r_xps, x_count(l, i - 1, d, 6))
                            if j >= 2:
                                pool.wait_ge(r_xps, x_count(l, i, d, j - 1))
                            lv = lv_(d).rearrange("p (q n) -> p q n", q=4)
                            gb = S(SR_, "gb", 1024, 1024 * d).rearrange("p (q n) -> p q n", q=4)[:, :, 0:P]
                            tr.sig(g_.tensor_tensor(lv, gb, C("lvl", P, j).unsqueeze(1).broadcast_to([P, 4, P]),
                                                    ALU.mult), r_lvl)
                            if j == 0:
                                tr.hold()
                                tr.sig(g_.tensor_tensor(S(SR_, "mt", 512, 512 * d).rearrange("p (q n) -> p q n", q=4),
                                                        C("ident").unsqueeze(1).broadcast_to([P, 4, P]), lv,
                                                        ALU.subtract), r_mt0)
                                tr.hold()
                    if i == 0:
                        pool.wait_ge(r_st, 5 * l + 1)
                        pool.dma_start(rwkv_out[l], fin_rw[:]).then_inc(s_out, 16)

            for l in range(DEPTH):
                small_loads(l)
                pads()
                pool.wait_ge(s_free[0], (N_DENSE * l + TV) // 2 + 1)
                pool.wait_ge(s_free[1], (N_DENSE // 2 - FFN_T) * l + TK_ // 2 + 1)
                pool.dma_start(k_out[l], proj[:, TK_, 0:CTX]).then_inc(s_out, 16)
                pool.dma_start(v_out[l], proj[:, TV, 0:CTX]).then_inc(s_out, 16)
                bar()
                bar()
                ssd(l)
                pool.wait_ge(s_out, 64 * l + 48)
                bar()
                rwkv_features(l)
                bar()
                rwkv_scan(l)
                bar()
                pool.wait_ge(s_out, 64 * l + 64)
                bar()



def constants():
    c = np.zeros((P, NCON), np.float32)

    def put(name, m, j=0):
        c[:, CON[name] + j * m.shape[1]:CON[name] + (j + 1) * m.shape[1]] = m

    i = np.arange(P)
    row, col = i[:, None], i[None, :]
    put("ident", np.eye(P))
    put("ones", np.full((P, P), 1.0 / D))
    put("blk", (row // HD == col // HD).astype(np.float32))
    perm = np.zeros((P, P))
    for m in range(P):
        if m % 32 < 16:
            perm[m + 16, m] = -1.0
        else:
            perm[m - 16, m] = 1.0
    put("perm", perm)
    put("incf", row <= col)
    put("incb", row >= col)
    put("strf", row < col)
    put("strb", row > col)
    for j in range(7):
        b = 2 ** j
        put("lvl", (row // (2 * b) == col // (2 * b)) & (row // b != col // b), j)
    put("gmf", np.concatenate([row < col, row <= col], 1))
    put("gmb", np.concatenate([row > col, row >= col], 1))
    put("bprev", np.where(col >= row, 0.0, NEG_BIG))
    put("bnext", np.where(col <= row, 0.0, NEG_BIG))
    half = HD // 2
    inv = (1.0 / (np.float32(ROPE_BASE) ** (np.arange(0, half, 2, dtype=np.float32) / np.float32(half)))).astype(np.float32)
    t = np.arange(LAT)
    pos = np.stack([t // GRID_W, t % GRID_W]).astype(np.float32)
    dd = i % HD
    ang = (pos[dd // half] * inv[dd % (half // 2)][:, None]).astype(np.float32)
    put("cos", np.cos(ang))
    put("sin", np.sin(ang))
    put("reset", np.broadcast_to((np.arange(TOK) % P != 0), (P, TOK)))
    put("eps", np.broadcast_to(np.array([LN_EPS, 1e-12, GN_EPS, 0.0], np.float32), (P, 4)))
    return c


def kernel(**inputs):
    import concourse.bacc as bacc
    from concourse.bass_utils import run_bass_kernel_spmd

    x = {k: np.asarray(v) for k, v in inputs.items()}
    L = DEPTH

    def cat(parts, axis):
        return np.concatenate(parts, axis=axis)

    def head_pairs(a, axis):
        s = np.split(a, ATT_H, axis=axis)
        return cat([s[t + 3 * j] for t in range(3) for j in range(2)], axis)

    def slots(w):
        k, n = w.shape
        return w.reshape(k // P, P, n // 256, 256).transpose(2, 1, 0, 3)

    def columns(a):
        return a.reshape(-1, P).T

    packed = {}
    for l in range(L):
        wi = x["w_in"][l]
        wi = cat([head_pairs(wi[:, :384], 1), wi[:, 384:1664], wi[:, 1676:2700], wi[:, 1664:1676],
                  np.zeros((D, 2816 - 2700), np.float32)], 1)
        packed["in", l] = slots(wi)
        packed["mod", l] = slots(x["w_mod"][l])
        packed["out", l] = slots(cat([head_pairs(x["w_out"][l][:384], 0), x["w_out"][l][384:]], 0))
        fi = x["ffn_w_in"][l]
        n = FFN_T * P
        packed["up", l] = slots(np.stack([fi[:, :n].reshape(D, FFN_T, P), fi[:, n:].reshape(D, FFN_T, P)], 2)
                                .reshape(D, 2 * n))
        fo = cat([x["ffn_w_out"][l], np.zeros((2 * P, D), np.float32)], 0)
        packed["down", l] = fo.reshape(3, 8, P, 4, 256).transpose(3, 0, 2, 1, 4).reshape(12, P, 8, 256)
    order = stream_order()
    stream = np.stack([packed[kind, l][i].reshape(P, SLOT) for kind, l, i in order])

    tok = cat([x["x_prompt"][0], x["x_sample"][0]], 0)
    xin = tok.T.reshape(KT, P, TOK).transpose(1, 0, 2)
    conds = np.stack([x["c_ctx"].reshape(KT, P).T, x["c"][0].reshape(KT, P).T], 2)
    bmods = np.stack([columns(x["b_mod"][l]) for l in range(L)], 1)
    vecs = np.stack([cat([columns(x["ssd_conv_w"][l]), columns(x["ssd_conv_b"][l]),
                          columns(np.repeat(x["ssd_d"][l], HD)), columns(x["ssd_norm_w"][l]),
                          columns(x["rwkv_mu"][l]), columns(x["rwkv_w0"][l]), columns(x["rwkv_a0"][l]),
                          columns(x["rwkv_k_k"][l]), columns(x["rwkv_k_a"][l]), columns(x["rwkv_r_k"][l]),
                          columns(x["rwkv_gn_w"][l]), columns(x["rwkv_gn_b"][l]),
                          columns(x["ln1_w"][l]), columns(x["ln1_b"][l]), columns(x["ln2_w"][l]),
                          columns(x["ln2_b"][l])], 1) for l in range(L)])
    rows = np.stack([np.broadcast_to(cat([head_pairs(x["attn_sink"][l], 0), x["ssd_dt_bias"][l].ravel(),
                                          x["ssd_a_log"][l].ravel()], 0), (P, NROW)) for l in range(L)])
    kctx = x["cache_k"][0].transpose(0, 2, 3, 1).reshape(L, P, CTX)
    vctx = x["cache_v"][0].reshape(L, CTX, P)
    lora = cat([x["rwkv_w_up"].transpose(0, 2, 1, 3), x["rwkv_a_up"].transpose(0, 2, 1, 3)], 1)
    gup = x["rwkv_g_up"]
    ssd0 = x["state_ssd"][0].reshape(L, 2, 2, 3, HD, HD).transpose(0, 2, 5, 1, 3, 4).reshape(L, P, 2, 192)
    rwkv0 = x["state_rwkv"][0].reshape(L, 2, 2, 2, HD, HD).transpose(0, 3, 5, 1, 2, 4).reshape(L, P, 256)

    arrays = {"stream": stream, "xin": xin, "consts": constants(), "conds": conds, "bmods": bmods, "vecs": vecs,
              "rows": rows, "kctx": kctx, "vctx": vctx, "lora": lora, "gup": gup, "ssd0": ssd0, "rwkv0": rwkv0}
    arrays = {k: np.ascontiguousarray(v) for k, v in arrays.items()}
    outs = {"y_out": (P, KT, TOK), "k_out": (L, P, CTX), "v_out": (L, P, CTX), "ssd_out": (L, P, 384),
            "rwkv_out": (L, P, 256)}

    nc = bacc.Bacc("TRN2", target_bir_lowering=False, num_devices=1)
    args = [nc.dram_tensor(k, v.shape, F32, kind="ExternalInput").ap() for k, v in arrays.items()]
    args += [nc.dram_tensor(k, s, F32, kind="ExternalOutput").ap() for k, s in outs.items()]
    build(nc, *args)
    r = run_bass_kernel_spmd(nc, [arrays], core_ids=[0]).results[0]

    y = r["y_out"].transpose(2, 1, 0).reshape(TOK, D)
    new_k = r["k_out"].transpose(0, 2, 1).reshape(1, L, CTX, 2, HD)
    new_v = r["v_out"].transpose(0, 2, 1).reshape(1, L, CTX, 2, HD)
    new_ssd = r["ssd_out"].reshape(L, 2, HD, 2, 3, HD).transpose(0, 3, 1, 4, 5, 2).reshape(1, L, 2, 6, HD, HD)
    new_rwkv = r["rwkv_out"].reshape(L, 2, HD, 2, 2, HD).transpose(0, 3, 4, 1, 5, 2).reshape(1, L, 2, 4, HD, HD)
    return (y[None, :CTX], y[None, CTX:], new_k, new_v, new_ssd, new_rwkv)
```

```python
from contextlib import ExitStack

import numpy as np

import concourse.bass as bass
import concourse.mybir as mybir

ALU = mybir.AluOpType
ACT = mybir.ActivationFunctionType
F32 = mybir.dt.float32
F32R = mybir.dt.float32r
AX = mybir.AxisListType

P = 128
D = 1024
KT = D // P
DEPTH = 2
CTX = 128
LAT = 512
TOK = CTX + LAT
NCH = TOK // P
HALVES = ((0, TOK // 2), (TOK // 2, TOK))
GRID_W = 64
HD = 64
ROPE_BASE = 10000.0
ATT_H = 6
ATT_T = 3
SSD_H = 6
RW_H = 4
CONV = 5
FFN_T = 22
ALPHA = (2 * DEPTH) ** 0.25
LN_EPS = 1e-5
GN_EPS = 64e-5
SCALE = HD ** -0.5
NEG_BIG = -1e30
DECAY = float(np.exp(np.float32(-0.5)))

TQ, TK_, TV, TZ, TX, TB, TC, TR, TKK, TVV, TWA, TG = 0, 3, 4, 5, 8, 11, 12, 13, 15, 17, 19, 20
N_IN = 21
PW = TOK + 6
CTX0, LAT0 = 2, CTX + 4

SLOT = 8 * 256
RING = 2
MOD_T = 48
MOD_AT = 384
MOD_SLOTS = 24
MOD_FIRST = 8
IN_SLOTS, OUT_SLOTS, UP_SLOTS, DOWN_PAIRS, DOWN_PARTS = 11, 4, FFN_T, 4, 3

VEC = {}
_n = 0
for _name, _cols in (("convw", CONV * 5), ("convb", 5), ("d", 3), ("normw", 3), ("mu", 8),
                     ("w0", 4), ("a0", 4), ("kk", 2), ("ka", 2), ("rk", 2), ("gnw", 2), ("gnb", 2),
                     ("ln1w", 8), ("ln1b", 8), ("ln2w", 8), ("ln2b", 8)):
    VEC[_name] = _n
    _n += _cols
NVEC = _n

CON = {}
_n = 0
for _name, _cols in (("ident", P), ("ones", P), ("blk", P), ("perm", P), ("incf", P), ("incb", P),
                     ("strf", P), ("strb", P), ("lvl", 7 * P), ("gmf", 2 * P), ("gmb", 2 * P),
                     ("bprev", P), ("bnext", P), ("cos", LAT), ("sin", LAT), ("reset", TOK), ("eps", 4)):
    CON[_name] = _n
    _n += _cols
NCON = _n

NROW = ATT_H + 4 * SSD_H
N_SMALL = 7


def stream_order():
    use = [("mod", 0, i) for i in range(MOD_FIRST)]
    for l in range(DEPTH):
        use += [("in", l, i) for i in range(IN_SLOTS)]
        use += [("mod", l, i) for i in range(MOD_FIRST, MOD_SLOTS)]
        if l + 1 < DEPTH:
            use += [("mod", l + 1, i) for i in range(MOD_FIRST)]
        use += [("out", l, i) for i in range(OUT_SLOTS)]
        use += [("up", l, i) for i in range(UP_SLOTS)]
        use += [("down", l, i) for i in range(DOWN_PAIRS * DOWN_PARTS)]
    return use


SCR_SIZE = 11776


def place(*sizes):
    at, out = 0, {}
    for name, size in sizes:
        out[name] = at
        at += size
    assert at <= SCR_SIZE, at
    return out


SA_ = place(("vt", 640), ("e", 2048), ("et", 2048), ("osb", 384), ("rot", 1024), ("nm", 30), ("mx", 30),
            ("sum", 30), ("es", 30), ("den", 30), ("nms", 30))
SS_ = place(("xb", 2560), ("cs0", 384), ("cs", 1536), ("sp", 1920), ("ea", 768), ("g", 1536), ("cbm", 512),
            ("xd", 768), ("t1", 768), ("y", 384), ("small", 640))
SR_ = place(("ar", 2560), ("gb", 2048), ("gk", 2048), ("m", 1024), ("mt", 1024), ("x", 1024),
            ("tok", 1024), ("s", 256), ("s0", 256), ("small", 160))
ST_ = place(("ar", 2560), ("sw", 2560), ("sa", 2560), ("kk", 1280), ("l", 640), ("t1", 640),
            ("kd", 1280))


ARENA = max(2 * KT * TOK, SCR_SIZE) + 4 * SLOT


def nc_offset(nc, tensor):
    return nc.sbuf_base - 4 * ARENA


class Track:

    def __init__(self, eng, own):
        self.eng, self.own_sem, self.count, self.last = eng, own, {}, None

    def sig(self, ins, sem):
        ins.then_inc(sem, 1)
        self.count[id(sem)] = self.count.get(id(sem), 0) + 1
        self.last = (sem, self.count[id(sem)])

    def own(self, ins):
        self.sig(ins, self.own_sem)

    def hold(self):
        self.eng.wait_ge(*self.last)


def build(nc, stream, xin, consts, conds, bmods, vecs, rows, kctx, vctx, lora, gup, ssd0, rwkv0,
          y_out, k_out, v_out, ssd_out, rwkv_out):
    ctx = ExitStack()
    with ctx:
        def sb(name, shape):
            return ctx.enter_context(nc.sbuf_tensor(name, shape, F32))

        def sem(name):
            return ctx.enter_context(nc.semaphore(name))

        def at(name, shape, offset, dtype=F32):
            return nc.alloc_sbuf_tensor_at(name, shape, dtype, offset=offset)

        xt = sb("xt", [P, KT, TOK])
        proj = sb("proj", [P, N_IN + 1, PW])
        ring = sb("ring", [P, RING, KT, 256])
        arena = ctx.enter_context(nc.sbuf_tensor("arena", [P, ARENA], F32))
        base = nc_offset(nc, arena)
        xh = at("xh", [P, KT, TOK], base, F32R)
        xl = at("xl", [P, KT, TOK], base + 4 * KT * TOK, F32R)
        scr = at("scr", [P, SCR_SIZE], base)
        wbase = base + 4 * max(2 * KT * TOK, SCR_SIZE)
        wh = at("wh", [P, 2, KT, 256], wbase, F32R)
        wl = at("wl", [P, 2, KT, 256], wbase + 8 * SLOT, F32R)
        mix = at("mix", [P, KT, TOK], wbase)
        con = sb("con", [P, NCON])
        vc = sb("vc", [P, NVEC])
        bm = sb("bm", [P, DEPTH, MOD_T])
        row = sb("row", [P, NROW + ATT_H])
        kc = sb("kc", [P, CTX])
        vcx = sb("vcx", [P, P])
        lo = sb("lo", [P, 2, 256])
        gu = sb("gu", [P, 256])
        mod = sb("mod", [P, MOD_T, 2])
        cond = sb("cond", [P, KT, 2])
        rawh = sb("rawh", [P, 2, TOK])
        dtr = sb("dtr", [P, NCH, 12])
        t2 = sb("t2", [P, 2, TOK])
        rstd = sb("rstd", [P, TOK])
        mus = sb("mus", [P, 24])
        dec = sb("dec", [P, 2, 4, NCH])
        init_rw = sb("init_rw", [P, 256])
        fin_rw = sb("fin_rw", [P, 256])
        ps = ctx.enter_context(nc.psum_tensor("ps", [P, 8, 512], F32))
        psf = ps[:].rearrange("p b n -> p (b n)")
        pflat = proj[:].rearrange("p t n -> p (t n)")

        def C(name, n=P, j=0):
            a = CON[name] + j * n
            return con[:, a:a + n]

        def V(name, j=0, n=1):
            return vc[:, VEC[name] + j:VEC[name] + j + n]

        def pair(i):
            return psf[:, 1024 * i + 192:1024 * i + 832]

        def chunks(i):
            return psf[:, 1024 * i + 384:1024 * i + 1024]

        def bank(i, n=512, a=0):
            return ps[:, i, a:a + n]

        def S(where, name, n, a=0):
            a = where[name] + a
            return scr[:, a:a + n]

        def T(t):
            return proj[:, t, 0:TOK]

        def ch(t, c):
            return proj[:, t, P * c:P * c + P]

        s_const = sem("s_const")
        s_x = sem("s_x")
        s_small = sem("s_small")
        s_slot = [sem(f"s_slot{i}") for i in range(RING)]
        s_init = sem("s_init")
        s_out = sem("s_out")
        s_y = sem("s_y")
        s_pe = sem("s_pe")
        s_act = sem("s_act")
        s_dve = sem("s_dve")
        s_pool = sem("s_pool")
        s_bar = sem("s_bar")
        s_dense = sem("s_dense")
        s_free = [sem("s_free_a"), sem("s_free_a2"), sem("s_free_v")]
        s_whigh = sem("s_whigh")
        s_wlow = sem("s_wlow")
        s_hhigh = sem("s_hhigh")
        s_hid_high = sem("s_hid_high")
        s_hid = sem("s_hid")
        s_hid_used = sem("s_hid_used")
        s_cond = sem("s_cond")
        s_modps = sem("s_modps")
        s_modrow = [sem("s_modrow_v"), sem("s_modrow_a")]
        s_modt = sem("s_modt")
        s_mod = sem("s_mod")
        s_h = sem("s_h")
        s_res = sem("s_res")
        s_mu = sem("s_mu")
        s_cen = sem("s_cen")
        s_sq = sem("s_sq")
        s_var = sem("s_var")
        s_std = sem("s_std")
        s_ln = sem("s_ln")
        a_v = sem("a_v")
        a_vt = sem("a_vt")
        a_rot = sem("a_rot")
        a_rope = sem("a_rope")
        a_score = sem("a_score")
        a_max = sem("a_max")
        a_exp = sem("a_exp")
        a_tr = sem("a_tr")
        a_trsb = sem("a_trsb")
        a_pv = sem("a_pv")
        a_nms = sem("a_nms")
        a_es = sem("a_es")
        a_on = sem("a_on")
        a_ot = sem("a_ot")
        a_out = sem("a_out")
        c_conv = sem("c_conv")
        c_silu = sem("c_silu")
        c_dtx = sem("c_dtx")
        c_dte = sem("c_dte")
        c_a = sem("c_a")
        c_cum = sem("c_cum")
        c_ecum = sem("c_ecum")
        c_dtend = sem("c_dtend")
        c_tr = sem("c_tr")
        c_xb = sem("c_xb")
        c_xe = sem("c_xe")
        c_st = sem("c_st")
        c_cs = sem("c_cs")
        c_sp = sem("c_sp")
        c_cb = sem("c_cb")
        c_cbm = sem("c_cbm")
        c_rh = sem("c_rh")
        c_arg = sem("c_arg")
        c_ea = sem("c_ea")
        c_g = sem("c_g")
        c_xd = sem("c_xd")
        c_y = sem("c_y")
        c_ytok = sem("c_ytok")
        c_yt = sem("c_yt")
        c_yf = sem("c_yf")
        c_gate = sem("c_gate")
        c_sq = sem("c_sq")
        c_var = sem("c_var")
        c_std = sem("c_std")
        r_mu = sem("r_mu")
        r_sum = sem("r_sum")
        r_scl = sem("r_scl")
        r_shift = sem("r_shift")
        r_act = sem("r_act")
        r_wps = sem("r_wps")
        r_sig = sem("r_sig")
        r_gps = sem("r_gps")
        r_g = sem("r_g")
        r_ksq = sem("r_ksq")
        r_kps = sem("r_kps")
        r_kstd = sem("r_kstd")
        r_kk = sem("r_kk")
        r_cum = sem("r_cum")
        r_exp = sem("r_exp")
        r_kd = sem("r_kd")
        r_ops = sem("r_ops")
        r_bon = sem("r_bon")
        r_bps = sem("r_bps")
        r_bv = sem("r_bv")
        r_v = sem("r_v")
        r_vt = sem("r_vt")
        r_gmat = sem("r_gmat")
        r_gsb = sem("r_gsb")
        r_lvl = sem("r_lvl")
        r_mt0 = sem("r_mt0")
        r_m0ps = sem("r_m0ps")
        r_m0 = sem("r_m0")
        r_xps = sem("r_xps")
        r_xsb = sem("r_xsb")
        r_mps = sem("r_mps")
        r_msb = sem("r_msb")
        r_tkps = sem("r_tkps")
        r_tk = sem("r_tk")
        r_s0 = sem("r_s0")
        r_rps = sem("r_rps")
        r_rsb = sem("r_rsb")
        r_ups = sem("r_ups")
        r_nu = sem("r_nu")
        r_ops2 = sem("r_ops2")
        r_sps = sem("r_sps")
        r_osb = sem("r_osb")
        r_st = sem("r_st")
        r_osq = sem("r_osq")
        r_ovar = sem("r_ovar")
        r_ostd = sem("r_ostd")
        r_on = sem("r_on")
        r_otps = sem("r_otps")
        r_y = sem("r_y")

        order = stream_order()
        NS = len(order)
        D_IN, D_OUT, D_UP, D_DOWN = 0, 22, 30, 74
        N_DENSE = 82
        N_BAR = 6

        def barrier(eng, tr, n):
            tr.hold()
            eng.sem_inc(s_bar, 1)
            eng.wait_ge(s_bar, 4 * (n + 1))

        def done(n):
            l, i = divmod(n, N_DENSE)
            return D_DOWN * l + i + 1

        def freed(n):
            l, i = divmod(n, N_DENSE)
            if n % 2 == 0:
                return s_free[0], n // 2 + 1
            if D_UP <= i < D_DOWN:
                return s_free[2], l * FFN_T + (i - D_UP) // 2 + 1
            return s_free[1], (N_DENSE // 2 - FFN_T) * l + (i // 2 if i < D_UP else i // 2 - FFN_T) + 1

        def wait_pair_free(eng, n):
            l, i = divmod(n, N_DENSE)
            if D_DOWN <= i < D_DOWN + 4:
                if i >= D_DOWN + 2:
                    eng.wait_ge(*freed(n - 4))
            elif D_DOWN + 4 <= i:
                eng.wait_ge(*freed(n - 4))
            elif n >= 2:
                eng.wait_ge(*freed(n - 2))

        def down_pair(i):
            return 2 if i % 2 == 0 else 0

        def hid_at(i, k):
            return (FFN_T * i + k) % KT

        def padded(i):
            return TX <= i < N_IN

        RW_UNITS = [(d, hp) for d in range(2) for hp in range(2)]

        def op_blocks(which, d, hp):
            i = (4 if which else 0) + 2 * d + hp
            if i < 6:
                a = pflat[:, 1280 * i:1280 * i + 1280]
            else:
                a = S(SR_, "ar", 1280, 1280 * (i - 6))
            return a.rearrange("p (c n) -> p c n", c=NCH)

        VTOK = pflat[:, TKK * PW:TKK * PW + 1280].rearrange("p (c n) -> p c n", c=NCH)
        OTOK = pflat[:, TR * PW:TR * PW + 1280].rearrange("p (c n) -> p c n", c=NCH)

        def s0(d, hp):
            return S(SR_, "s0", HD, HD * (2 * d + hp))

        def lv_(d):
            return t2[:, d, 0:512]

        def xs(which, n, a):
            return S(SR_, "x", n, 512 * which + a)

        def lvl_count(l, i, d, j):
            return 14 * (NCH * l + i) + 2 * j + d + 1

        def x_count(l, i, d, j):
            return 12 * (NCH * l + i) + 2 * (j - 1) + d + 1

        def inv_count(l, i, d, j, turned):
            base = 22 * (NCH * l + i)
            return base + (20 + d + 1 if j == 6 else 4 * (j - 1) + 2 * d + turned + 1)

        used_by, mods, dense_slots = [], 0, 0
        split_slots = []
        for n, (kind, l, i) in enumerate(order):
            if kind == "mod":
                mods += 1
                used_by.append((s_modps, mods))
            else:
                dense_slots += 1
                used_by.append((s_wlow, dense_slots))
                split_slots.append((n, kind, l, i))
        PER_DENSE = IN_SLOTS + OUT_SLOTS + UP_SLOTS + DOWN_PAIRS * DOWN_PARTS

        def slot_read(q):
            n, kind, l, i = split_slots[q]
            if kind == "down":
                mp, part = divmod(i, DOWN_PARTS)
                return s_hid_used, (DOWN_PAIRS * l + mp) * FFN_T + min(KT * part + KT, FFN_T)
            first = {"in": D_IN, "out": D_OUT, "up": D_UP}[kind]
            return s_dense, D_DOWN * l + first + 2 * i + 2

        split_after = {KT - 3: 1, 2 * KT - 3: 2, FFN_T - 1: 3}

        def mod_to_h(e):
            g, k = divmod(e, KT)
            return KT * (g + (g + 1) // 2) + k + 1

        block = ctx.enter_context(nc.Block())

        @block.sync
        def _(sp):
            sp.dma_start(con[:], consts).then_inc(s_const, 16)
            sp.dma_start(cond[:], conds).then_inc(s_const, 16)
            sp.dma_start(bm[:], bmods).then_inc(s_const, 16)
            for n in range(NS):
                if n == MOD_FIRST // 2:
                    sp.dma_start(xt[:], xin).then_inc(s_x, 16)
                if n >= RING:
                    sp.wait_ge(*used_by[n - RING])
                sp.dma_start(ring[:, n % RING].rearrange("p k n -> p (k n)"), stream[n])\
                  .then_inc(s_slot[n % RING], 16)
            for k in range(KT):
                sp.wait_ge(s_ln, 8 * (2 * DEPTH - 1) + k + 1)
                sp.dma_start(y_out[:, k], xt[:, k]).then_inc(s_y, 16)
            sp.wait_ge(s_y, 16 * KT)
            sp.wait_ge(s_out, 64 * DEPTH)

        @block.tensor
        def _(pe):
            tr = Track(pe, s_pe)
            mm = nc.tensor.matmul
            nbar = [0]

            def bar():
                barrier(pe, tr, nbar[0])
                nbar[0] += 1

            def take(l, i):
                n = order.index(("mod", l, i))
                pe.wait_ge(s_slot[n % RING], 16 * (n // RING + 1))
                return ring[:, n % RING]

            def tp(out, in_):
                return nc.tensor.transpose(out, in_, C("ident"))

            turned = [0, 0]

            def mod_rows(l, i, b, ks=range(KT)):
                w = take(l, i)
                for k in ks:
                    ins = mm(ps[0:2, b, 0:256], cond[:, k, :], w[:, k, :], start=(k == 0), stop=(k == KT - 1))
                if ks[-1] == KT - 1:
                    tr.sig(ins, s_modps)

            def mod_turn(i):
                first = i < MOD_FIRST
                turned[first] += 1
                pe.wait_ge(s_modrow[first], turned[first])
                for j in range(2):
                    ins = nc.tensor.transpose(bank(7, 2, MOD_AT + 2 * (2 * i + j)),
                                              t2[0:2, i % 2, P * j:P * j + P], C("ident")[0:2, 0:2])
                tr.sig(ins, s_modt)

            def mod_first(l):
                for i in range(MOD_FIRST):
                    mod_rows(l, i, 5 + i % 2)
                    if i:
                        mod_turn(i - 1)
                mod_turn(MOD_FIRST - 1)

            dense_slot = [0]

            def take_split():
                q = dense_slot[0]
                dense_slot[0] += 1
                pe.wait_ge(s_wlow, q + 1)
                return q % 2

            def terms(out, a_hi, a_lo, b_hi, b_lo, first, last):
                mm(out, a_hi, b_hi, start=first, stop=False)
                mm(out, a_lo, b_hi, start=False, stop=False)
                return mm(out, a_hi, b_lo, start=False, stop=last)

            def dense(n, w, col, first=None):
                wait_pair_free(pe, n)
                acc = pair(n % 2)
                for k in range(KT):
                    if first is not None:
                        pe.wait_ge(s_h, first + k + 1)
                    for a, b in HALVES:
                        ins = terms(acc[:, a:b], wh[:, w, k, col:col + P], wl[:, w, k, col:col + P],
                                    xh[:, k, a:b], xl[:, k, a:b], k == 0, k == KT - 1)
                tr.sig(ins, s_dense)

            pe.wait_ge(s_const, 48)
            pe.wait_ge(s_cond, 1)
            mod_first(0)

            def norm(n, last):
                pe.wait_ge(*freed(last))
                pe.wait_ge(*freed(last - 1))
                for k in range(KT):
                    pe.wait_ge(s_res, KT * n + k + 1)
                    for a, b in HALVES:
                        ins = mm(pair(2)[:, a:b], C("ones"), xt[:, k, a:b], start=(k == 0),
                                 stop=(k == KT - 1))
                tr.sig(ins, s_mu)
                for k in range(KT):
                    pe.wait_ge(s_sq, KT * n + k + 1)
                    for a, b in HALVES:
                        ins = mm(pair(3)[:, a:b], C("ones"), t2[:, k % 2, a:b], start=(k == 0),
                                 stop=(k == KT - 1))
                    tr.sig(ins, s_var)

            def attention(l):
                for c in range(NCH):
                    ins = tp(psf[:, P * c:P * c + P], ch(TV, c))
                tr.sig(ins, a_v)
                for t in range(4):
                    if t >= 2:
                        pe.wait_ge(a_rope, 4 * l + t - 1)
                    tr.sig(mm(bank(2 + t % 2), C("perm"), proj[:, TQ + t, CTX:TOK], start=True, stop=True),
                           a_rot)

                def keys(qb):
                    if qb == 0:
                        return []
                    n = qb - 1
                    return list(range(max(n - 1, 0), min(n + 1, 3) + 1))

                def scores(u):
                    qb, t = divmod(u, ATT_T)
                    if u == 0:
                        pe.wait_ge(a_vt, l + 1)
                        pe.wait_ge(a_rope, 4 * l + 4)
                    if u >= 2:
                        pe.wait_ge(a_exp, 15 * l + u - 1)
                    blocks = keys(qb)
                    for hh in range(2):
                        r = slice(HD * hh, HD * hh + HD)
                        b = 2 * (u % 2) + hh
                        q = ch(TQ + t, qb)[r]
                        own = kc[r, :] if qb else ch(TK_, 0)[r]
                        ins = mm(ps[:, b, 0:CTX], q, own, start=True, stop=True)
                        if blocks:
                            a = CTX + P * blocks[0]
                            ins = mm(ps[:, b, P:P + P * len(blocks)], q,
                                     proj[r, TK_, a:a + P * len(blocks)], start=True, stop=True)
                    tr.sig(ins, a_score)

                def turn(u):
                    qb, t = divmod(u, ATT_T)
                    pe.wait_ge(a_exp, 15 * l + u + 1)
                    if u:
                        pe.wait_ge(a_trsb, 15 * l + u)
                    if t == 1 and qb:
                        pe.wait_ge(a_out, 5 * l + qb)
                    for hh in range(2):
                        for j in range(1 + len(keys(qb))):
                            ins = tp(ps[:, 4 + hh, P * j:P * j + P],
                                     S(SA_, "e", P, 1024 * (u % 2) + 512 * hh + P * j))
                    tr.sig(ins, a_tr)

                def values(u):
                    qb, t = divmod(u, ATT_T)
                    pe.wait_ge(a_trsb, 15 * l + u + 1)
                    if t == 0 and qb:
                        pe.wait_ge(a_on, 5 * l + qb)
                    blocks = keys(qb)
                    for hh in range(2):
                        for j in range(1 + len(blocks)):
                            if j == 0:
                                v = vcx[:, HD * hh:HD * hh + HD] if qb else S(SA_, "vt", HD, HD * hh)
                            else:
                                v = S(SA_, "vt", HD, P * (1 + blocks[j - 1]) + HD * hh)
                            ins = mm(bank(6, HD, P * t + HD * hh),
                                     S(SA_, "et", P, 1024 * (u % 2) + 512 * hh + P * j), v,
                                     start=(j == 0), stop=(j == len(blocks)))
                    tr.sig(ins, a_pv)

                def out(qb):
                    pe.wait_ge(a_on, 5 * l + qb + 1)
                    for t in range(ATT_T):
                        ins = tp(bank(4, P, P * t), S(SA_, "osb", P, P * t))
                    tr.sig(ins, a_ot)

                scores(0)
                for u in range(15):
                    if u + 1 < 15:
                        scores(u + 1)
                    if u:
                        mod_turn(MOD_FIRST + u - 1)
                    mod_rows(l, MOD_FIRST + u, 7, range(KT // 2))
                    turn(u)
                    mod_rows(l, MOD_FIRST + u, 7, range(KT // 2, KT))
                    values(u)
                    if u % 3 == 0 and u:
                        out(u // 3 - 1)
                mod_turn(MOD_SLOTS - 2)
                mod_rows(l, MOD_SLOTS - 1, 7)
                out(4)
                mod_turn(MOD_SLOTS - 1)

            def ssd(l):
                pe.wait_ge(s_mod, 2 * l + 2)
                if l + 1 < DEPTH:
                    mod_first(l + 1)
                pe.wait_ge(c_a, l + 1)
                sm = SS_["small"]
                af, ab = scr[:, sm:sm + 30], scr[:, sm + 30:sm + 60]
                mm(bank(4, 30, 0), C("incf"), af, start=True, stop=True)
                mm(bank(4, 30, 30), C("incb"), ab, start=True, stop=True)
                mm(bank(4, 30, 60), C("strb"), af, start=True, stop=True)
                mm(bank(4, 30, 90), C("strf"), ab, start=True, stop=True)
                ins = mm(bank(4, 60, 120), C("ones"), scr[:, sm:sm + 60], start=True, stop=True)
                tr.sig(ins, c_cum)
                for c in range(NCH):
                    if c == 0:
                        pe.wait_ge(c_silu, 5 * l + 5)
                    if c >= 2:
                        pe.wait_ge(c_xb, 5 * l + c - 1)
                    for i, t in enumerate((TX, TX + 1, TX + 2, TB)):
                        ins = tp(bank(c % 2, P, P * i), ch(t, c))
                    tr.sig(ins, c_tr)
                    if c:
                        states(l, c - 1)
                states(l, NCH - 1)
                for c in range(NCH):
                    pe.wait_ge(c_xb, 5 * l + 5)
                    if c:
                        pe.wait_ge(c_cbm, 5 * l + c)
                    for g in range(2):
                        r = slice(HD * g, HD * g + HD)
                        ins = mm(bank(g, P), ch(TB, c)[r], ch(TC, c)[r], start=True, stop=True)
                    tr.sig(ins, c_cb)
                    pe.wait_ge(c_rh, 5 * l + c + 1)
                    pe.wait_ge(c_cs, 5 * l + 5)
                    if c:
                        pe.wait_ge(c_ea, 5 * l + c)
                    for g in range(2):
                        mm(bank(2 + g, 384), C("strb"), S(SS_, "cs", 384, 384 * g), start=True, stop=False)
                        ins = mm(bank(2 + g, 384), C("strf"), S(SS_, "cs", 384, 768 + 384 * g),
                                 start=False, stop=True)
                    tr.sig(ins, c_arg)
                    if c == 1:
                        pe.wait_ge(c_sp, l + 1)
                    pe.wait_ge(c_ecum, l + 1)
                    if c:
                        pe.wait_ge(c_ytok, 5 * l + c)
                        for g in range(2):
                            r = slice(HD * g, HD * g + HD)
                            for d in range(2):
                                mm(bank(5 + g, 192, 192 * d), ch(TC, c)[r],
                                   scr[r, SS_["sp"] + 960 * d + 192 * c:SS_["sp"] + 960 * d + 192 * c + 192],
                                   start=True, stop=True)
                    pe.wait_ge(c_g, 5 * l + c + 1)
                    pe.wait_ge(c_xd, 5 * l + c + 1)
                    for hh in range(SSD_H):
                        for d in range(2):
                            ins = mm(bank(4, HD, HD * hh), S(SS_, "g", P, 768 * d + P * hh),
                                     S(SS_, "xd", HD, 384 * d + HD * hh), start=(d == 0), stop=(d == 1))
                    tr.sig(ins, c_y)
                    pe.wait_ge(c_ytok, 5 * l + c + 1)
                    if c:
                        pe.wait_ge(c_yf, 5 * l + c)
                    for t in range(3):
                        ins = tp(bank(7, P, P * t), S(SS_, "y", P, P * t))
                    tr.sig(ins, c_yt)
                for t in range(3):
                    pe.wait_ge(c_sq, 3 * l + t + 1)
                    for a, b in HALVES:
                        ins = mm(pair(0)[:, a:b], C("ones"), t2[:, t % 2, a:b], start=(t == 0), stop=(t == 2))
                    tr.sig(ins, c_var)

            def states(l, c):
                pe.wait_ge(c_xb, 5 * l + c + 1)
                pe.wait_ge(c_xe, 5 * l + c + 1)
                if c >= 2:
                    pe.wait_ge(c_cs, 5 * l + c - 1)
                for g in range(2):
                    for d in range(2):
                        ins = mm(ps[HD * g:HD * g + HD, 2 + c % 2, 192 * d:192 * d + 192],
                                 S(SS_, "xb", HD, 512 * c + 384 + HD * g),
                                 S(SS_, "xd", 192, 384 * d + 192 * g), start=True, stop=True)
                tr.sig(ins, c_st)

            def rwkv_features(l):
                if l + 1 < DEPTH:
                    pe.wait_ge(s_mod, 2 * l + 3)
                pe.wait_ge(r_act, 2 * l + 2)
                for hp in range(2):
                    if hp:
                        pe.wait_ge(r_g, 2 * l + 1)
                    for a, b in HALVES:
                        ins = mm(pair(2)[:, a:b], gu[:, P * hp:P * hp + P], T(TG)[:, a:b], start=True, stop=True)
                    tr.sig(ins, r_gps)
                    pe.wait_ge(r_ksq, 2 * l + hp + 1)
                    if hp:
                        pe.wait_ge(r_kstd, 2 * l + 1)
                    for a, b in HALVES:
                        ins = mm(pair(3)[:, a:b], C("blk"), t2[:, hp, a:b], start=True, stop=True)
                    tr.sig(ins, r_kps)
                for i, (d, hp) in enumerate(RW_UNITS):
                    for w in range(2):
                        if i:
                            pe.wait_ge(r_sig, 8 * l + 2 * (i - 1) + w + 1)
                        r = slice(HD * w, HD * w + HD)
                        for a, b in HALVES:
                            ins = mm(pair(w)[:, a:b], lo[r, d, P * hp:P * hp + P], T(TWA)[r, a:b],
                                     start=True, stop=True)
                        tr.sig(ins, r_wps)
                for hp in range(2):
                    pe.wait_ge(r_bon, 2 * l + hp + 1)
                    for a, b in HALVES:
                        ins = mm(pair(2 + hp)[:, a:b], C("blk"), T(TWA + hp)[:, a:b], start=True, stop=True)
                    tr.sig(ins, r_bps)

            def rwkv_scan(l):
                for c in range(NCH):
                    for hp in range(2):
                        ins = tp(psf[:, 256 * c + P * hp:256 * c + P * hp + P], ch(TVV + hp, c))
                tr.sig(ins, r_v)
                for i in range(NCH):
                    cs = (0, 0) if i == 0 else (i, NCH - i)
                    for d in range(2):
                        n = 10 * l + 2 * i + d
                        if n % 10 == 0:
                            pe.wait_ge(r_vt, l + 1)
                        if d:
                            pe.wait_ge(r_gsb, 2 * n)
                        if d == 0 and i:
                            pe.wait_ge(r_osb, 5 * l + i)
                            pe.wait_ge(r_st, 5 * l + i)
                        for w in range(2):
                            for hp in range(2):
                                for par in range(2):
                                    r = slice(HD * par, HD * par + HD)
                                    ins = mm(bank(2 * w + par, 256, 256 * hp),
                                             op_blocks(0, d, hp)[r, cs[d], P * w:P * w + P],
                                             op_blocks(1, d, hp)[r, cs[d], :], start=True, stop=True)
                            tr.sig(ins, r_gmat)
                    for d in range(2):
                        n = 10 * l + 2 * i + d
                        pe.wait_ge(r_mt0, n + 1)
                        for q in range(4):
                            ins = tp(bank(5 + 2 * d, P, P * q), S(SR_, "mt", P, 512 * d + P * q))
                        tr.sig(ins, r_m0ps)
                    for j in range(1, 7):
                        for d in range(2):
                            n = 10 * l + 2 * i + d
                            k = 6 * n + j - 1
                            if j == 1:
                                pe.wait_ge(r_m0, n + 1)
                            else:
                                pe.wait_ge(r_msb, inv_count(l, i, d, j - 1, 1))
                            pe.wait_ge(r_lvl, lvl_count(l, i, d, j))
                            for q in range(4):
                                ins = mm(bank(4 + 2 * d, P, P * q), lv_(d)[:, P * q:P * q + P],
                                         S(SR_, "m", P, 512 * d + P * q), start=True, stop=True)
                            tr.sig(ins, r_xps)
                        for d in range(2):
                            n = 10 * l + 2 * i + d
                            pe.wait_ge(r_xsb, x_count(l, i, d, j))
                            if j < 6:
                                for q in range(4):
                                    ins = mm(bank(5 + 2 * d, P, P * q), S(SR_, "mt", P, 512 * d + P * q),
                                             S(SR_, "x", P, 512 * d + P * q), start=True, stop=True)
                                tr.sig(ins, r_mps)
                            for q in range(4):
                                ins = mm(bank(4 + 2 * d, P, P * q), S(SR_, "x", P, 512 * d + P * q),
                                         S(SR_, "mt", P, 512 * d + P * q), start=True, stop=True)
                            tr.sig(ins, r_mps)
                    for d in range(2):
                        pe.wait_ge(r_gsb, 4 * (5 * l + i + 1))
                        for w in range(2):
                            for hp in range(2):
                                ins = tp(bank(d, P, 256 * w + P * hp),
                                         op_blocks(0, d, hp)[:, cs[d], P * w:P * w + P])
                    tr.sig(ins, r_tkps)
                    if i:
                        pe.wait_ge(r_s0, 4 * l + i)
                    for par in range(2):
                        r = slice(HD * par, HD * par + HD)
                        for d in range(2):
                            for hp in range(2):
                                o = bank(2 + par, HD, HD * (2 * d + hp))
                                if i:
                                    mm(o, op_blocks(1, d, hp)[r, cs[d], 0:P],
                                       s0(d, hp)[r], start=True, stop=False)
                                ins = mm(o, S(SR_, "gk", P, 1024 * d + 512 * par + 256 * hp),
                                         VTOK[:, cs[d], HD * (2 * hp + par):HD * (2 * hp + par) + HD],
                                         start=(i == 0), stop=True)
                    tr.sig(ins, r_rps)
                    pe.wait_ge(r_tk, 5 * l + i + 1)
                    pe.wait_ge(r_rsb, 5 * l + i + 1)
                    pe.wait_ge(r_msb, inv_count(l, i, 1, 6, 1))
                    for par in range(2):
                        for d in range(2):
                            for hp in range(2):
                                k = 4 * par + 2 * d + hp
                                ins = mm(bank(0, HD, HD * k),
                                         S(SR_, "mt", P, 512 * d + 256 * par + P * hp), xs(0, HD, HD * k),
                                         start=True, stop=True)
                    tr.sig(ins, r_ups)
                    pe.wait_ge(r_nu, 5 * l + i + 1)
                    for par in range(2):
                        for d in range(2):
                            for hp in range(2):
                                k = 4 * par + 2 * d + hp
                                o = ps[HD * par:HD * par + HD, 1, HD * (2 * d + hp):HD * (2 * d + hp) + HD]
                                a = 512 * d + P * hp + HD * par
                                mm(o, S(SR_, "tok", HD, a + 256),
                                   VTOK[:, cs[d], HD * (2 * hp + par):HD * (2 * hp + par) + HD],
                                   start=True, stop=False)
                                ins = mm(o, S(SR_, "tok", HD, a), xs(1, HD, HD * k), start=False, stop=True)
                    tr.sig(ins, r_sps)
                    for par in range(2):
                        r = slice(HD * par, HD * par + HD)
                        for d in range(2):
                            for hp in range(2):
                                k = 4 * par + 2 * d + hp
                                o = bank(2 + par, HD, HD * (2 * d + hp))
                                a = 1024 * d + 512 * par + 256 * hp + P
                                if i:
                                    mm(o, op_blocks(1, d, hp)[r, cs[d], P:2 * P], s0(d, hp)[r],
                                       start=True, stop=False)
                                mm(o, S(SR_, "gk", P, a),
                                   VTOK[:, cs[d], HD * (2 * hp + par):HD * (2 * hp + par) + HD],
                                   start=(i == 0), stop=False)
                                ins = mm(o, S(SR_, "gb", P, a), xs(1, HD, HD * k), start=False, stop=True)
                    tr.sig(ins, r_ops2)
                pe.wait_ge(r_on, l + 1)
                for c in range(NCH):
                    for hp in range(2):
                        ins = tp(chunks(hp)[:, P * c:P * c + P], OTOK[:, c, P * hp:P * hp + P])
                tr.sig(ins, r_otps)

            for l in range(DEPTH):
                base = N_DENSE * l
                for i in range(IN_SLOTS):
                    w = take_split()
                    for j in range(2):
                        t = 2 * i + j
                        if t < N_IN:
                            dense(base + t, w, P * j, first=(3 * l * KT if t == 0 else None))
                        else:
                            wait_pair_free(pe, base + t)
                            for c in range(NCH):
                                for k in range(KT):
                                    ins = terms(psf[:, 1024 + 12 * c:1024 + 12 * c + 12],
                                                xh[:, k, P * c:P * c + P], xl[:, k, P * c:P * c + P],
                                                wh[:, w, k, P:P + 12], wl[:, w, k, P:P + 12],
                                                k == 0, k == KT - 1)
                            tr.sig(ins, s_dense)
                bar()
                attention(l)
                bar()
                ssd(l)
                bar()
                rwkv_features(l)
                bar()
                rwkv_scan(l)
                bar()
                for i in range(OUT_SLOTS):
                    w = take_split()
                    for j in range(2):
                        dense(base + D_OUT + 2 * i + j, w, P * j,
                              first=((3 * l + 1) * KT if i == 0 and j == 0 else None))
                norm(2 * l, base + D_UP - 1)
                for i in range(UP_SLOTS):
                    w = take_split()
                    for j in range(2):
                        dense(base + D_UP + 2 * i + j, w, P * j,
                              first=((3 * l + 2) * KT if i == 0 and j == 0 else None))
                for i in range(DOWN_PAIRS):
                    accs = [pair(down_pair(i) + j) for j in range(2)]
                    for j in range(2):
                        wait_pair_free(pe, base + D_DOWN + 2 * i + j)
                    for k in range(FFN_T):
                        if k % KT == 0:
                            w = take_split()
                        e = (DOWN_PAIRS * l + i) * FFN_T + k
                        pe.wait_ge(s_hid, e + 1)
                        for j in range(2):
                            col = P * j
                            for a, b in HALVES:
                                ins = terms(accs[j][:, a:b], wh[:, w, k % KT, col:col + P],
                                            wl[:, w, k % KT, col:col + P], xh[:, hid_at(i, k), a:b],
                                            xl[:, hid_at(i, k), a:b], k == 0, k == FFN_T - 1)
                        tr.sig(ins, s_hid_used)
                norm(2 * l + 1, base + D_DOWN + 5)
                bar()

        @block.scalar
        def _(act):
            tr = Track(act, s_act)
            nbar = [0]

            def bar():
                barrier(act, tr, nbar[0])
                nbar[0] += 1

            def A(out, in_, f, bias=0.0, scale=1.0, **kw):
                return nc.scalar.activation(out, in_, f, bias=bias, scale=scale, **kw)

            def split_high(q):
                if q >= len(split_slots):
                    return
                n = split_slots[q][0]
                act.wait_ge(s_slot[n % RING], 16 * (n // RING + 1))
                if q >= 2:
                    act.wait_ge(*slot_read(q - 2))
                tr.sig(nc.scalar.copy(wh[:, q % 2], ring[:, n % RING]), s_whigh)

            def evict(n, out):
                act.wait_ge(s_dense, done(n))
                acc = pair(n % 2)
                if out is None:
                    return acc
                i = n % N_DENSE
                if padded(i):
                    tr.own(nc.scalar.copy(proj[:, i, CTX0:CTX0 + CTX], acc[:, 0:CTX]))
                    ins = nc.scalar.copy(proj[:, i, LAT0:LAT0 + LAT], acc[:, CTX:TOK])
                else:
                    ins = nc.scalar.copy(out, acc)
                tr.sig(ins, s_free[n % 2])

            def modulate(k, which, e):
                sh, sc = (0, 8) if which == 0 else (24, 32)
                if e >= 2:
                    act.wait_ge(s_h, mod_to_h(e - 2))
                for c, (a, b) in ((1, (CTX, TOK)), (0, (0, CTX))):
                    ins = A(rawh[:, k % 2, a:b], xt[:, k, a:b], ACT.Identity, bias=mod[:, sh + k, c:c + 1],
                            scale=mod[:, sc + k, c:c + 1])
                    if c:
                        tr.own(ins)
                tr.own(ins)
                tr.hold()
                tr.sig(nc.scalar.copy(xh[:, k], rawh[:, k % 2]), s_hhigh)

            def gated(n, k, gate, group, pr=None):
                if pr is None:
                    act.wait_ge(s_dense, done(n))
                    pr = n % 2
                g = KT * group + k
                if g >= 2:
                    act.wait_ge(s_res, g - 1)
                if k < 2 and group:
                    act.wait_ge(s_var, KT * group)
                acc = pair(pr)
                tr.own(A(t2[:, k % 2, CTX:TOK], acc[:, CTX:TOK], ACT.Copy, scale=mod[:, gate + k, 1:2]))
                tr.sig(A(t2[:, k % 2, 0:CTX], acc[:, 0:CTX], ACT.Copy, scale=mod[:, gate + k, 0:1]),
                       s_free[n % 2])

            def norm(group, modulate_next):
                for k in range(KT):
                    act.wait_ge(s_cen, KT * group + k + 1)
                    if k >= 2:
                        act.wait_ge(s_var, KT * group + k - 1)
                    tr.sig(A(t2[:, k % 2], xt[:, k], ACT.Square), s_sq)
                act.wait_ge(s_var, KT * group + KT)
                tr.sig(A(rstd[:], pair(3), ACT.Sqrt, bias=C("eps", 1)), s_std)
                if modulate_next is not None:
                    for k in range(KT):
                        act.wait_ge(s_ln, KT * group + k + 1)
                        modulate(k, modulate_next, KT * (group + 1) + k)

            mod_rows = [0]

            def mod_row(l):
                if l < DEPTH and mod_rows[0] < MOD_FIRST * (l + 1):
                    i = mod_rows[0] % MOD_FIRST
                    mod_rows[0] += 1
                    act.wait_ge(s_modps, MOD_SLOTS * l + i + 1)
                    tr.sig(nc.scalar.copy(t2[0:2, i % 2, 0:256], ps[0:2, 5 + i % 2, 0:256]), s_modrow[1])

            act.wait_ge(s_const, 48)
            tr.sig(A(cond[:], cond[:], ACT.Silu), s_cond)
            for _ in range(MOD_FIRST):
                mod_row(0)
            act.wait_ge(s_x, 16)
            act.wait_ge(s_mod, 1)
            for k in range(KT):
                modulate(k, 0, k)
            split_high(0)
            split_high(1)

            def attention(l):
                act.wait_ge(a_v, l + 1)
                tr.sig(nc.scalar.copy(S(SA_, "vt", 640), psf[:, 0:640]), a_vt)

                def nk(u):
                    qb = u // 3
                    if qb == 0:
                        return CTX
                    n = qb - 1
                    return P * (2 + min(n + 1, 3) - max(n - 1, 0))

                def exps(u):
                    qb, t = divmod(u, ATT_T)
                    act.wait_ge(a_max, 15 * l + u + 1)
                    if u >= 2:
                        act.wait_ge(a_tr, 15 * l + u - 1)
                    for hh in range(2):
                        k = 6 * qb + 2 * t + hh
                        ins = A(S(SA_, "e", nk(u), 1024 * (u % 2) + 512 * hh), ps[:, 2 * (u % 2) + hh, 0:nk(u)],
                                ACT.Exp, bias=S(SA_, "nm", 1, k), scale=SCALE, accum_out=S(SA_, "sum", 1, k))
                        if hh == 0:
                            tr.own(ins)
                    tr.sig(ins, a_exp)

                exps(0)
                for u in range(15):
                    qb, t = divmod(u, ATT_T)
                    if u + 1 < 15:
                        exps(u + 1)
                    act.wait_ge(a_tr, 15 * l + u + 1)
                    if u >= 2:
                        act.wait_ge(a_pv, 15 * l + u - 1)
                    n = nk(u)
                    et = S(SA_, "et", 1024, 1024 * (u % 2)).rearrange("p (a n) -> p a n", a=2)[:, :, 0:n]
                    tr.sig(nc.scalar.copy(et, ps[:, 4:6, 0:n]), a_trsb)
                    if t == 2:
                        act.wait_ge(a_nms, 5 * l + qb + 1)
                        tr.sig(A(S(SA_, "es", 6, 6 * qb), S(SA_, "nms", 6, 6 * qb), ACT.Exp), a_es)
                    if t == 0 and qb:
                        out(l, qb - 1)
                out(l, 4)

            def out(l, qb):
                act.wait_ge(a_ot, 5 * l + qb + 1)
                tr.sig(nc.scalar.copy(mix[:, 0:ATT_T, P * qb:P * qb + P],
                                      bank(4, 384).rearrange("p (t n) -> p t n", t=3)), a_out)

            def ssd(l):
                mod_row(l + 1)
                for t in range(5):
                    act.wait_ge(c_conv, 5 * l + t + 1)
                    cv = S(SS_, "ea", 646, 646 * (t % 2))
                    tr.own(A(T(TX + t)[:, 0:CTX], cv[:, CTX0:CTX0 + CTX], ACT.Silu))
                    tr.sig(A(T(TX + t)[:, CTX:TOK], cv[:, LAT0:LAT0 + LAT], ACT.Silu), c_silu)
                    mod_row(l + 1)
                for t in range(3):
                    tr.own(A(T(TZ + t), T(TZ + t), ACT.Silu))
                    mod_row(l + 1)
                sm = SS_["small"]
                act.wait_ge(c_dtx, l + 1)
                tr.own(A(scr[:, sm + 120:sm + 180], scr[:, sm + 120:sm + 180], ACT.Exp))
                tr.sig(A(row[:, 18:30], row[:, 18:30], ACT.Exp), c_dte)
                act.wait_ge(c_cum, l + 1)
                tr.own(A(S(SS_, "small", 120, 240), bank(4, 120), ACT.Exp))
                tr.sig(A(S(SS_, "small", 60, 360), bank(4, 60, 120), ACT.Exp, scale=float(D)), c_ecum)

                def added(c):
                    act.wait_ge(c_st, 5 * l + c + 1)
                    tr.sig(nc.scalar.copy(S(SS_, "cs0", 384, 384 * c), bank(2 + c % 2, 384)), c_cs)

                for c in range(NCH):
                    act.wait_ge(c_tr, 5 * l + c + 1)
                    tr.sig(nc.scalar.copy(S(SS_, "xb", 512, 512 * c), bank(c % 2)), c_xb)
                    if c:
                        added(c - 1)
                added(NCH - 1)
                for c in range(NCH):
                    act.wait_ge(c_arg, 5 * l + c + 1)
                    if c:
                        act.wait_ge(c_g, 5 * l + c)
                    tr.sig(A(S(SS_, "ea", 768).rearrange("p (g n) -> p g n", g=2), ps[:, 2:4, 0:384],
                             ACT.Exp), c_ea)
                for t in range(3):
                    act.wait_ge(c_gate, 3 * l + t + 1)
                    if t >= 2:
                        act.wait_ge(c_var, 3 * l + t - 1)
                    tr.sig(A(t2[:, t % 2], mix[:, 3 + t], ACT.Square), c_sq)
                act.wait_ge(c_var, 3 * l + 3)
                tr.sig(A(rstd[:], pair(0), ACT.Sqrt, bias=C("eps", 1), scale=D / 384.0), c_std)

            def rwkv_features(l):
                act.wait_ge(r_mu, l + 1)
                for t in range(8):
                    if t >= 2:
                        act.wait_ge(r_shift, 8 * l + t - 1)
                    tr.sig(A(S(ST_, "kk", 642, 642 * (t % 2)), proj[:, TR + t, 2:644], ACT.Copy,
                             scale=mus[:, t:t + 1]), r_scl)
                act.wait_ge(r_shift, 8 * l + 8)
                tr.sig(A(T(TWA)[0:HD], T(TWA)[0:HD], ACT.Tanh), r_act)
                tr.sig(A(T(TG), T(TG), ACT.Sigmoid), r_act)
                for hp in range(2):
                    act.wait_ge(r_gps, 2 * l + hp + 1)
                    tr.sig(nc.scalar.copy(mix[:, 6 + hp], pair(2)), r_g)
                    act.wait_ge(r_kps, 2 * l + hp + 1)
                    tr.sig(A(t2[:, hp], pair(3), ACT.Sqrt, bias=C("eps", 1, 1)), r_kstd)
                for i, (d, hp) in enumerate(RW_UNITS):
                    for w, name in enumerate(("w0", "a0")):
                        act.wait_ge(r_wps, 8 * l + 2 * i + w + 1)
                        tr.sig(A(S(ST_, "sw" if w == 0 else "sa", TOK, TOK * i), pair(w), ACT.Sigmoid,
                                 bias=V(name, i)), r_sig)
                for u, (hp, d) in enumerate((hp, d) for hp in range(2) for d in range(2)):
                    i = 2 * d + hp
                    act.wait_ge(r_cum, 4 * l + u + 1)
                    lcol = S(ST_, "l", TOK).rearrange("p (c n) -> p c n", c=NCH)
                    t1 = S(ST_, "t1", TOK).rearrange("p (c n) -> p c n", c=NCH)
                    tt2 = rawh[:, 0].rearrange("p (c n) -> p c n", c=NCH)
                    end = P - 1 if d == 0 else 0
                    tr.own(A(dec[:, 0, i], lcol[:, :, HD], ACT.Exp, scale=-DECAY))
                    tr.own(A(dec[:, 1, i], t1[:, :, end], ACT.Exp, scale=-DECAY))
                    tr.own(A(op_blocks(1, d, hp)[:, :, P:2 * P], t1, ACT.Exp, scale=-DECAY))
                    tr.own(A(op_blocks(1, d, hp)[:, :, 0:P], tt2, ACT.Exp, scale=-DECAY))
                    tr.sig(A(op_blocks(0, d, hp)[:, :, P:2 * P], t1, ACT.Exp, scale=DECAY), r_exp)

            def rwkv_scan(l):
                act.wait_ge(r_v, l + 1)
                tr.sig(nc.scalar.copy(VTOK.rearrange("p c n -> p (c n)"), psf[:, 0:1280]), r_vt)
                for i in range(NCH):
                    for j in range(1, 7):
                        for d in range(2):
                            act.wait_ge(r_xps, x_count(l, i, d, j))
                            tr.sig(nc.scalar.copy(S(SR_, "x", 512, 512 * d), bank(4 + 2 * d)), r_xsb)
                    act.wait_ge(r_tkps, 5 * l + i + 1)
                    tr.sig(nc.scalar.copy(S(SR_, "tok", 1024), psf[:, 0:1024]), r_tk)
                    act.wait_ge(r_rps, 5 * l + i + 1)
                    tr.sig(nc.scalar.copy(xs(0, 512, 0).rearrange("p (a n) -> p a n", a=2), ps[:, 2:4, 0:256]),
                           r_rsb)
                sq = S(SR_, "gb", 1280)
                act.wait_ge(r_osq, 2 * l + 1)
                tr.sig(A(sq, OTOK.rearrange("p c n -> p (c n)"), ACT.Square), r_ovar)
                act.wait_ge(r_osq, 2 * l + 2)
                sm = S(SR_, "small", 20, 20)
                tr.sig(A(sm, sm, ACT.Sqrt, bias=C("eps", 1, 2), scale=1.0 / HD), r_ostd)

            for l in range(DEPTH):
                base = N_DENSE * l
                q0 = PER_DENSE * l
                for t in range(N_IN):
                    evict(base + t, T(t))
                    if t % 2 == 1 and t // 2 + 2 < IN_SLOTS:
                        split_high(q0 + t // 2 + 2)
                n = base + N_IN
                act.wait_ge(s_dense, done(n))
                tr.sig(nc.scalar.copy(dtr[:].rearrange("p c n -> p (c n)"), psf[:, 1024:1084]), s_free[1])
                bar()
                attention(l)
                bar()
                act.wait_ge(s_small, 16 * N_SMALL * (l + 1))
                ssd(l)
                bar()
                rwkv_features(l)
                bar()
                rwkv_scan(l)
                bar()
                act.wait_ge(s_mod, 2 * l + 2)
                for k in range(KT):
                    tr.sig(nc.scalar.copy(xh[:, k], mix[:, k]), s_hhigh)
                act.wait_ge(s_h, (3 * l + 2) * KT)
                q0 += IN_SLOTS
                split_high(q0)
                split_high(q0 + 1)
                for k in range(KT):
                    gated(base + D_OUT + k, k, 16, 2 * l)
                    if k % 2 == 1:
                        split_high(q0 + 2 + k // 2)
                norm(2 * l, 1)
                q0 += OUT_SLOTS
                for i in range(FFN_T):
                    n = base + D_UP + 2 * i
                    act.wait_ge(s_dense, done(n))
                    tr.sig(A(T(i), pair(0), ACT.Silu), s_free[0])
                    split_high(q0 + 2 + i)
                q0 += UP_SLOTS
                for i in range(DOWN_PAIRS):
                    for k in range(FFN_T):
                        e = (DOWN_PAIRS * l + i) * FFN_T + k
                        if i == 0 and k < KT:
                            act.wait_ge(s_dense, done(base + D_DOWN - 1))
                        else:
                            act.wait_ge(s_hid_used, e - KT + 1)
                        if i == 0:
                            act.wait_ge(s_free[2], FFN_T * l + k + 1)
                        tr.sig(nc.scalar.copy(xh[:, hid_at(i, k)], T(k)), s_hid_high)
                        if i and k == KT:
                            for j in range(2):
                                gated(base + D_DOWN + 2 * i - 2 + j, 2 * i - 2 + j, 40, 2 * l + 1,
                                      down_pair(i - 1) + j)
                        if k in split_after and (i or split_after[k] > 1):
                            split_high(q0 + DOWN_PARTS * i + split_after[k])
                q0 += DOWN_PAIRS * DOWN_PARTS
                if l + 1 < DEPTH:
                    split_high(q0 + 1)
                act.wait_ge(s_hid_used, DOWN_PAIRS * FFN_T * (l + 1))
                for j in range(2):
                    gated(base + D_DOWN + 6 + j, 6 + j, 40, 2 * l + 1, down_pair(DOWN_PAIRS - 1) + j)
                if l + 1 < DEPTH:
                    act.wait_ge(s_mod, 2 * (l + 1) + 1)
                norm(2 * l + 1, 0 if l + 1 < DEPTH else None)
                bar()

        @block.vector
        def _(dve):
            tr = Track(dve, s_dve)
            nbar = [0]
            v = nc.vector

            def bar():
                barrier(dve, tr, nbar[0])
                nbar[0] += 1

            def own(ins):
                tr.own(ins)
                tr.hold()

            def mod_row(l, i):
                dve.wait_ge(s_modps, MOD_SLOTS * l + i + 1)
                tr.sig(v.tensor_copy(t2[0:2, i % 2, 0:256], ps[0:2, 7, 0:256]), s_modrow[0])

            def modulation(l, a, b):
                first = a == 0
                dve.wait_ge(s_modt, MOD_SLOTS * l + (MOD_FIRST if first else MOD_SLOTS))
                own(v.tensor_tensor(mod[:, a:b, :], bank(7, 2 * (b - a), MOD_AT + 2 * a).rearrange("p (t c) -> p t c", c=2),
                                    bm[:, l, a:b].unsqueeze(2).broadcast_to([P, b - a, 2]), ALU.add))
                s = (8, 16) if first else (32, 40)
                tr.sig(v.tensor_scalar(mod[:, s[0]:s[1], :], mod[:, s[0]:s[1], :], 1.0, None, ALU.add), s_mod)

            def split_low(q):
                if q >= len(split_slots):
                    return
                n = split_slots[q][0]
                dve.wait_ge(s_whigh, q + 1)
                tr.sig(v.tensor_tensor(wl[:, q % 2], ring[:, n % RING], wh[:, q % 2], ALU.subtract), s_wlow)

            def input_low(k, e, src):
                dve.wait_ge(s_hhigh, e + 1)
                tr.sig(v.tensor_tensor(xl[:, k], src, xh[:, k], ALU.subtract), s_h)

            def residual(group, first, k):
                dve.wait_ge(*freed(first + k))
                tr.sig(v.scalar_tensor_tensor(xt[:, k], xt[:, k], ALPHA, t2[:, k % 2], ALU.mult, ALU.add), s_res)

            def norm(group, w, b, h_event):
                dve.wait_ge(s_mu, group + 1)
                for k in range(KT):
                    tr.sig(v.tensor_tensor(xt[:, k], xt[:, k], pair(2), ALU.subtract), s_cen)
                dve.wait_ge(s_std, group + 1)
                own(v.reciprocal(rstd[:], rstd[:]))
                for k in range(KT):
                    own(v.tensor_tensor(xt[:, k], xt[:, k], rstd[:], ALU.mult))
                    tr.sig(v.tensor_scalar(xt[:, k], xt[:, k], V(w, k), V(b, k), ALU.mult, ALU.add), s_ln)
                    if h_event is not None and k:
                        input_low(k - 1, h_event + k - 1, rawh[:, (k - 1) % 2])
                if h_event is not None:
                    input_low(KT - 1, h_event + KT - 1, rawh[:, (KT - 1) % 2])

            def attention(l):
                for t in range(4):
                    x = proj[:, TQ + t, CTX:TOK]
                    rot = S(SA_, "rot", LAT, LAT * (t % 2))
                    dve.wait_ge(a_rot, 4 * l + t + 1)
                    tr.own(v.tensor_tensor(rot, bank(2 + t % 2), C("sin", LAT), ALU.mult))
                    own(v.tensor_tensor(x, x, C("cos", LAT), ALU.mult))
                    tr.sig(v.tensor_tensor(x, x, rot, ALU.add), a_rope)
                own(v.tensor_scalar(row[:, 30:36], row[:, 0:6], -1.0, None, ALU.mult))

                def maxima(u):
                    qb, t = divmod(u, ATT_T)
                    dve.wait_ge(a_score, 15 * l + u + 1)
                    b = 2 * (u % 2)
                    nk = CTX
                    if qb:
                        n = qb - 1
                        lo_, hi = max(n - 1, 0), min(n + 1, 3)
                        nk = P * (2 + hi - lo_)
                        for there, at, name in ((n > 0, P, "bprev"), (n < 3, nk - P, "bnext")):
                            if there:
                                o = ps[:, b:b + 2, at:at + P]
                                own(v.tensor_tensor(o, o, C(name).unsqueeze(1).broadcast_to([P, 2, P]), ALU.add))
                    k = 6 * qb + 2 * t
                    own(v.tensor_reduce(S(SA_, "mx", 2, k), ps[:, b:b + 2, 0:nk], AX.X, ALU.max))
                    tr.sig(v.scalar_tensor_tensor(S(SA_, "nm", 2, k), S(SA_, "mx", 2, k), -SCALE,
                                                  row[:, 30 + 2 * t:32 + 2 * t], ALU.mult, ALU.min), a_max)
                    if t == 2:
                        k = 6 * qb
                        tr.hold()
                        tr.sig(v.tensor_tensor(S(SA_, "nms", 6, k), S(SA_, "nm", 6, k), row[:, 0:6], ALU.add), a_nms)

                def normalise(qb):
                    k = 6 * qb
                    dve.wait_ge(a_es, 5 * l + qb + 1)
                    own(v.tensor_tensor(S(SA_, "den", 6, k), S(SA_, "sum", 6, k), S(SA_, "es", 6, k), ALU.add))
                    own(v.reciprocal(S(SA_, "den", 6, k), S(SA_, "den", 6, k)))
                    dve.wait_ge(a_pv, 15 * l + 3 * qb + 3)
                    if qb:
                        dve.wait_ge(a_ot, 5 * l + qb)
                    tr.sig(v.tensor_tensor(S(SA_, "osb", 384).rearrange("p (h n) -> p h n", h=6),
                                           bank(6, 384).rearrange("p (h n) -> p h n", h=6),
                                           S(SA_, "den", 6, k).unsqueeze(2).broadcast_to([P, 6, HD]), ALU.mult),
                           a_on)

                maxima(0)
                for u in range(15):
                    if u + 1 < 15:
                        maxima(u + 1)
                    mod_row(l, MOD_FIRST + u)
                    if u % 3 == 2:
                        normalise(u // 3)
                mod_row(l, MOD_SLOTS - 1)

            def ssd(l):
                for t in range(5):
                    cv = S(SS_, "ea", 642, 646 * (t % 2) + 2)
                    if t >= 2:
                        dve.wait_ge(c_silu, 5 * l + t - 1)
                    x = proj[:, TX + t]
                    own(v.tensor_scalar(cv, x[:, 0:642], V("convw", t), V("convb", t), ALU.mult, ALU.add))
                    for k in range(1, CONV):
                        ins = v.scalar_tensor_tensor(cv, x[:, k:k + 642], V("convw", 5 * k + t), cv,
                                                     ALU.mult, ALU.add)
                        if k < CONV - 1:
                            own(ins)
                    tr.sig(ins, c_conv)
                sm = SS_["small"]

                def X(a, n=60):
                    return scr[:, sm + a:sm + a + n]

                x, e, dt_, z, q = X(60), X(120), X(180), X(420), X(480)
                x5 = x.rearrange("p (c n) -> p c n", c=NCH)
                own(v.tensor_tensor(x5, dtr[:], row[:, 6:18].unsqueeze(1).broadcast_to([P, NCH, 12]), ALU.add))
                tr.sig(v.scalar_tensor_tensor(e, x, -1.0, x, ALU.mult, ALU.min), c_dtx)
                own(v.tensor_scalar(x, x, 0.0, None, ALU.max))
                dve.wait_ge(c_dte, l + 1)
                own(v.tensor_scalar(z, e, 2.0, None, ALU.add))
                own(v.reciprocal(z, z))
                own(v.tensor_tensor(e, e, z, ALU.mult))
                own(v.tensor_tensor(z, e, e, ALU.mult))
                own(v.tensor_scalar(q, z, 1.0 / 17, None, ALU.mult))
                for c in (15, 13, 11, 9, 7, 5, 3):
                    own(v.scalar_tensor_tensor(q, q, 1.0 / c, z, ALU.add, ALU.mult))
                own(v.scalar_tensor_tensor(q, q, 1.0, e, ALU.add, ALU.mult))
                own(v.scalar_tensor_tensor(dt_, q, 2.0, x, ALU.mult, ALU.add))
                d5 = dt_.rearrange("p (c n) -> p c n", c=NCH)
                for d in range(2):
                    ins = v.scalar_tensor_tensor(scr[:, sm + 30 * d:sm + 30 * d + 30].rearrange("p (c n) -> p c n", c=NCH),
                                                 d5[:, :, 6 * d:6 * d + 6], -1.0,
                                                 row[:, 18 + 6 * d:24 + 6 * d].unsqueeze(1).broadcast_to([P, NCH, 6]),
                                                 ALU.mult, ALU.mult)
                    if d == 0:
                        tr.own(ins)
                tr.sig(ins, c_a)
                dve.wait_ge(c_ecum, l + 1)
                for d in range(2):
                    ins = v.tensor_tensor(X(540 + 30 * d, 30).rearrange("p (c n) -> p c n", c=NCH),
                                          d5[:, :, 6 * d:6 * d + 6],
                                          X(300 + 30 * d, 30).rearrange("p (c n) -> p c n", c=NCH), ALU.mult)
                    if d == 0:
                        tr.own(ins)
                tr.sig(ins, c_dtend)
                for g in range(2):
                    own(v.tensor_copy(scr[HD * g:HD * g + HD, sm + 600:sm + 630].rearrange("p (a n) -> p a n", n=3),
                                      scr[HD * g:HD * g + HD, sm + 360:sm + 420]
                                      .rearrange("p (a n) -> p a n", n=6)[:, :, 3 * g:3 * g + 3]))
                dve.wait_ge(c_cs, 5 * l + 5)
                dve.wait_ge(s_init, 32 * (l + 1))
                for step in range(3):
                    for d in range(2):
                        c = 1 + step if d == 0 else 4 - step
                        nxt = c + 1 if d == 0 else c - 1
                        old = S(SS_, "sp", 192, 960 * d + 192 * c).rearrange("p (h n) -> p h n", h=3)
                        new = S(SS_, "sp", 192, 960 * d + 192 * nxt)
                        own(v.tensor_tensor(new.rearrange("p (h n) -> p h n", h=3), old,
                                            X(600 + 15 * d + 3 * c, 3).unsqueeze(2).broadcast_to([P, 3, HD]),
                                            ALU.mult))
                        own(v.tensor_tensor(new, new, S(SS_, "cs0", 192, 384 * c + 192 * d), ALU.add))
                tr.sig(v.tensor_copy(X(630, 1), X(600, 1)), c_sp)
                for c in range(NCH):
                    dve.wait_ge(c_cb, 5 * l + c + 1)
                    cbm = S(SS_, "cbm", 512).rearrange("p (g d n) -> p g d n", g=2, d=2)
                    for d, name in enumerate(("incf", "incb")):
                        ins = v.tensor_tensor(cbm[:, :, d], ps[:, 0:2, 0:P],
                                              C(name).unsqueeze(1).broadcast_to([P, 2, P]), ALU.mult)
                        if d == 0:
                            tr.own(ins)
                    tr.sig(ins, c_cbm)
                    tr.hold()
                    dve.wait_ge(c_ea, 5 * l + c + 1)
                    if c:
                        dve.wait_ge(c_y, 5 * l + c)
                    for d in range(2):
                        for g in range(2):
                            ins = v.tensor_tensor(
                                S(SS_, "g", 384, 768 * d + 384 * g).rearrange("p (h n) -> p h n", h=3),
                                S(SS_, "ea", 384, 384 * g).rearrange("p (h n) -> p h n", h=3),
                                cbm[:, g, d].unsqueeze(1).broadcast_to([P, 3, P]), ALU.mult)
                            if d == 0 or g == 0:
                                tr.own(ins)
                    tr.sig(ins, c_g)
                    dve.wait_ge(c_y, 5 * l + c + 1)
                    y = S(SS_, "y", 384)
                    if c:
                        dve.wait_ge(c_yt, 5 * l + c)
                        for d in range(2):
                            t1 = S(SS_, "t1", 384, 384 * d).rearrange("p (g h n) -> p g h n", g=2, h=3)
                            ec = X(240 + 30 * d + 6 * c, 6).rearrange("p (g h) -> p g h", g=2)
                            for g in range(2):
                                tr.own(v.tensor_tensor(t1[:, g], bank(5 + g, 192, 192 * d)
                                                       .rearrange("p (h n) -> p h n", h=3),
                                                       ec[:, g].unsqueeze(2).broadcast_to([P, 3, HD]), ALU.mult))
                        tr.hold()
                        own(v.tensor_tensor(y, S(SS_, "t1", 384), S(SS_, "t1", 384, 384), ALU.add))
                        tr.sig(v.tensor_tensor(y, y, bank(4, 384), ALU.add), c_ytok)
                    else:
                        tr.sig(v.tensor_copy(y, bank(4, 384)), c_ytok)
                    dve.wait_ge(c_yt, 5 * l + c + 1)
                    for t in range(3):
                        ins = v.scalar_tensor_tensor(mix[:, 3 + t, P * c:P * c + P], ch(TX + t, c), V("d", t),
                                                     bank(7, P, P * t), ALU.mult, ALU.add)
                        if t < 2:
                            tr.own(ins)
                    tr.sig(ins, c_yf)
                tr.hold()
                for t in range(3):
                    tr.sig(v.tensor_tensor(mix[:, 3 + t], mix[:, 3 + t], T(TZ + t), ALU.mult), c_gate)
                dve.wait_ge(c_std, l + 1)
                own(v.reciprocal(rstd[:], rstd[:]))
                for t in range(3):
                    own(v.scalar_tensor_tensor(mix[:, 3 + t], mix[:, 3 + t], V("normw", t), rstd[:],
                                               ALU.mult, ALU.mult))

            def rwkv_features(l):
                tr.own(v.tensor_scalar(mus[:, 8:16], V("mu", 0, 8), 0.5, None, ALU.mult))
                tr.own(v.tensor_scalar(mus[:, 16:18], V("ka", 0, 2), -1.0, 1.0, ALU.mult, ALU.add))
                tr.sig(v.tensor_scalar(mus[:, 0:8], V("mu", 0, 8), -1.0, 1.0, ALU.mult, ALU.add), r_mu)
                tr.hold()
                for t in range(8):
                    dve.wait_ge(r_sum, 8 * l + t + 1)
                    dve.wait_ge(r_scl, 8 * l + t + 1)
                    a = 642 * (t % 2)
                    for i, (o, n, f) in enumerate(((0, CTX, 0), (CTX, LAT, LAT0 - CTX0))):
                        ins = v.scalar_tensor_tensor(T(TR + t)[:, o:o + n], S(ST_, "sw", n, a + f),
                                                     mus[:, 8 + t:9 + t], S(ST_, "kk", n, a + f),
                                                     ALU.mult, ALU.add)
                        if i == 0:
                            tr.own(ins)
                    tr.sig(ins, r_shift)
                tr.hold()
                kk = S(ST_, "kk", 1280).rearrange("p (a n) -> p a n", a=2)
                for hp in range(2):
                    own(v.tensor_scalar(kk[:, hp], T(TKK + hp), V("kk", hp), None, ALU.mult))
                    tr.sig(v.tensor_tensor(t2[:, hp], kk[:, hp], kk[:, hp], ALU.mult), r_ksq)
                for hp in range(2):
                    dve.wait_ge(r_kstd, 2 * l + hp + 1)
                    own(v.reciprocal(t2[:, hp], t2[:, hp]))
                    tr.sig(v.tensor_tensor(kk[:, hp], kk[:, hp], t2[:, hp], ALU.mult), r_kk)
                for u, (hp, d) in enumerate((hp, d) for hp in range(2) for d in range(2)):
                    i = 2 * d + hp
                    dve.wait_ge(r_sig, 8 * l + 8)
                    if u:
                        dve.wait_ge(r_exp, 4 * l + u)
                    L, t1, tt2 = S(ST_, "l", TOK), S(ST_, "t1", TOK), rawh[:, 0]
                    sw = S(ST_, "sw", TOK, TOK * i)
                    if d == 0:
                        own(v.tensor_tensor_scan(L, C("reset", TOK), sw, 0.0, ALU.mult, ALU.add))
                    else:
                        own(v.tensor_tensor_scan(L[:, ::-1], C("reset", TOK), sw[:, ::-1], 0.0, ALU.mult, ALU.add))
                    L5, t15 = (x.rearrange("p (c n) -> p c n", c=NCH) for x in (L, t1))
                    own(v.tensor_tensor(t15, L5, L5[:, :, HD:HD + 1].broadcast_to([P, NCH, P]), ALU.subtract))
                    tr.sig(v.tensor_tensor(tt2, t1, sw, ALU.subtract), r_cum)
                    dve.wait_ge(r_exp, 4 * l + u + 1)
                    dve.wait_ge(r_kd, 8 * l + 2 * u + 2)
                    al, rho = op_blocks(1, d, hp)[:, :, 0:P], op_blocks(1, d, hp)[:, :, P:2 * P]
                    be, ka = op_blocks(0, d, hp)[:, :, 0:P], op_blocks(0, d, hp)[:, :, P:2 * P]

                    def c5(x):
                        return x.rearrange("p (c n) -> p c n", c=NCH)

                    tr.own(v.tensor_tensor(rho, rho, c5(T(TR + hp)), ALU.mult))
                    tr.own(v.tensor_tensor(al, al, c5(kk[:, hp]), ALU.mult))
                    own(v.tensor_tensor(be, ka, c5(S(ST_, "sa", TOK, TOK * i)), ALU.mult))
                    own(v.tensor_tensor(ka, ka, c5(S(ST_, "kd", TOK, TOK * d)), ALU.mult))
                    if d == 1:
                        kd0, kd1 = S(ST_, "kd", TOK), S(ST_, "kd", TOK, TOK)
                        dve.wait_ge(r_wps, 8 * l + 8)
                        dve.wait_ge(r_gps, 2 * l + 2)
                        own(v.tensor_tensor(kd0, kd0, kd1, ALU.add))
                        tr.sig(v.scalar_tensor_tensor(T(TWA + hp), kd0, V("rk", hp), T(TR + hp),
                                                      ALU.mult, ALU.mult), r_bon)
                for hp in range(2):
                    dve.wait_ge(r_bps, 2 * l + hp + 1)
                    tr.sig(v.tensor_tensor(T(TWA + hp), pair(2 + hp), T(TVV + hp), ALU.mult), r_bv)

            def rwkv_scan(l):
                own(v.memset(OTOK, 0.0))
                sx, s0x = S(SR_, "s", 256), S(SR_, "s0", 256)
                for i in range(NCH):
                    cs = (0, 0) if i == 0 else (i, NCH - i)
                    if i:
                        dve.wait_ge(r_lvl, 14 * (NCH * l + i))
                    for d in range(2):
                        n = 10 * l + 2 * i + d
                        for w, name in enumerate(("gb", "gk")):
                            dve.wait_ge(r_gmat, 2 * n + w + 1)
                            tr.sig(v.tensor_tensor(
                                S(SR_, name, 1024, 1024 * d).rearrange("p (q n) -> p q n", q=4),
                                ps[:, 2 * w:2 * w + 2, :].rearrange("p b (h n) -> p (b h) n", h=2),
                                C("gmf" if d == 0 else "gmb", 256).unsqueeze(1).broadcast_to([P, 4, 256]),
                                ALU.mult), r_gsb)
                    for d in range(2):
                        n = 10 * l + 2 * i + d
                        dve.wait_ge(r_m0ps, n + 1)
                        tr.sig(v.tensor_copy(S(SR_, "m", 512, 512 * d), bank(5 + 2 * d)), r_m0)
                    if i:
                        for d in range(2):
                            src = (init_rw[:] if i == 1 else sx)
                            ins = v.tensor_tensor(s0x[:, 128 * d:128 * d + 128].rearrange("p (h n) -> p h n", h=2),
                                                  src[:, 128 * d:128 * d + 128].rearrange("p (h n) -> p h n", h=2),
                                                  dec[:, 0, 2 * d:2 * d + 2, cs[d]:cs[d] + 1].broadcast_to([P, 2, HD]),
                                                  ALU.mult)
                            if d == 0:
                                tr.own(ins)
                        tr.sig(ins, r_s0)
                    for j in range(1, 7):
                        for d in range(2):
                            for turned in range(2):
                                if j == 6 and not turned:
                                    continue
                                dve.wait_ge(r_mps, inv_count(l, i, d, j, turned))
                                m = S(SR_, "mt" if turned else "m", 512, 512 * d)
                                tr.sig(v.tensor_tensor(m, m, bank((4 if turned else 5) + 2 * d), ALU.subtract), r_msb)
                    dve.wait_ge(r_ups, 5 * l + i + 1)
                    tr.sig(v.tensor_scalar(xs(1, 512, 0), bank(0), -1.0, None, ALU.mult), r_nu)
                    dve.wait_ge(r_sps, 5 * l + i + 1)
                    if i:
                        own(v.tensor_tensor(sx, s0x, bank(1, 256), ALU.add))
                    else:
                        own(v.tensor_copy(sx, bank(1, 256)))
                    for d in range(2):
                        o = (fin_rw[:] if i == 0 else sx)[:, 128 * d:128 * d + 128]
                        ins = v.tensor_tensor(o.rearrange("p (h n) -> p h n", h=2),
                                              sx[:, 128 * d:128 * d + 128].rearrange("p (h n) -> p h n", h=2),
                                              dec[:, 1, 2 * d:2 * d + 2, cs[d]:cs[d] + 1].broadcast_to([P, 2, HD]),
                                              ALU.mult)
                        if d == 0:
                            tr.own(ins)
                    tr.sig(ins, r_st)
                    dve.wait_ge(r_ops2, 5 * l + i + 1)
                    for d in range(2):
                        o = OTOK[:, cs[d]].rearrange("p (h a n) -> p a h n", h=2, a=2)
                        for par in range(2):
                            ins = v.tensor_tensor(o[:, par], o[:, par],
                                                  bank(2 + par, P, P * d).rearrange("p (h n) -> p h n", h=2),
                                                  ALU.add)
                            if d == 0 or par == 0:
                                own(ins)
                    tr.sig(ins, r_osb)
                tr.hold()
                o20 = OTOK.rearrange("p c (h n) -> p (c h) n", h=4)
                mu, var = S(SR_, "small", 20), S(SR_, "small", 20, 20)
                own(v.tensor_reduce(mu, o20, AX.X, ALU.add))
                own(v.tensor_scalar(mu, mu, 1.0 / HD, None, ALU.mult))
                tr.sig(v.tensor_tensor(o20, o20, mu.unsqueeze(2).broadcast_to([P, 20, HD]), ALU.subtract), r_osq)
                dve.wait_ge(r_ovar, l + 1)
                tr.sig(v.tensor_reduce(var, S(SR_, "gb", 1280).rearrange("p (a n) -> p a n", a=20), AX.X, ALU.add),
                       r_osq)
                dve.wait_ge(r_ostd, l + 1)
                own(v.reciprocal(var, var))
                tr.sig(v.tensor_tensor(o20, o20, var.unsqueeze(2).broadcast_to([P, 20, HD]), ALU.mult), r_on)
                dve.wait_ge(r_otps, l + 1)
                for hp in range(2):
                    y = S(SR_, "gb", TOK, TOK * hp)
                    own(v.tensor_scalar(y, chunks(hp), V("gnw", hp), V("gnb", hp), ALU.mult, ALU.add))
                    own(v.tensor_tensor(y, y, T(TWA + hp), ALU.add))
                    own(v.tensor_tensor(mix[:, 6 + hp], mix[:, 6 + hp], y, ALU.mult))

            dve.wait_ge(s_const, 48)
            modulation(0, 0, 16)
            for k in range(KT):
                input_low(k, k, rawh[:, k % 2])
            split_low(0)
            split_low(1)
            for l in range(DEPTH):
                q0 = PER_DENSE * l
                for i in range(2, IN_SLOTS):
                    split_low(q0 + i)
                bar()
                dve.wait_ge(s_small, 16 * N_SMALL * (l + 1))
                attention(l)
                bar()
                modulation(l, 2 * MOD_FIRST, MOD_T)
                ssd(l)
                bar()
                if l + 1 < DEPTH:
                    modulation(l + 1, 0, 2 * MOD_FIRST)
                rwkv_features(l)
                bar()
                rwkv_scan(l)
                bar()
                for k in range(KT):
                    input_low(k, (3 * l + 1) * KT + k, mix[:, k])
                q0 += IN_SLOTS
                split_low(q0)
                split_low(q0 + 1)
                for k in range(KT):
                    residual(2 * l, N_DENSE * l + D_OUT, k)
                    if k % 2 == 1:
                        split_low(q0 + 2 + k // 2)
                norm(2 * l, "ln1w", "ln1b", (3 * l + 2) * KT)
                q0 += OUT_SLOTS
                for i in range(FFN_T):
                    n = N_DENSE * l + D_UP + 2 * i
                    dve.wait_ge(s_dense, done(n + 1))
                    dve.wait_ge(s_free[0], n // 2 + 1)
                    tr.sig(v.tensor_tensor(T(i), T(i), pair(1), ALU.mult), s_free[2])
                    split_low(q0 + 2 + i)
                q0 += UP_SLOTS
                for i in range(DOWN_PAIRS):
                    for k in range(FFN_T):
                        e = (DOWN_PAIRS * l + i) * FFN_T + k
                        dve.wait_ge(s_hid_high, e + 1)
                        tr.sig(v.tensor_tensor(xl[:, hid_at(i, k)], T(k), xh[:, hid_at(i, k)], ALU.subtract),
                               s_hid)
                        if i and k == KT:
                            residual(2 * l + 1, N_DENSE * l + D_DOWN, 2 * i - 2)
                            residual(2 * l + 1, N_DENSE * l + D_DOWN, 2 * i - 1)
                        if k in split_after and (i or split_after[k] > 1):
                            split_low(q0 + DOWN_PARTS * i + split_after[k])
                q0 += DOWN_PAIRS * DOWN_PARTS
                if l + 1 < DEPTH:
                    split_low(q0 + 1)
                residual(2 * l + 1, N_DENSE * l + D_DOWN, 6)
                residual(2 * l + 1, N_DENSE * l + D_DOWN, 7)
                norm(2 * l + 1, "ln2w", "ln2b", (3 * l + 3) * KT if l + 1 < DEPTH else None)
                bar()

        @block.gpsimd
        def _(pool):
            tr = Track(pool, s_pool)
            nbar = [0]
            g_ = nc.gpsimd

            def bar():
                barrier(pool, tr, nbar[0])
                nbar[0] += 1

            def own(ins):
                tr.own(ins)
                tr.hold()

            def small_loads(l):
                for dst, src in ((vc[:], vecs), (row[:, 0:NROW], rows), (kc[:], kctx), (vcx[:], vctx), (lo[:], lora),
                                 (gu[:], gup)):
                    pool.dma_start(dst, src[l]).then_inc(s_small, 16)
                pool.dma_start(init_rw[:], rwkv0[l]).then_inc(s_small, 16)

            def pads():
                for a in (0, CTX0 + CTX, LAT0 + LAT):
                    own(g_.memset(proj[:, TX:N_IN, a:a + 2], 0.0))

            def ssd(l):
                sm = SS_["small"]
                pool.dma_start(S(SS_, "sp", 192, 192 * 1), ssd0[l, :, 0]).then_inc(s_init, 16)
                pool.dma_start(S(SS_, "sp", 192, 960 + 192 * 4), ssd0[l, :, 1]).then_inc(s_init, 16)
                pool.wait_ge(c_dtend, l + 1)
                for c in range(NCH):
                    pool.wait_ge(c_xb, 5 * l + c + 1)
                    if c:
                        pool.wait_ge(c_st, 5 * l + c)
                    scaled_x(l, c, 540, c_xe)
                for c in range(NCH):
                    if c == 0:
                        pool.wait_ge(c_sp, l + 1)
                    else:
                        pool.wait_ge(c_arg, 5 * l + c)
                    for d, name in enumerate(("incf", "incb")):
                        ins = g_.tensor_tensor(S(SS_, "cs", 768, 768 * d).rearrange("p (h n) -> p h n", h=6),
                                               C(name).unsqueeze(1).broadcast_to([P, 6, P]),
                                               scr[:, sm + 30 * d + 6 * c:sm + 30 * d + 6 * c + 6]
                                               .unsqueeze(2).broadcast_to([P, 6, P]), ALU.mult)
                        if d == 0:
                            tr.own(ins)
                    tr.sig(ins, c_rh)
                    if c == 0:
                        pool.wait_ge(c_st, 5 * l + 5)
                    else:
                        pool.wait_ge(c_y, 5 * l + c)
                    scaled_x(l, c, None, c_xd)
                pool.wait_ge(c_cs, 5 * l + 1)
                pool.dma_start(ssd_out[l], S(SS_, "cs0", 384)).then_inc(s_out, 16)

            def scaled_x(l, c, at, sig):
                sm = SS_["small"]
                for d in range(2):
                    a = sm + (180 + 12 * c + 6 * d if at is None else at + 30 * d + 6 * c)
                    ins = g_.tensor_tensor(S(SS_, "xd", 384, 384 * d).rearrange("p (h n) -> p h n", h=6),
                                           S(SS_, "xb", 384, 512 * c).rearrange("p (h n) -> p h n", h=6),
                                           scr[:, a:a + 6].unsqueeze(2).broadcast_to([P, 6, HD]), ALU.mult)
                    if d == 0:
                        tr.own(ins)
                tr.sig(ins, sig)

            def rwkv_features(l):
                for t in range(8):
                    if t >= 2:
                        pool.wait_ge(r_shift, 8 * l + t - 1)
                    tr.sig(g_.tensor_tensor(S(ST_, "sw", 642, 642 * (t % 2)), proj[:, TR + t, 1:643],
                                            proj[:, TR + t, 3:645], ALU.add), r_sum)
                pool.wait_ge(r_kk, 2 * l + 2)
                for u, (hp, d) in enumerate((hp, d) for hp in range(2) for d in range(2)):
                    i = 2 * d + hp
                    kd, sa = S(ST_, "kd", TOK, TOK * d), S(ST_, "sa", TOK, TOK * i)
                    if u == 0:
                        pool.wait_ge(r_sig, 8 * l + 8)
                    if u >= 2:
                        pool.wait_ge(r_bon, 2 * l + 1)
                    own(g_.tensor_scalar(kd, sa, V("ka", hp), mus[:, 16 + hp:17 + hp], ALU.mult, ALU.add))
                    tr.sig(g_.tensor_tensor(kd, kd, T(TKK + hp), ALU.mult), r_kd)
                    tr.hold()
                    tr.sig(g_.tensor_tensor(sa, sa, S(ST_, "kk", TOK, TOK * hp), ALU.mult), r_kd)

            def rwkv_scan(l):
                for i in range(NCH):
                    for j in range(7):
                        for d in range(2):
                            if j == 0:
                                pool.wait_ge(r_gsb, 4 * (NCH * l + i) + 2 * d + 1)
                            if j == 0 and i:
                                pool.wait_ge(r_xps, x_count(l, i - 1, d, 6))
                            if j >= 2:
                                pool.wait_ge(r_xps, x_count(l, i, d, j - 1))
                            lv = lv_(d).rearrange("p (q n) -> p q n", q=4)
                            gb = S(SR_, "gb", 1024, 1024 * d).rearrange("p (q n) -> p q n", q=4)[:, :, 0:P]
                            tr.sig(g_.tensor_tensor(lv, gb, C("lvl", P, j).unsqueeze(1).broadcast_to([P, 4, P]),
                                                    ALU.mult), r_lvl)
                            if j == 0:
                                tr.hold()
                                tr.sig(g_.tensor_tensor(S(SR_, "mt", 512, 512 * d).rearrange("p (q n) -> p q n", q=4),
                                                        C("ident").unsqueeze(1).broadcast_to([P, 4, P]), lv,
                                                        ALU.subtract), r_mt0)
                                tr.hold()
                    if i == 0:
                        pool.wait_ge(r_st, 5 * l + 1)
                        pool.dma_start(rwkv_out[l], fin_rw[:]).then_inc(s_out, 16)

            for l in range(DEPTH):
                small_loads(l)
                pads()
                pool.wait_ge(s_free[0], (N_DENSE * l + TV) // 2 + 1)
                pool.wait_ge(s_free[1], (N_DENSE // 2 - FFN_T) * l + TK_ // 2 + 1)
                pool.dma_start(k_out[l], proj[:, TK_, 0:CTX]).then_inc(s_out, 16)
                pool.dma_start(v_out[l], proj[:, TV, 0:CTX]).then_inc(s_out, 16)
                bar()
                bar()
                ssd(l)
                pool.wait_ge(s_out, 64 * l + 48)
                bar()
                rwkv_features(l)
                bar()
                rwkv_scan(l)
                bar()
                pool.wait_ge(s_out, 64 * l + 64)
                bar()



def constants():
    c = np.zeros((P, NCON), np.float32)

    def put(name, m, j=0):
        c[:, CON[name] + j * m.shape[1]:CON[name] + (j + 1) * m.shape[1]] = m

    i = np.arange(P)
    row, col = i[:, None], i[None, :]
    put("ident", np.eye(P))
    put("ones", np.full((P, P), 1.0 / D))
    put("blk", (row // HD == col // HD).astype(np.float32))
    perm = np.zeros((P, P))
    for m in range(P):
        if m % 32 < 16:
            perm[m + 16, m] = -1.0
        else:
            perm[m - 16, m] = 1.0
    put("perm", perm)
    put("incf", row <= col)
    put("incb", row >= col)
    put("strf", row < col)
    put("strb", row > col)
    for j in range(7):
        b = 2 ** j
        put("lvl", (row // (2 * b) == col // (2 * b)) & (row // b != col // b), j)
    put("gmf", np.concatenate([row < col, row <= col], 1))
    put("gmb", np.concatenate([row > col, row >= col], 1))
    put("bprev", np.where(col >= row, 0.0, NEG_BIG))
    put("bnext", np.where(col <= row, 0.0, NEG_BIG))
    half = HD // 2
    inv = (1.0 / (np.float32(ROPE_BASE) ** (np.arange(0, half, 2, dtype=np.float32) / np.float32(half)))).astype(np.float32)
    t = np.arange(LAT)
    pos = np.stack([t // GRID_W, t % GRID_W]).astype(np.float32)
    dd = i % HD
    ang = (pos[dd // half] * inv[dd % (half // 2)][:, None]).astype(np.float32)
    put("cos", np.cos(ang))
    put("sin", np.sin(ang))
    put("reset", np.broadcast_to((np.arange(TOK) % P != 0), (P, TOK)))
    put("eps", np.broadcast_to(np.array([LN_EPS, 1e-12, GN_EPS, 0.0], np.float32), (P, 4)))
    return c


def kernel(**inputs):
    import concourse.bacc as bacc
    from concourse.bass_utils import run_bass_kernel_spmd

    x = {k: np.asarray(v) for k, v in inputs.items()}
    L = DEPTH

    def cat(parts, axis):
        return np.concatenate(parts, axis=axis)

    def head_pairs(a, axis):
        s = np.split(a, ATT_H, axis=axis)
        return cat([s[t + 3 * j] for t in range(3) for j in range(2)], axis)

    def slots(w):
        k, n = w.shape
        return w.reshape(k // P, P, n // 256, 256).transpose(2, 1, 0, 3)

    def columns(a):
        return a.reshape(-1, P).T

    packed = {}
    for l in range(L):
        wi = x["w_in"][l]
        wi = cat([head_pairs(wi[:, :384], 1), wi[:, 384:1664], wi[:, 1676:2700], wi[:, 1664:1676],
                  np.zeros((D, 2816 - 2700), np.float32)], 1)
        packed["in", l] = slots(wi)
        packed["mod", l] = slots(x["w_mod"][l])
        packed["out", l] = slots(cat([head_pairs(x["w_out"][l][:384], 0), x["w_out"][l][384:]], 0))
        fi = x["ffn_w_in"][l]
        n = FFN_T * P
        packed["up", l] = slots(np.stack([fi[:, :n].reshape(D, FFN_T, P), fi[:, n:].reshape(D, FFN_T, P)], 2)
                                .reshape(D, 2 * n))
        fo = cat([x["ffn_w_out"][l], np.zeros((2 * P, D), np.float32)], 0)
        packed["down", l] = fo.reshape(3, 8, P, 4, 256).transpose(3, 0, 2, 1, 4).reshape(12, P, 8, 256)
    order = stream_order()
    stream = np.stack([packed[kind, l][i].reshape(P, SLOT) for kind, l, i in order])

    tok = cat([x["x_prompt"][0], x["x_sample"][0]], 0)
    xin = tok.T.reshape(KT, P, TOK).transpose(1, 0, 2)
    conds = np.stack([x["c_ctx"].reshape(KT, P).T, x["c"][0].reshape(KT, P).T], 2)
    bmods = np.stack([columns(x["b_mod"][l]) for l in range(L)], 1)
    vecs = np.stack([cat([columns(x["ssd_conv_w"][l]), columns(x["ssd_conv_b"][l]),
                          columns(np.repeat(x["ssd_d"][l], HD)), columns(x["ssd_norm_w"][l]),
                          columns(x["rwkv_mu"][l]), columns(x["rwkv_w0"][l]), columns(x["rwkv_a0"][l]),
                          columns(x["rwkv_k_k"][l]), columns(x["rwkv_k_a"][l]), columns(x["rwkv_r_k"][l]),
                          columns(x["rwkv_gn_w"][l]), columns(x["rwkv_gn_b"][l]),
                          columns(x["ln1_w"][l]), columns(x["ln1_b"][l]), columns(x["ln2_w"][l]),
                          columns(x["ln2_b"][l])], 1) for l in range(L)])
    rows = np.stack([np.broadcast_to(cat([head_pairs(x["attn_sink"][l], 0), x["ssd_dt_bias"][l].ravel(),
                                          x["ssd_a_log"][l].ravel()], 0), (P, NROW)) for l in range(L)])
    kctx = x["cache_k"][0].transpose(0, 2, 3, 1).reshape(L, P, CTX)
    vctx = x["cache_v"][0].reshape(L, CTX, P)
    lora = cat([x["rwkv_w_up"].transpose(0, 2, 1, 3), x["rwkv_a_up"].transpose(0, 2, 1, 3)], 1)
    gup = x["rwkv_g_up"]
    ssd0 = x["state_ssd"][0].reshape(L, 2, 2, 3, HD, HD).transpose(0, 2, 5, 1, 3, 4).reshape(L, P, 2, 192)
    rwkv0 = x["state_rwkv"][0].reshape(L, 2, 2, 2, HD, HD).transpose(0, 3, 5, 1, 2, 4).reshape(L, P, 256)

    arrays = {"stream": stream, "xin": xin, "consts": constants(), "conds": conds, "bmods": bmods, "vecs": vecs,
              "rows": rows, "kctx": kctx, "vctx": vctx, "lora": lora, "gup": gup, "ssd0": ssd0, "rwkv0": rwkv0}
    arrays = {k: np.ascontiguousarray(v) for k, v in arrays.items()}
    outs = {"y_out": (P, KT, TOK), "k_out": (L, P, CTX), "v_out": (L, P, CTX), "ssd_out": (L, P, 384),
            "rwkv_out": (L, P, 256)}

    nc = bacc.Bacc("TRN2", target_bir_lowering=False, num_devices=1)
    args = [nc.dram_tensor(k, v.shape, F32, kind="ExternalInput").ap() for k, v in arrays.items()]
    args += [nc.dram_tensor(k, s, F32, kind="ExternalOutput").ap() for k, s in outs.items()]
    build(nc, *args)
    r = run_bass_kernel_spmd(nc, [arrays], core_ids=[0]).results[0]

    y = r["y_out"].transpose(2, 1, 0).reshape(TOK, D)
    new_k = r["k_out"].transpose(0, 2, 1).reshape(1, L, CTX, 2, HD)
    new_v = r["v_out"].transpose(0, 2, 1).reshape(1, L, CTX, 2, HD)
    new_ssd = r["ssd_out"].reshape(L, 2, HD, 2, 3, HD).transpose(0, 3, 1, 4, 5, 2).reshape(1, L, 2, 6, HD, HD)
    new_rwkv = r["rwkv_out"].reshape(L, 2, HD, 2, 2, HD).transpose(0, 3, 4, 1, 5, 2).reshape(1, L, 2, 4, HD, HD)
    return (y[None, :CTX], y[None, CTX:], new_k, new_v, new_ssd, new_rwkv)
```

```python
from contextlib import ExitStack

import numpy as np

import concourse.bass as bass
import concourse.mybir as mybir

ALU = mybir.AluOpType
ACT = mybir.ActivationFunctionType
F32 = mybir.dt.float32
F32R = mybir.dt.float32r
AX = mybir.AxisListType

P = 128
D = 1024
KT = D // P
DEPTH = 2
CTX = 128
LAT = 512
TOK = CTX + LAT
NCH = TOK // P
HALVES = ((0, TOK // 2), (TOK // 2, TOK))
GRID_W = 64
HD = 64
ROPE_BASE = 10000.0
ATT_H = 6
ATT_T = 3
SSD_H = 6
RW_H = 4
CONV = 5
FFN_T = 22
ALPHA = (2 * DEPTH) ** 0.25
LN_EPS = 1e-5
GN_EPS = 64e-5
SCALE = HD ** -0.5
NEG_BIG = -1e30
DECAY = float(np.exp(np.float32(-0.5)))

TQ, TK_, TV, TZ, TX, TB, TC, TR, TKK, TVV, TWA, TG = 0, 3, 4, 5, 8, 11, 12, 13, 15, 17, 19, 20
N_IN = 21
PW = TOK + 6
CTX0, LAT0 = 2, CTX + 4

SHIFT_ORDER = (TWA - TR, TG - TR, TKK - TR, TKK + 1 - TR, 0, 1, TVV - TR, TVV + 1 - TR)

SLOT = 8 * 256
RING = 2
MOD_T = 48
MOD_AT = 384
MOD_SLOTS = 24
MOD_FIRST = 8
IN_SLOTS, OUT_SLOTS, UP_SLOTS, DOWN_PAIRS, DOWN_PARTS = 11, 4, FFN_T, 4, 3

VEC = {}
_n = 0
for _name, _cols in (("convw", CONV * 5), ("convb", 5), ("d", 3), ("normw", 3), ("mu", 8),
                     ("w0", 4), ("a0", 4), ("kk", 2), ("ka", 2), ("rk", 2), ("gnw", 2), ("gnb", 2),
                     ("ln1w", 8), ("ln1b", 8), ("ln2w", 8), ("ln2b", 8)):
    VEC[_name] = _n
    _n += _cols
NVEC = _n

CON = {}
_n = 0
for _name, _cols in (("ident", P), ("ones", P), ("blk", P), ("perm", P), ("incf", P), ("incb", P),
                     ("strf", P), ("strb", P), ("lvl", 7 * P), ("gmf", 2 * P), ("gmb", 2 * P),
                     ("bprev", P), ("bnext", P), ("cos", LAT), ("sin", LAT), ("reset", TOK), ("eps", 4)):
    CON[_name] = _n
    _n += _cols
NCON = _n

NROW = ATT_H + 4 * SSD_H
N_SMALL = 7


def stream_order():
    use = [("mod", 0, i) for i in range(MOD_FIRST)]
    for l in range(DEPTH):
        use += [("in", l, i) for i in range(IN_SLOTS)]
        use += [("mod", l, i) for i in range(MOD_FIRST, MOD_SLOTS)]
        if l + 1 < DEPTH:
            use += [("mod", l + 1, i) for i in range(MOD_FIRST)]
        use += [("out", l, i) for i in range(OUT_SLOTS)]
        use += [("up", l, i) for i in range(UP_SLOTS)]
        use += [("down", l, i) for i in range(DOWN_PAIRS * DOWN_PARTS)]
    return use


SCR_SIZE = 11776


def place(*sizes):
    at, out = 0, {}
    for name, size in sizes:
        out[name] = at
        at += size
    assert at <= SCR_SIZE, at
    return out


SA_ = place(("vt", 640), ("e", 2048), ("et", 2048), ("osb", 384), ("rot", 1024), ("nm", 30), ("mx", 30),
            ("sum", 30), ("es", 30), ("den", 30), ("nms", 30))
SS_ = place(("xb", 2560), ("cs0", 384), ("cs", 1536), ("sp", 1920), ("ea", 768), ("g", 1536), ("cbm", 512),
            ("xd", 768), ("t1", 768), ("y", 384), ("small", 640))
SR_ = place(("ar", 2560), ("gb", 2048), ("gk", 2048), ("m", 1024), ("mt", 1024), ("x", 1024),
            ("tok", 1024), ("s", 256), ("s0", 256), ("small", 160))
ST_ = place(("ar", 2560), ("sw", 2560), ("sa", 2560), ("kk", 1280), ("l", 640), ("t1", 640),
            ("kd", 1280))


ARENA = max(2 * KT * TOK, SCR_SIZE) + 4 * SLOT


def nc_offset(nc, tensor):
    return nc.sbuf_base - 4 * ARENA


class Track:

    def __init__(self, eng, own):
        self.eng, self.own_sem, self.count, self.last = eng, own, {}, None

    def sig(self, ins, sem):
        ins.then_inc(sem, 1)
        self.count[id(sem)] = self.count.get(id(sem), 0) + 1
        self.last = (sem, self.count[id(sem)])

    def own(self, ins):
        self.sig(ins, self.own_sem)

    def hold(self):
        self.eng.wait_ge(*self.last)


def build(nc, stream, xin, consts, conds, bmods, vecs, rows, kctx, vctx, lora, gup, ssd0, rwkv0,
          y_out, k_out, v_out, ssd_out, rwkv_out):
    ctx = ExitStack()
    with ctx:
        def sb(name, shape):
            return ctx.enter_context(nc.sbuf_tensor(name, shape, F32))

        def sem(name):
            return ctx.enter_context(nc.semaphore(name))

        def at(name, shape, offset, dtype=F32):
            return nc.alloc_sbuf_tensor_at(name, shape, dtype, offset=offset)

        xt = sb("xt", [P, KT, TOK])
        proj = sb("proj", [P, N_IN + 1, PW])
        ring = sb("ring", [P, RING, KT, 256])
        arena = ctx.enter_context(nc.sbuf_tensor("arena", [P, ARENA], F32))
        base = nc_offset(nc, arena)
        xh = at("xh", [P, KT, TOK], base, F32R)
        xl = at("xl", [P, KT, TOK], base + 4 * KT * TOK, F32R)
        scr = at("scr", [P, SCR_SIZE], base)
        wbase = base + 4 * max(2 * KT * TOK, SCR_SIZE)
        wh = at("wh", [P, 2, KT, 256], wbase, F32R)
        wl = at("wl", [P, 2, KT, 256], wbase + 8 * SLOT, F32R)
        mix = at("mix", [P, KT, TOK], wbase)
        tail = at("tail", [P, 3072], wbase + 4 * KT * TOK)
        con = sb("con", [P, NCON])
        vc = sb("vc", [P, NVEC])
        bm = sb("bm", [P, DEPTH, MOD_T])
        row = sb("row", [P, NROW + ATT_H])
        kc = sb("kc", [P, CTX])
        vcx = sb("vcx", [P, P])
        lo = sb("lo", [P, 2, 256])
        gu = sb("gu", [P, 256])
        mod = sb("mod", [P, MOD_T, 2])
        cond = sb("cond", [P, KT, 2])
        rawh = sb("rawh", [P, 2, TOK])
        dtr = sb("dtr", [P, NCH, 12])
        t2 = sb("t2", [P, 2, TOK])
        rstd = sb("rstd", [P, TOK])
        mus = sb("mus", [P, 24])
        both = sb("both", [P, 2, KT, 2])
        dec = sb("dec", [P, 2, 4, NCH])
        init_rw = sb("init_rw", [P, 256])
        fin_rw = sb("fin_rw", [P, 256])
        ps = ctx.enter_context(nc.psum_tensor("ps", [P, 8, 512], F32))
        psf = ps[:].rearrange("p b n -> p (b n)")
        pflat = proj[:].rearrange("p t n -> p (t n)")

        def C(name, n=P, j=0):
            a = CON[name] + j * n
            return con[:, a:a + n]

        def V(name, j=0, n=1):
            return vc[:, VEC[name] + j:VEC[name] + j + n]

        def pair(i):
            return psf[:, 1024 * i + 192:1024 * i + 832]

        def chunks(i):
            return psf[:, 1024 * i + 384:1024 * i + 1024]

        def bank(i, n=512, a=0):
            return ps[:, i, a:a + n]

        def S(where, name, n, a=0):
            a = where[name] + a
            return scr[:, a:a + n]

        def T(t):
            return proj[:, t, 0:TOK]

        def ch(t, c):
            return proj[:, t, P * c:P * c + P]

        s_const = sem("s_const")
        s_x = sem("s_x")
        s_small = sem("s_small")
        s_slot = [sem(f"s_slot{i}") for i in range(RING)]
        s_init = sem("s_init")
        s_out = sem("s_out")
        s_y = sem("s_y")
        s_pe = sem("s_pe")
        s_act = sem("s_act")
        s_dve = sem("s_dve")
        s_pool = sem("s_pool")
        s_bar = sem("s_bar")
        s_dense = sem("s_dense")
        s_free = [sem("s_free_a"), sem("s_free_a2"), sem("s_free_v")]
        s_whigh = sem("s_whigh")
        s_wlow = sem("s_wlow")
        s_hhigh = sem("s_hhigh")
        s_hid_high = sem("s_hid_high")
        s_hid = sem("s_hid")
        s_hid_used = sem("s_hid_used")
        s_cond = sem("s_cond")
        s_modps = sem("s_modps")
        s_modrow = [sem("s_modrow_v"), sem("s_modrow_a")]
        s_modt = sem("s_modt")
        s_mod = sem("s_mod")
        s_h = sem("s_h")
        s_res = sem("s_res")
        s_mu = sem("s_mu")
        s_cen = sem("s_cen")
        s_sq = sem("s_sq")
        s_var = sem("s_var")
        s_std = sem("s_std")
        s_hat = sem("s_hat")
        s_raw = sem("s_raw")
        s_sum = sem("s_sum")
        s_ln = sem("s_ln")
        a_v = sem("a_v")
        a_vt = sem("a_vt")
        a_rot = sem("a_rot")
        a_rope = sem("a_rope")
        a_score = sem("a_score")
        a_max = sem("a_max")
        a_exp = sem("a_exp")
        a_tr = sem("a_tr")
        a_trsb = sem("a_trsb")
        a_pv = sem("a_pv")
        a_nms = sem("a_nms")
        a_es = sem("a_es")
        a_on = sem("a_on")
        a_ot = sem("a_ot")
        a_out = sem("a_out")
        c_conv = sem("c_conv")
        c_silu = sem("c_silu")
        c_dtx = sem("c_dtx")
        c_dte = sem("c_dte")
        c_a = sem("c_a")
        c_cum = sem("c_cum")
        c_ecum = sem("c_ecum")
        c_dtend = sem("c_dtend")
        c_tr = sem("c_tr")
        c_xb = sem("c_xb")
        c_xe = sem("c_xe")
        c_st = sem("c_st")
        c_cs = sem("c_cs")
        c_sp = sem("c_sp")
        c_cb = sem("c_cb")
        c_cbm = sem("c_cbm")
        c_rh = sem("c_rh")
        c_arg = sem("c_arg")
        c_ea = sem("c_ea")
        c_g = sem("c_g")
        c_xd = sem("c_xd")
        c_off = sem("c_off")
        c_y = sem("c_y")
        c_ytok = sem("c_ytok")
        c_yt = sem("c_yt")
        c_yf = sem("c_yf")
        c_gate = sem("c_gate")
        c_sq = sem("c_sq")
        c_var = sem("c_var")
        c_std = sem("c_std")
        r_mu = sem("r_mu")
        r_sum = sem("r_sum")
        r_scl = sem("r_scl")
        r_shift = sem("r_shift")
        r_act = sem("r_act")
        r_wps = sem("r_wps")
        r_sig = sem("r_sig")
        r_gps = sem("r_gps")
        r_g = sem("r_g")
        r_ksq = sem("r_ksq")
        r_kps = sem("r_kps")
        r_kstd = sem("r_kstd")
        r_kk = sem("r_kk")
        r_cum = sem("r_cum")
        r_exp = sem("r_exp")
        r_kd = sem("r_kd")
        r_bon = sem("r_bon")
        r_bps = sem("r_bps")
        r_bv = sem("r_bv")
        r_v = sem("r_v")
        r_vt = sem("r_vt")
        r_gmat = sem("r_gmat")
        r_gsb = sem("r_gsb")
        r_lvl = sem("r_lvl")
        r_mt0 = sem("r_mt0")
        r_m0ps = sem("r_m0ps")
        r_m0 = sem("r_m0")
        r_xps = sem("r_xps")
        r_xsb = sem("r_xsb")
        r_mps = sem("r_mps")
        r_msb = sem("r_msb")
        r_tps = sem("r_tps")
        r_tsb = sem("r_tsb")
        r_tkps = sem("r_tkps")
        r_tk = sem("r_tk")
        r_s0 = sem("r_s0")
        r_rps = sem("r_rps")
        r_rsb = sem("r_rsb")
        r_ups = sem("r_ups")
        r_nu = sem("r_nu")
        r_ops2 = sem("r_ops2")
        r_sps = sem("r_sps")
        r_osb = sem("r_osb")
        r_st = sem("r_st")
        r_osq = sem("r_osq")
        r_ovar = sem("r_ovar")
        r_ostd = sem("r_ostd")
        r_on = sem("r_on")
        r_otps = sem("r_otps")

        order = stream_order()
        NS = len(order)
        D_IN, D_OUT, D_UP, D_DOWN = 0, 22, 30, 74
        N_DENSE = 82
        N_BAR = 6

        def barrier(eng, tr, n):
            tr.hold()
            eng.sem_inc(s_bar, 1)
            eng.wait_ge(s_bar, 4 * (n + 1))

        def done(n):
            l, i = divmod(n, N_DENSE)
            return D_DOWN * l + i + 1

        def freed(n):
            l, i = divmod(n, N_DENSE)
            if n % 2 == 0:
                return s_free[0], n // 2 + 1
            if D_UP <= i < D_DOWN:
                return s_free[2], l * FFN_T + (i - D_UP) // 2 + 1
            return s_free[1], (N_DENSE // 2 - FFN_T) * l + (i // 2 if i < D_UP else i // 2 - FFN_T) + 1

        def wait_pair_free(eng, n):
            l, i = divmod(n, N_DENSE)
            if D_DOWN <= i < D_DOWN + 4:
                if i >= D_DOWN + 2:
                    eng.wait_ge(*freed(n - 4))
            elif D_DOWN + 4 <= i:
                eng.wait_ge(*freed(n - 4))
            elif n >= 2:
                eng.wait_ge(*freed(n - 2))

        def down_pair(i):
            return 2 if i % 2 == 0 else 0

        def hid_at(i, k):
            return (FFN_T * i + k) % KT

        def padded(i):
            return TX <= i < N_IN

        def sums_of(u):
            if u % 2:
                return tail[:, 0:TOK], tail[:, TOK:2 * TOK], rawh[:, 1]
            return S(ST_, "l", TOK), S(ST_, "t1", TOK), rawh[:, 0]

        RW_UNITS = [(d, hp) for d in range(2) for hp in range(2)]

        def op_blocks(which, d, hp):
            i = (4 if which else 0) + 2 * d + hp
            if i < 6:
                a = pflat[:, 1280 * i:1280 * i + 1280]
            else:
                a = S(SR_, "ar", 1280, 1280 * (i - 6))
            return a.rearrange("p (c n) -> p c n", c=NCH)

        VTOK = pflat[:, TKK * PW:TKK * PW + 1280].rearrange("p (c n) -> p c n", c=NCH)
        OTOK = pflat[:, TR * PW:TR * PW + 1280].rearrange("p (c n) -> p c n", c=NCH)

        def s0(d, hp):
            return S(SR_, "s0", HD, HD * (2 * d + hp))

        def lv_(d):
            return t2[:, d, 0:512]

        def xs(which, n, a):
            return tail[:, 2048 + 512 * which + a:2048 + 512 * which + a + n]

        def lvl_count(l, i, d, j):
            return 14 * (NCH * l + i) + 2 * j + d + 1

        def x_count(l, i, d, j):
            return 12 * (NCH * l + i) + 2 * (j - 1) + d + 1

        def turn_count(l, i, d, j):
            return 10 * (NCH * l + i) + 2 * (j - 1) + d + 1

        def token_chunk(i, d):
            return 0 if i == 0 else (NCH - i if d else i)

        def gb_of(i, d):
            return S(SR_, "gb", 1024, 1024 * d) if i % 2 == 0 else tail[:, 1024 * d:1024 * d + 1024]

        def gk_of(i, d):
            if i % 2 == 0:
                return S(SR_, "gk", 1024, 1024 * d)
            if d == 0:
                return rawh[:].rearrange("p a n -> p (a n)")[:, 0:1024]
            return pflat[:, TVV * PW:TVV * PW + 1024]

        def mt_of(i, d):
            if i % 2 == 0:
                return S(SR_, "mt", 512, 512 * d)
            a = N_IN * PW if d else 6 * 2 * TOK
            return pflat[:, a:a + 512]

        used_by, mods, dense_slots = [], 0, 0
        split_slots = []
        for n, (kind, l, i) in enumerate(order):
            if kind == "mod":
                mods += 1
                used_by.append((s_modps, mods))
            else:
                dense_slots += 1
                used_by.append((s_wlow, dense_slots))
                split_slots.append((n, kind, l, i))
        PER_DENSE = IN_SLOTS + OUT_SLOTS + UP_SLOTS + DOWN_PAIRS * DOWN_PARTS

        def slot_read(q):
            n, kind, l, i = split_slots[q]
            if kind == "down":
                mp, part = divmod(i, DOWN_PARTS)
                return s_hid_used, (DOWN_PAIRS * l + mp) * FFN_T + min(KT * part + KT, FFN_T)
            first = {"in": D_IN, "out": D_OUT, "up": D_UP}[kind]
            return s_dense, D_DOWN * l + first + 2 * i + 2

        split_after = {KT - 3: 1, 2 * KT - 3: 2, FFN_T - 1: 3}

        def mod_to_h(e):
            g, k = divmod(e, KT)
            return KT * (g + (g + 1) // 2) + k + 1

        block = ctx.enter_context(nc.Block())

        @block.sync
        def _(sp):
            sp.dma_start(con[:], consts).then_inc(s_const, 16)
            sp.dma_start(cond[:], conds).then_inc(s_const, 16)
            sp.dma_start(bm[:], bmods).then_inc(s_const, 16)
            for n in range(NS):
                if n == MOD_FIRST // 2:
                    sp.dma_start(xt[:], xin).then_inc(s_x, 16)
                if n >= RING:
                    sp.wait_ge(*used_by[n - RING])
                sp.dma_start(ring[:, n % RING].rearrange("p k n -> p (k n)"), stream[n])\
                  .then_inc(s_slot[n % RING], 16)
            for k in range(KT):
                sp.wait_ge(s_ln, 8 * (2 * DEPTH - 1) + k + 1)
                sp.dma_start(y_out[:, k], xt[:, k]).then_inc(s_y, 16)
            sp.wait_ge(s_y, 16 * KT)
            sp.wait_ge(s_out, 64 * DEPTH)

        @block.tensor
        def _(pe):
            tr = Track(pe, s_pe)
            mm = nc.tensor.matmul
            nbar = [0]

            def bar():
                barrier(pe, tr, nbar[0])
                nbar[0] += 1

            def take(l, i):
                n = order.index(("mod", l, i))
                pe.wait_ge(s_slot[n % RING], 16 * (n // RING + 1))
                return ring[:, n % RING]

            def tp(out, in_):
                return nc.tensor.transpose(out, in_, C("ident"))

            turned = [0, 0]

            def mod_rows(l, i, b, ks=range(KT)):
                w = take(l, i)
                for k in ks:
                    ins = mm(ps[0:2, b, 0:256], cond[:, k, :], w[:, k, :], start=(k == 0), stop=(k == KT - 1))
                if ks[-1] == KT - 1:
                    tr.sig(ins, s_modps)

            def mod_turn(i):
                first = i < MOD_FIRST
                turned[first] += 1
                pe.wait_ge(s_modrow[first], turned[first])
                for j in range(2):
                    ins = nc.tensor.transpose(bank(7, 2, MOD_AT + 2 * (2 * i + j)),
                                              t2[0:2, i % 2, P * j:P * j + P], C("ident")[0:2, 0:2])
                tr.sig(ins, s_modt)

            def mod_first(l):
                for i in range(MOD_FIRST):
                    mod_rows(l, i, 5 + i % 2)
                    if i:
                        mod_turn(i - 1)
                mod_turn(MOD_FIRST - 1)

            dense_slot = [0]

            def take_split():
                q = dense_slot[0]
                dense_slot[0] += 1
                pe.wait_ge(s_wlow, q + 1)
                return q % 2

            def terms(out, a_hi, a_lo, b_hi, b_lo, first, last):
                mm(out, a_hi, b_hi, start=first, stop=False)
                mm(out, a_lo, b_hi, start=False, stop=False)
                return mm(out, a_hi, b_lo, start=False, stop=last)

            def dense_step(n, w, col, k):
                for a, b in HALVES:
                    ins = terms(pair(n % 2)[:, a:b], wh[:, w, k, col:col + P], wl[:, w, k, col:col + P],
                                xh[:, k, a:b], xl[:, k, a:b], k == 0, k == KT - 1)
                if k == KT - 1:
                    tr.sig(ins, s_dense)

            def dense(n, w, col):
                wait_pair_free(pe, n)
                for k in range(KT):
                    dense_step(n, w, col, k)

            def dense_first(n, first):
                w = take_split()
                wait_pair_free(pe, n)
                wait_pair_free(pe, n + 1)
                for k in range(KT):
                    pe.wait_ge(s_h, first + k + 1)
                    dense_step(n, w, 0, k)
                    dense_step(n + 1, w, P, k)

            pe.wait_ge(s_const, 48)
            pe.wait_ge(s_cond, 1)
            mod_first(0)

            def norm(n, last):
                pe.wait_ge(*freed(last))
                pe.wait_ge(*freed(last - 1))
                pe.wait_ge(s_sum, n + 1)
                for a, b in HALVES:
                    ins = mm(pair(2)[:, a:b], C("ones"), rstd[:, a:b], start=True, stop=True)
                tr.sig(ins, s_mu)
                for k in range(KT):
                    pe.wait_ge(s_sq, KT * n + k + 1)
                    for a, b in HALVES:
                        ins = mm(pair(3)[:, a:b], C("ones"), t2[:, k % 2, a:b], start=(k == 0),
                                 stop=(k == KT - 1))
                    tr.sig(ins, s_var)

            def attention(l):
                for c in range(NCH):
                    ins = tp(psf[:, P * c:P * c + P], ch(TV, c))
                tr.sig(ins, a_v)
                for t in range(4):
                    if t >= 2:
                        pe.wait_ge(a_rope, 4 * l + t - 1)
                    tr.sig(mm(bank(2 + t % 2), C("perm"), proj[:, TQ + t, CTX:TOK], start=True, stop=True),
                           a_rot)

                def keys(qb):
                    if qb == 0:
                        return []
                    n = qb - 1
                    return list(range(max(n - 1, 0), min(n + 1, 3) + 1))

                def scores(u):
                    qb, t = divmod(u, ATT_T)
                    if u == 0:
                        pe.wait_ge(a_vt, l + 1)
                        pe.wait_ge(a_rope, 4 * l + 4)
                    if u >= 2:
                        pe.wait_ge(a_exp, 15 * l + u - 1)
                    blocks = keys(qb)
                    for hh in range(2):
                        r = slice(HD * hh, HD * hh + HD)
                        b = 2 * (u % 2) + hh
                        q = ch(TQ + t, qb)[r]
                        own = kc[r, :] if qb else ch(TK_, 0)[r]
                        ins = mm(ps[:, b, 0:CTX], q, own, start=True, stop=True)
                        if blocks:
                            a = CTX + P * blocks[0]
                            ins = mm(ps[:, b, P:P + P * len(blocks)], q,
                                     proj[r, TK_, a:a + P * len(blocks)], start=True, stop=True)
                    tr.sig(ins, a_score)

                def turn(u):
                    qb, t = divmod(u, ATT_T)
                    pe.wait_ge(a_exp, 15 * l + u + 1)
                    if u:
                        pe.wait_ge(a_trsb, 15 * l + u)
                    if t == 1 and qb:
                        pe.wait_ge(a_out, 5 * l + qb)
                    for hh in range(2):
                        for j in range(1 + len(keys(qb))):
                            ins = tp(ps[:, 4 + hh, P * j:P * j + P],
                                     S(SA_, "e", P, 1024 * (u % 2) + 512 * hh + P * j))
                    tr.sig(ins, a_tr)

                def values(u):
                    qb, t = divmod(u, ATT_T)
                    pe.wait_ge(a_trsb, 15 * l + u + 1)
                    if t == 0 and qb:
                        pe.wait_ge(a_on, 5 * l + qb)
                    blocks = keys(qb)
                    for hh in range(2):
                        for j in range(1 + len(blocks)):
                            if j == 0:
                                v = vcx[:, HD * hh:HD * hh + HD] if qb else S(SA_, "vt", HD, HD * hh)
                            else:
                                v = S(SA_, "vt", HD, P * (1 + blocks[j - 1]) + HD * hh)
                            ins = mm(bank(6, HD, P * t + HD * hh),
                                     S(SA_, "et", P, 1024 * (u % 2) + 512 * hh + P * j), v,
                                     start=(j == 0), stop=(j == len(blocks)))
                    tr.sig(ins, a_pv)

                def out(qb):
                    pe.wait_ge(a_on, 5 * l + qb + 1)
                    for t in range(ATT_T):
                        ins = tp(bank(4, P, P * t), S(SA_, "osb", P, P * t))
                    tr.sig(ins, a_ot)

                scores(0)
                for u in range(15):
                    if u + 1 < 15:
                        scores(u + 1)
                    if u:
                        mod_turn(MOD_FIRST + u - 1)
                    mod_rows(l, MOD_FIRST + u, 7, range(KT // 2))
                    turn(u)
                    mod_rows(l, MOD_FIRST + u, 7, range(KT // 2, KT))
                    values(u)
                    if u % 3 == 0 and u:
                        out(u // 3 - 1)
                mod_turn(MOD_SLOTS - 2)
                mod_rows(l, MOD_SLOTS - 1, 7)
                out(4)
                mod_turn(MOD_SLOTS - 1)

            def ssd(l):
                pe.wait_ge(s_mod, 2 * l + 2)
                if l + 1 < DEPTH:
                    mod_first(l + 1)
                pe.wait_ge(c_a, l + 1)
                sm = SS_["small"]
                af, ab = scr[:, sm:sm + 30], scr[:, sm + 30:sm + 60]
                mm(bank(4, 30, 0), C("incf"), af, start=True, stop=True)
                mm(bank(4, 30, 30), C("incb"), ab, start=True, stop=True)
                mm(bank(4, 30, 60), C("strb"), af, start=True, stop=True)
                mm(bank(4, 30, 90), C("strf"), ab, start=True, stop=True)
                ins = mm(bank(4, 60, 120), C("ones"), scr[:, sm:sm + 60], start=True, stop=True)
                tr.sig(ins, c_cum)
                for c in range(NCH):
                    if c == 0:
                        pe.wait_ge(c_silu, 5 * l + 5)
                    if c >= 2:
                        pe.wait_ge(c_xb, 5 * l + c - 1)
                    for i, t in enumerate((TX, TX + 1, TX + 2, TB)):
                        ins = tp(bank(c % 2, P, P * i), ch(t, c))
                    tr.sig(ins, c_tr)
                    if c:
                        states(l, c - 1)
                states(l, NCH - 1)

                def within(c):
                    if c:
                        pe.wait_ge(c_cbm, 5 * l + c)
                    for g in range(2):
                        r = slice(HD * g, HD * g + HD)
                        ins = mm(bank(g, P), ch(TB, c)[r], ch(TC, c)[r], start=True, stop=True)
                    tr.sig(ins, c_cb)
                    pe.wait_ge(c_rh, 5 * l + c + 1)
                    if c:
                        pe.wait_ge(c_ea, 5 * l + c)
                    for g in range(2):
                        mm(bank(2 + g, 384), C("strb"), S(SS_, "cs", 384, 384 * g), start=True, stop=False)
                        ins = mm(bank(2 + g, 384), C("strf"), S(SS_, "cs", 384, 768 + 384 * g),
                                 start=False, stop=True)
                    tr.sig(ins, c_arg)

                def turned(c):
                    pe.wait_ge(c_ytok, 5 * l + c + 1)
                    if c:
                        pe.wait_ge(c_yf, 5 * l + c)
                    for t in range(3):
                        ins = tp(bank(7, P, P * t), S(SS_, "y", P, P * t))
                    tr.sig(ins, c_yt)

                pe.wait_ge(c_xb, 5 * l + 5)
                pe.wait_ge(c_cs, 5 * l + 5)
                pe.wait_ge(c_ecum, l + 1)
                within(0)
                for c in range(NCH):
                    if c + 1 < NCH:
                        within(c + 1)
                    if c:
                        turned(c - 1)
                        if c == 1:
                            pe.wait_ge(c_sp, l + 1)
                        for g in range(2):
                            r = slice(HD * g, HD * g + HD)
                            for d in range(2):
                                a = SS_["sp"] + 960 * d + 192 * c
                                ins = mm(bank(5 + g, 192, 192 * d), ch(TC, c)[r], scr[r, a:a + 192],
                                         start=True, stop=True)
                        tr.sig(ins, c_off)
                    pe.wait_ge(c_g, 5 * l + c + 1)
                    pe.wait_ge(c_xd, 5 * l + c + 1)
                    for hh in range(SSD_H):
                        for d in range(2):
                            ins = mm(bank(4, HD, HD * hh), S(SS_, "g", P, 768 * d + P * hh),
                                     S(SS_, "xd", HD, 384 * d + HD * hh), start=(d == 0), stop=(d == 1))
                    tr.sig(ins, c_y)
                turned(NCH - 1)
                for t in range(3):
                    pe.wait_ge(c_sq, 3 * l + t + 1)
                    for a, b in HALVES:
                        ins = mm(pair(0)[:, a:b], C("ones"), t2[:, t % 2, a:b], start=(t == 0), stop=(t == 2))
                    tr.sig(ins, c_var)

            def states(l, c):
                pe.wait_ge(c_xb, 5 * l + c + 1)
                pe.wait_ge(c_xe, 5 * l + c + 1)
                if c >= 2:
                    pe.wait_ge(c_cs, 5 * l + c - 1)
                for g in range(2):
                    for d in range(2):
                        ins = mm(ps[HD * g:HD * g + HD, 2 + c % 2, 192 * d:192 * d + 192],
                                 S(SS_, "xb", HD, 512 * c + 384 + HD * g),
                                 S(SS_, "xd", 192, 384 * d + 192 * g), start=True, stop=True)
                tr.sig(ins, c_st)

            def rwkv_features(l):
                if l + 1 < DEPTH:
                    pe.wait_ge(s_mod, 2 * l + 3)
                for hp in range(2):
                    pe.wait_ge(r_ksq, 2 * l + hp + 1)
                    for a, b in HALVES:
                        ins = mm(pair(2 + hp)[:, a:b], C("blk"), t2[:, hp, a:b], start=True, stop=True)
                    tr.sig(ins, r_kps)
                pe.wait_ge(r_act, 2 * l + 2)
                for i, (d, hp) in enumerate(RW_UNITS):
                    for w in range(2):
                        if i:
                            pe.wait_ge(r_sig, 8 * l + 2 * (i - 1) + w + 1)
                        r = slice(HD * w, HD * w + HD)
                        for a, b in HALVES:
                            ins = mm(pair(w)[:, a:b], lo[r, d, P * hp:P * hp + P], T(TWA)[r, a:b],
                                     start=True, stop=True)
                        tr.sig(ins, r_wps)
                for hp in range(2):
                    pe.wait_ge(r_kstd, 2 * l + hp + 1)
                    for a, b in HALVES:
                        ins = mm(pair(2 + hp)[:, a:b], gu[:, P * hp:P * hp + P], T(TG)[:, a:b],
                                 start=True, stop=True)
                    tr.sig(ins, r_gps)
                for hp in range(2):
                    pe.wait_ge(r_bon, 2 * l + hp + 1)
                    pe.wait_ge(r_g, 2 * l + hp + 1)
                    for a, b in HALVES:
                        ins = mm(pair(2 + hp)[:, a:b], C("blk"), T(TWA + hp)[:, a:b], start=True, stop=True)
                    tr.sig(ins, r_bps)

            def rwkv_scan(l):
                for c in range(NCH):
                    for hp in range(2):
                        ins = tp(psf[:, 256 * c + P * hp:256 * c + P * hp + P], ch(TVV + hp, c))
                tr.sig(ins, r_v)

                def products(i, d):
                    n = 10 * l + 2 * i + d
                    if n % 10 == 0:
                        pe.wait_ge(r_vt, l + 1)
                    else:
                        pe.wait_ge(r_gsb, 2 * n)
                    if d == 0 and i >= 2:
                        pe.wait_ge(r_osb, 5 * l + i - 1)
                    for w in range(2):
                        for hp in range(2):
                            for par in range(2):
                                r = slice(HD * par, HD * par + HD)
                                ins = mm(bank(2 * w + par, 256, 256 * hp),
                                         op_blocks(0, d, hp)[r, token_chunk(i, d), P * w:P * w + P],
                                         op_blocks(1, d, hp)[r, token_chunk(i, d), :], start=True, stop=True)
                        tr.sig(ins, r_gmat)

                def level_x(i, j):
                    for d in range(2):
                        if j == 1:
                            pe.wait_ge(r_m0, 10 * l + 2 * i + d + 1)
                        else:
                            pe.wait_ge(r_msb, x_count(l, i, d, j - 1))
                        pe.wait_ge(r_lvl, lvl_count(l, i, d, j))
                        for q in range(4):
                            ins = mm(bank(4 + 2 * d, P, P * q), lv_(d)[:, P * q:P * q + P],
                                     S(SR_, "m", P, 512 * d + P * q), start=True, stop=True)
                        tr.sig(ins, r_xps)
                        if j > 1:
                            for q in range(4):
                                ins = tp(bank(5 + 2 * d, P, P * q), S(SR_, "m", P, 512 * d + P * q))
                            tr.sig(ins, r_tps)

                def level_m(i, j):
                    for d in range(2):
                        pe.wait_ge(r_xsb, x_count(l, i, d, j))
                        if j > 1:
                            pe.wait_ge(r_tsb, turn_count(l, i, d, j - 1))
                        for q in range(4):
                            x = S(SR_, "x", P, 512 * d + P * q)
                            mt = mt_of(i, d)[:, P * q:P * q + P]
                            if j < 6:
                                ins = mm(bank(5 + 2 * d, P, P * q), mt, x, start=True, stop=True)
                            else:
                                ins = mm(bank(5 + 2 * d, P, P * q), x, mt, start=True, stop=True)
                        tr.sig(ins, r_mps)

                def start_inverse(i):
                    for d in range(2):
                        n = 10 * l + 2 * i + d
                        pe.wait_ge(r_mt0, n + 1)
                        if i:
                            pe.wait_ge(r_msb, x_count(l, i - 1, d, 6))
                        for q in range(4):
                            ins = tp(bank(5 + 2 * d, P, P * q), mt_of(i, d)[:, P * q:P * q + P])
                        tr.sig(ins, r_m0ps)

                def chain_right(c):
                    pe.wait_ge(r_gsb, 4 * (5 * l + min(c + 2, NCH)))
                    for d in range(2):
                        for w in range(2):
                            for hp in range(2):
                                ins = tp(bank(d, P, 256 * w + P * hp),
                                         op_blocks(0, d, hp)[:, token_chunk(c, d), P * w:P * w + P])
                    tr.sig(ins, r_tkps)
                    if c:
                        pe.wait_ge(r_s0, 4 * l + c)
                        pe.wait_ge(r_osb, 5 * l + c)
                    for par in range(2):
                        r = slice(HD * par, HD * par + HD)
                        for d in range(2):
                            for hp in range(2):
                                o = bank(2 + par, HD, HD * (2 * d + hp))
                                if c:
                                    mm(o, op_blocks(1, d, hp)[r, token_chunk(c, d), 0:P],
                                       s0(d, hp)[r], start=True, stop=False)
                                a = 512 * par + 256 * hp
                                ins = mm(o, gk_of(c, d)[:, a:a + P],
                                         VTOK[:, token_chunk(c, d), HD * (2 * hp + par):HD * (2 * hp + par) + HD],
                                         start=(c == 0), stop=True)
                    tr.sig(ins, r_rps)

                def chain_solve(c):
                    pe.wait_ge(r_tk, 5 * l + c + 1)
                    pe.wait_ge(r_rsb, 5 * l + c + 1)
                    pe.wait_ge(r_msb, x_count(l, c, 1, 6))
                    for par in range(2):
                        for d in range(2):
                            for hp in range(2):
                                k = 4 * par + 2 * d + hp
                                a = 256 * par + P * hp
                                ins = mm(bank(0, HD, HD * k), mt_of(c, d)[:, a:a + P], xs(0, HD, HD * k),
                                         start=True, stop=True)
                    tr.sig(ins, r_ups)

                def chain_state(c):
                    pe.wait_ge(r_nu, 5 * l + c + 1)
                    for par in range(2):
                        for d in range(2):
                            for hp in range(2):
                                k = 4 * par + 2 * d + hp
                                o = ps[HD * par:HD * par + HD, 1, HD * (2 * d + hp):HD * (2 * d + hp) + HD]
                                a = 512 * d + P * hp + HD * par
                                mm(o, S(SR_, "tok", HD, a + 256),
                                   VTOK[:, token_chunk(c, d), HD * (2 * hp + par):HD * (2 * hp + par) + HD],
                                   start=True, stop=False)
                                ins = mm(o, S(SR_, "tok", HD, a), xs(1, HD, HD * k), start=False, stop=True)
                    tr.sig(ins, r_sps)

                def chain_out(c, par):
                    r = slice(HD * par, HD * par + HD)
                    for d in range(2):
                        for hp in range(2):
                            k = 4 * par + 2 * d + hp
                            o = bank(2 + par, HD, HD * (2 * d + hp))
                            a = 512 * par + 256 * hp + P
                            if c:
                                mm(o, op_blocks(1, d, hp)[r, token_chunk(c, d), P:2 * P], s0(d, hp)[r],
                                   start=True, stop=False)
                            mm(o, gk_of(c, d)[:, a:a + P],
                               VTOK[:, token_chunk(c, d), HD * (2 * hp + par):HD * (2 * hp + par) + HD],
                               start=(c == 0), stop=False)
                            ins = mm(o, gb_of(c, d)[:, a:a + P], xs(1, HD, HD * k), start=False, stop=True)
                    if par:
                        tr.sig(ins, r_ops2)

                products(0, 0)
                products(0, 1)
                for i in range(NCH + 1):
                    inv, chain, ahead = i < NCH, i > 0, i + 1 < NCH
                    if chain:
                        chain_right(i - 1)
                    if inv:
                        start_inverse(i)
                        level_x(i, 1)
                    if chain:
                        chain_solve(i - 1)
                    if inv:
                        level_m(i, 1)
                        level_x(i, 2)
                    if chain:
                        chain_state(i - 1)
                    if inv:
                        level_m(i, 2)
                        level_x(i, 3)
                    if chain:
                        chain_out(i - 1, 0)
                    if inv:
                        level_m(i, 3)
                        level_x(i, 4)
                    if chain:
                        chain_out(i - 1, 1)
                    if inv:
                        level_m(i, 4)
                        level_x(i, 5)
                        if ahead:
                            products(i + 1, 0)
                        level_m(i, 5)
                        level_x(i, 6)
                        if ahead:
                            products(i + 1, 1)
                        level_m(i, 6)
                pe.wait_ge(r_on, l + 1)
                for c in range(NCH):
                    for hp in range(2):
                        ins = tp(chunks(hp)[:, P * c:P * c + P], OTOK[:, c, P * hp:P * hp + P])
                tr.sig(ins, r_otps)

            for l in range(DEPTH):
                base = N_DENSE * l
                dense_first(base, 3 * l * KT)
                for i in range(1, IN_SLOTS):
                    w = take_split()
                    for j in range(2):
                        t = 2 * i + j
                        if t < N_IN:
                            dense(base + t, w, P * j)
                        else:
                            wait_pair_free(pe, base + t)
                            for c in range(NCH):
                                for k in range(KT):
                                    ins = terms(psf[:, 1024 + 12 * c:1024 + 12 * c + 12],
                                                xh[:, k, P * c:P * c + P], xl[:, k, P * c:P * c + P],
                                                wh[:, w, k, P:P + 12], wl[:, w, k, P:P + 12],
                                                k == 0, k == KT - 1)
                            tr.sig(ins, s_dense)
                bar()
                attention(l)
                bar()
                ssd(l)
                bar()
                rwkv_features(l)
                bar()
                rwkv_scan(l)
                bar()
                dense_first(base + D_OUT, (3 * l + 1) * KT)
                for i in range(1, OUT_SLOTS):
                    w = take_split()
                    for j in range(2):
                        dense(base + D_OUT + 2 * i + j, w, P * j)
                norm(2 * l, base + D_UP - 1)
                dense_first(base + D_UP, (3 * l + 2) * KT)
                for i in range(1, UP_SLOTS):
                    w = take_split()
                    for j in range(2):
                        dense(base + D_UP + 2 * i + j, w, P * j)
                for i in range(DOWN_PAIRS):
                    accs = [pair(down_pair(i) + j) for j in range(2)]
                    for j in range(2):
                        wait_pair_free(pe, base + D_DOWN + 2 * i + j)
                    for k in range(FFN_T):
                        if k % KT == 0:
                            w = take_split()
                        e = (DOWN_PAIRS * l + i) * FFN_T + k
                        pe.wait_ge(s_hid, e + 1)
                        for j in range(2):
                            col = P * j
                            for a, b in HALVES:
                                ins = terms(accs[j][:, a:b], wh[:, w, k % KT, col:col + P],
                                            wl[:, w, k % KT, col:col + P], xh[:, hid_at(i, k), a:b],
                                            xl[:, hid_at(i, k), a:b], k == 0, k == FFN_T - 1)
                        tr.sig(ins, s_hid_used)
                norm(2 * l + 1, base + D_DOWN + 5)
                bar()

        @block.scalar
        def _(act):
            tr = Track(act, s_act)
            nbar = [0]

            def bar():
                barrier(act, tr, nbar[0])
                nbar[0] += 1

            def A(out, in_, f, bias=0.0, scale=1.0, **kw):
                return nc.scalar.activation(out, in_, f, bias=bias, scale=scale, **kw)

            def split_high(q):
                if q >= len(split_slots):
                    return
                n = split_slots[q][0]
                act.wait_ge(s_slot[n % RING], 16 * (n // RING + 1))
                if q >= 2:
                    act.wait_ge(*slot_read(q - 2))
                tr.sig(nc.scalar.copy(wh[:, q % 2], ring[:, n % RING]), s_whigh)

            def evict(n, out):
                act.wait_ge(s_dense, done(n))
                acc = pair(n % 2)
                if out is None:
                    return acc
                i = n % N_DENSE
                if padded(i):
                    tr.own(nc.scalar.copy(proj[:, i, CTX0:CTX0 + CTX], acc[:, 0:CTX]))
                    ins = nc.scalar.copy(proj[:, i, LAT0:LAT0 + LAT], acc[:, CTX:TOK])
                else:
                    ins = nc.scalar.copy(out, acc)
                tr.sig(ins, s_free[n % 2])

            def modulate(k, e, scale, shift):
                if e >= 2:
                    act.wait_ge(s_h, mod_to_h(e - 2))
                for c, (a, b) in ((1, (CTX, TOK)), (0, (0, CTX))):
                    ins = A(rawh[:, k % 2, a:b], xt[:, k, a:b], ACT.Identity, bias=shift[:, k, c:c + 1],
                            scale=scale[:, k, c:c + 1])
                    if c:
                        tr.own(ins)
                tr.sig(ins, s_raw)
                tr.hold()
                tr.sig(nc.scalar.copy(xh[:, k], rawh[:, k % 2]), s_hhigh)

            def gated(n, k, gate, group, pr=None):
                if pr is None:
                    act.wait_ge(s_dense, done(n))
                    pr = n % 2
                g = KT * group + k
                if g >= 2:
                    act.wait_ge(s_res, g - 1)
                if k < 2 and group:
                    act.wait_ge(s_var, KT * group)
                acc = pair(pr)
                tr.own(A(t2[:, k % 2, CTX:TOK], acc[:, CTX:TOK], ACT.Copy, scale=mod[:, gate + k, 1:2]))
                tr.sig(A(t2[:, k % 2, 0:CTX], acc[:, 0:CTX], ACT.Copy, scale=mod[:, gate + k, 0:1]),
                       s_free[n % 2])

            def norm(group, modulate_next, q):
                for k in range(KT):
                    act.wait_ge(s_cen, KT * group + k + 1)
                    if k >= 2:
                        act.wait_ge(s_var, KT * group + k - 1)
                    tr.sig(A(t2[:, k % 2], xt[:, k], ACT.Square), s_sq)
                    if k == 1:
                        split_high(q)
                act.wait_ge(s_var, KT * group + KT)
                tr.sig(A(rstd[:], pair(3), ACT.Sqrt, bias=C("eps", 1)), s_std)
                if modulate_next:
                    for k in range(KT):
                        act.wait_ge(s_hat, KT * group + k + 1)
                        modulate(k, KT * (group + 1) + k, both[:, 0], both[:, 1])

            mod_rows = [0]

            def mod_row(l):
                if l < DEPTH and mod_rows[0] < MOD_FIRST * (l + 1):
                    i = mod_rows[0] % MOD_FIRST
                    mod_rows[0] += 1
                    act.wait_ge(s_modps, MOD_SLOTS * l + i + 1)
                    tr.sig(nc.scalar.copy(t2[0:2, i % 2, 0:256], ps[0:2, 5 + i % 2, 0:256]), s_modrow[1])

            act.wait_ge(s_const, 48)
            tr.sig(A(cond[:], cond[:], ACT.Silu), s_cond)
            for _ in range(MOD_FIRST):
                mod_row(0)
            act.wait_ge(s_x, 16)
            act.wait_ge(s_mod, 1)
            for k in range(KT):
                modulate(k, k, mod[:, 8:16], mod[:, 0:8])
            split_high(0)
            split_high(1)

            def attention(l):
                act.wait_ge(a_v, l + 1)
                tr.sig(nc.scalar.copy(S(SA_, "vt", 640), psf[:, 0:640]), a_vt)

                def nk(u):
                    qb = u // 3
                    if qb == 0:
                        return CTX
                    n = qb - 1
                    return P * (2 + min(n + 1, 3) - max(n - 1, 0))

                def exps(u):
                    qb, t = divmod(u, ATT_T)
                    act.wait_ge(a_max, 15 * l + u + 1)
                    if u >= 2:
                        act.wait_ge(a_tr, 15 * l + u - 1)
                    for hh in range(2):
                        k = 6 * qb + 2 * t + hh
                        ins = A(S(SA_, "e", nk(u), 1024 * (u % 2) + 512 * hh), ps[:, 2 * (u % 2) + hh, 0:nk(u)],
                                ACT.Exp, bias=S(SA_, "nm", 1, k), scale=SCALE, accum_out=S(SA_, "sum", 1, k))
                        if hh == 0:
                            tr.own(ins)
                    tr.sig(ins, a_exp)

                exps(0)
                for u in range(15):
                    qb, t = divmod(u, ATT_T)
                    if u + 1 < 15:
                        exps(u + 1)
                    act.wait_ge(a_tr, 15 * l + u + 1)
                    if u >= 2:
                        act.wait_ge(a_pv, 15 * l + u - 1)
                    n = nk(u)
                    et = S(SA_, "et", 1024, 1024 * (u % 2)).rearrange("p (a n) -> p a n", a=2)[:, :, 0:n]
                    tr.sig(nc.scalar.copy(et, ps[:, 4:6, 0:n]), a_trsb)
                    if t == 2:
                        act.wait_ge(a_nms, 5 * l + qb + 1)
                        tr.sig(A(S(SA_, "es", 6, 6 * qb), S(SA_, "nms", 6, 6 * qb), ACT.Exp), a_es)
                    if t == 0 and qb:
                        out(l, qb - 1)
                out(l, 4)

            def out(l, qb):
                act.wait_ge(a_ot, 5 * l + qb + 1)
                tr.sig(nc.scalar.copy(mix[:, 0:ATT_T, P * qb:P * qb + P],
                                      bank(4, 384).rearrange("p (t n) -> p t n", t=3)), a_out)

            def ssd(l):
                mod_row(l + 1)
                for t in range(5):
                    act.wait_ge(c_conv, 5 * l + t + 1)
                    cv = S(SS_, "ea", 646, 646 * (t % 2))
                    tr.own(A(T(TX + t)[:, 0:CTX], cv[:, CTX0:CTX0 + CTX], ACT.Silu))
                    tr.sig(A(T(TX + t)[:, CTX:TOK], cv[:, LAT0:LAT0 + LAT], ACT.Silu), c_silu)
                    mod_row(l + 1)
                for t in range(3):
                    tr.own(A(T(TZ + t), T(TZ + t), ACT.Silu))
                    mod_row(l + 1)
                sm = SS_["small"]
                act.wait_ge(c_dtx, l + 1)
                tr.own(A(scr[:, sm + 120:sm + 180], scr[:, sm + 120:sm + 180], ACT.Exp))
                tr.sig(A(row[:, 18:30], row[:, 18:30], ACT.Exp), c_dte)
                act.wait_ge(c_cum, l + 1)
                tr.own(A(S(SS_, "small", 120, 240), bank(4, 120), ACT.Exp))
                tr.sig(A(S(SS_, "small", 60, 360), bank(4, 60, 120), ACT.Exp, scale=float(D)), c_ecum)

                def added(c):
                    act.wait_ge(c_st, 5 * l + c + 1)
                    tr.sig(nc.scalar.copy(S(SS_, "cs0", 384, 384 * c), bank(2 + c % 2, 384)), c_cs)

                for c in range(NCH):
                    act.wait_ge(c_tr, 5 * l + c + 1)
                    tr.sig(nc.scalar.copy(S(SS_, "xb", 512, 512 * c), bank(c % 2)), c_xb)
                    if c:
                        added(c - 1)
                added(NCH - 1)
                for c in range(NCH):
                    act.wait_ge(c_arg, 5 * l + c + 1)
                    if c:
                        act.wait_ge(c_g, 5 * l + c)
                    tr.sig(A(S(SS_, "ea", 768).rearrange("p (g n) -> p g n", g=2), ps[:, 2:4, 0:384],
                             ACT.Exp), c_ea)
                for t in range(3):
                    act.wait_ge(c_gate, 3 * l + t + 1)
                    if t >= 2:
                        act.wait_ge(c_var, 3 * l + t - 1)
                    tr.sig(A(t2[:, t % 2], mix[:, 3 + t], ACT.Square), c_sq)
                act.wait_ge(c_var, 3 * l + 3)
                tr.sig(A(rstd[:], pair(0), ACT.Sqrt, bias=C("eps", 1), scale=D / 384.0), c_std)

            def rwkv_features(l):
                act.wait_ge(r_mu, l + 1)
                for n, t in enumerate(SHIFT_ORDER):
                    if n >= 2:
                        act.wait_ge(r_shift, 8 * l + n - 1)
                    tr.sig(A(tail[:, 1284 + 642 * (n % 2):1926 + 642 * (n % 2)], proj[:, TR + t, 2:644], ACT.Copy,
                             scale=mus[:, t:t + 1]), r_scl)
                    if n == 3:
                        act.wait_ge(r_shift, 8 * l + 1)
                        tr.sig(A(T(TWA)[0:HD], T(TWA)[0:HD], ACT.Tanh), r_act)
                    if n == 5:
                        act.wait_ge(r_shift, 8 * l + 2)
                        tr.sig(A(T(TG), T(TG), ACT.Sigmoid), r_act)
                for hp in range(2):
                    act.wait_ge(r_kps, 2 * l + hp + 1)
                    tr.sig(A(t2[:, hp], pair(2 + hp), ACT.Sqrt, bias=C("eps", 1, 1)), r_kstd)
                for i, (d, hp) in enumerate(RW_UNITS):
                    for w, name in enumerate(("w0", "a0")):
                        act.wait_ge(r_wps, 8 * l + 2 * i + w + 1)
                        tr.sig(A(S(ST_, "sw" if w == 0 else "sa", TOK, TOK * i), pair(w), ACT.Sigmoid,
                                 bias=V(name, i)), r_sig)
                for hp in range(2):
                    act.wait_ge(r_gps, 2 * l + hp + 1)
                    tr.sig(nc.scalar.copy(mix[:, 6 + hp], pair(2 + hp)), r_g)
                for u, (hp, d) in enumerate((hp, d) for hp in range(2) for d in range(2)):
                    i = 2 * d + hp
                    act.wait_ge(r_cum, 4 * l + u + 1)
                    lcol, t1, tt2 = (x.rearrange("p (c n) -> p c n", c=NCH) for x in sums_of(u))
                    end = P - 1 if d == 0 else 0
                    tr.own(A(dec[:, 0, i], lcol[:, :, HD], ACT.Exp, scale=-DECAY))
                    tr.own(A(dec[:, 1, i], t1[:, :, end], ACT.Exp, scale=-DECAY))
                    tr.own(A(op_blocks(1, d, hp)[:, :, P:2 * P], t1, ACT.Exp, scale=-DECAY))
                    tr.own(A(op_blocks(1, d, hp)[:, :, 0:P], tt2, ACT.Exp, scale=-DECAY))
                    tr.sig(A(op_blocks(0, d, hp)[:, :, P:2 * P], t1, ACT.Exp, scale=DECAY), r_exp)

            def rwkv_scan(l):
                act.wait_ge(r_v, l + 1)
                tr.sig(nc.scalar.copy(VTOK.rearrange("p c n -> p (c n)"), psf[:, 0:1280]), r_vt)
                for i in range(NCH + 1):
                    if i:
                        act.wait_ge(r_tkps, 5 * l + i)
                        tr.sig(nc.scalar.copy(S(SR_, "tok", 1024), psf[:, 0:1024]), r_tk)
                        act.wait_ge(r_rps, 5 * l + i)
                        tr.sig(nc.scalar.copy(xs(0, 512, 0).rearrange("p (a n) -> p a n", a=2), ps[:, 2:4, 0:256]),
                               r_rsb)
                    for j in range(1, 7 if i < NCH else 1):
                        for d in range(2):
                            act.wait_ge(r_xps, x_count(l, i, d, j))
                            tr.sig(nc.scalar.copy(S(SR_, "x", 512, 512 * d), bank(4 + 2 * d)), r_xsb)
                            if j > 1:
                                act.wait_ge(r_tps, turn_count(l, i, d, j - 1))
                                tr.sig(nc.scalar.copy(mt_of(i, d), bank(5 + 2 * d)), r_tsb)
                sq = S(SR_, "gb", 1280)
                act.wait_ge(r_osq, 2 * l + 1)
                tr.sig(A(sq, OTOK.rearrange("p c n -> p (c n)"), ACT.Square), r_ovar)
                act.wait_ge(r_osq, 2 * l + 2)
                sm = S(SR_, "small", 20, 20)
                tr.sig(A(sm, sm, ACT.Sqrt, bias=C("eps", 1, 2), scale=1.0 / HD), r_ostd)

            for l in range(DEPTH):
                base = N_DENSE * l
                q0 = PER_DENSE * l
                for t in range(N_IN):
                    evict(base + t, T(t))
                    if t % 2 == 1 and t // 2 + 2 < IN_SLOTS:
                        split_high(q0 + t // 2 + 2)
                n = base + N_IN
                act.wait_ge(s_dense, done(n))
                tr.sig(nc.scalar.copy(dtr[:].rearrange("p c n -> p (c n)"), psf[:, 1024:1084]), s_free[1])
                bar()
                attention(l)
                bar()
                act.wait_ge(s_small, 16 * N_SMALL * (l + 1))
                ssd(l)
                bar()
                rwkv_features(l)
                bar()
                rwkv_scan(l)
                bar()
                act.wait_ge(s_mod, 2 * l + 2)
                for k in range(KT):
                    tr.sig(nc.scalar.copy(xh[:, k], mix[:, k]), s_hhigh)
                act.wait_ge(s_h, (3 * l + 2) * KT)
                q0 += IN_SLOTS
                split_high(q0)
                split_high(q0 + 1)
                for k in range(KT):
                    gated(base + D_OUT + k, k, 16, 2 * l)
                    if k % 2 == 1 and k < KT - 1:
                        split_high(q0 + 2 + k // 2)
                norm(2 * l, True, q0 + 1 + KT // 2)
                q0 += OUT_SLOTS
                for i in range(FFN_T):
                    n = base + D_UP + 2 * i
                    act.wait_ge(s_dense, done(n))
                    tr.sig(A(T(i), pair(0), ACT.Silu), s_free[0])
                    split_high(q0 + 2 + i)
                q0 += UP_SLOTS
                for i in range(DOWN_PAIRS):
                    for k in range(FFN_T):
                        e = (DOWN_PAIRS * l + i) * FFN_T + k
                        if i == 0 and k < KT:
                            act.wait_ge(s_dense, done(base + D_DOWN - 1))
                        else:
                            act.wait_ge(s_hid_used, e - KT + 1)
                        if i == 0:
                            act.wait_ge(s_free[2], FFN_T * l + k + 1)
                        tr.sig(nc.scalar.copy(xh[:, hid_at(i, k)], T(k)), s_hid_high)
                        if i and k == KT:
                            for j in range(2):
                                gated(base + D_DOWN + 2 * i - 2 + j, 2 * i - 2 + j, 40, 2 * l + 1,
                                      down_pair(i - 1) + j)
                        if k in split_after and (i or split_after[k] > 1):
                            split_high(q0 + DOWN_PARTS * i + split_after[k])
                q0 += DOWN_PAIRS * DOWN_PARTS
                act.wait_ge(s_hid_used, DOWN_PAIRS * FFN_T * (l + 1))
                for j in range(2):
                    gated(base + D_DOWN + 6 + j, 6 + j, 40, 2 * l + 1, down_pair(DOWN_PAIRS - 1) + j)
                if l + 1 < DEPTH:
                    act.wait_ge(s_mod, 2 * (l + 1) + 1)
                norm(2 * l + 1, l + 1 < DEPTH, q0 + 1)
                bar()

        @block.vector
        def _(dve):
            tr = Track(dve, s_dve)
            nbar = [0]
            v = nc.vector

            def bar():
                barrier(dve, tr, nbar[0])
                nbar[0] += 1

            def own(ins):
                tr.own(ins)
                tr.hold()

            def mod_row(l, i):
                dve.wait_ge(s_modps, MOD_SLOTS * l + i + 1)
                tr.sig(v.tensor_copy(t2[0:2, i % 2, 0:256], ps[0:2, 7, 0:256]), s_modrow[0])

            def modulation(l, a, b):
                first = a == 0
                dve.wait_ge(s_modt, MOD_SLOTS * l + (MOD_FIRST if first else MOD_SLOTS))
                own(v.tensor_tensor(mod[:, a:b, :], bank(7, 2 * (b - a), MOD_AT + 2 * a).rearrange("p (t c) -> p t c", c=2),
                                    bm[:, l, a:b].unsqueeze(2).broadcast_to([P, b - a, 2]), ALU.add))
                s = (8, 16) if first else (32, 40)
                tr.sig(v.tensor_scalar(mod[:, s[0]:s[1], :], mod[:, s[0]:s[1], :], 1.0, None, ALU.add), s_mod)

            def split_low(q):
                if q >= len(split_slots):
                    return
                n = split_slots[q][0]
                dve.wait_ge(s_whigh, q + 1)
                tr.sig(v.tensor_tensor(wl[:, q % 2], ring[:, n % RING], wh[:, q % 2], ALU.subtract), s_wlow)

            def input_low(k, e, src):
                dve.wait_ge(s_hhigh, e + 1)
                tr.sig(v.tensor_tensor(xl[:, k], src, xh[:, k], ALU.subtract), s_h)

            def residual(group, first, k):
                dve.wait_ge(*freed(first + k))
                if group:
                    dve.wait_ge(s_ln, KT * (group - 1) + k + 1)
                tr.sig(v.scalar_tensor_tensor(xt[:, k], xt[:, k], ALPHA, t2[:, k % 2], ALU.mult, ALU.add), s_res)
                if k:
                    tr.hold()
                    ins = v.tensor_tensor(rstd[:], xt[:, 0] if k == 1 else rstd[:], xt[:, k], ALU.add)
                    if k == KT - 1:
                        tr.sig(ins, s_sum)
                    else:
                        tr.own(ins)

            def norm(group, w, b, h_event, q):
                if h_event is not None:
                    sh, sc = (24, 32) if group % 2 == 0 else (0, 8)
                    for j, name in enumerate((w, b)):
                        tr.own(v.tensor_tensor(both[:, j], mod[:, sc:sc + KT],
                                               V(name, 0, KT).unsqueeze(2).broadcast_to([P, KT, 2]), ALU.mult))
                    tr.hold()
                    tr.own(v.tensor_tensor(both[:, 1], both[:, 1], mod[:, sh:sh + KT], ALU.add))
                dve.wait_ge(s_mu, group + 1)
                for k in range(KT):
                    tr.sig(v.tensor_tensor(xt[:, k], xt[:, k], pair(2), ALU.subtract), s_cen)
                split_low(q)
                dve.wait_ge(s_std, group + 1)
                own(v.reciprocal(rstd[:], rstd[:]))
                for k in range(KT):
                    tr.sig(v.tensor_tensor(xt[:, k], xt[:, k], rstd[:], ALU.mult), s_hat)
                    if h_event is not None and k:
                        input_low(k - 1, h_event + k - 1, rawh[:, (k - 1) % 2])
                if h_event is not None:
                    input_low(KT - 1, h_event + KT - 1, rawh[:, (KT - 1) % 2])

            def attention(l):
                for t in range(4):
                    x = proj[:, TQ + t, CTX:TOK]
                    rot = S(SA_, "rot", LAT, LAT * (t % 2))
                    dve.wait_ge(a_rot, 4 * l + t + 1)
                    tr.own(v.tensor_tensor(rot, bank(2 + t % 2), C("sin", LAT), ALU.mult))
                    own(v.tensor_tensor(x, x, C("cos", LAT), ALU.mult))
                    tr.sig(v.tensor_tensor(x, x, rot, ALU.add), a_rope)
                own(v.tensor_scalar(row[:, 30:36], row[:, 0:6], -1.0, None, ALU.mult))

                def maxima(u):
                    qb, t = divmod(u, ATT_T)
                    dve.wait_ge(a_score, 15 * l + u + 1)
                    b = 2 * (u % 2)
                    nk = CTX
                    if qb:
                        n = qb - 1
                        lo_, hi = max(n - 1, 0), min(n + 1, 3)
                        nk = P * (2 + hi - lo_)
                        for there, at, name in ((n > 0, P, "bprev"), (n < 3, nk - P, "bnext")):
                            if there:
                                o = ps[:, b:b + 2, at:at + P]
                                own(v.tensor_tensor(o, o, C(name).unsqueeze(1).broadcast_to([P, 2, P]), ALU.add))
                    k = 6 * qb + 2 * t
                    own(v.tensor_reduce(S(SA_, "mx", 2, k), ps[:, b:b + 2, 0:nk], AX.X, ALU.max))
                    tr.sig(v.scalar_tensor_tensor(S(SA_, "nm", 2, k), S(SA_, "mx", 2, k), -SCALE,
                                                  row[:, 30 + 2 * t:32 + 2 * t], ALU.mult, ALU.min), a_max)
                    if t == 2:
                        k = 6 * qb
                        tr.hold()
                        tr.sig(v.tensor_tensor(S(SA_, "nms", 6, k), S(SA_, "nm", 6, k), row[:, 0:6], ALU.add), a_nms)

                def normalise(qb):
                    k = 6 * qb
                    dve.wait_ge(a_es, 5 * l + qb + 1)
                    own(v.tensor_tensor(S(SA_, "den", 6, k), S(SA_, "sum", 6, k), S(SA_, "es", 6, k), ALU.add))
                    own(v.reciprocal(S(SA_, "den", 6, k), S(SA_, "den", 6, k)))
                    dve.wait_ge(a_pv, 15 * l + 3 * qb + 3)
                    if qb:
                        dve.wait_ge(a_ot, 5 * l + qb)
                    tr.sig(v.tensor_tensor(S(SA_, "osb", 384).rearrange("p (h n) -> p h n", h=6),
                                           bank(6, 384).rearrange("p (h n) -> p h n", h=6),
                                           S(SA_, "den", 6, k).unsqueeze(2).broadcast_to([P, 6, HD]), ALU.mult),
                           a_on)

                maxima(0)
                for u in range(15):
                    if u + 1 < 15:
                        maxima(u + 1)
                    mod_row(l, MOD_FIRST + u)
                    if u % 3 == 2:
                        normalise(u // 3)
                mod_row(l, MOD_SLOTS - 1)

            def ssd(l):
                for t in range(5):
                    cv = S(SS_, "ea", 642, 646 * (t % 2) + 2)
                    if t >= 2:
                        dve.wait_ge(c_silu, 5 * l + t - 1)
                    x = proj[:, TX + t]
                    own(v.tensor_scalar(cv, x[:, 0:642], V("convw", t), V("convb", t), ALU.mult, ALU.add))
                    for k in range(1, CONV):
                        ins = v.scalar_tensor_tensor(cv, x[:, k:k + 642], V("convw", 5 * k + t), cv,
                                                     ALU.mult, ALU.add)
                        if k < CONV - 1:
                            own(ins)
                    tr.sig(ins, c_conv)
                sm = SS_["small"]

                def X(a, n=60):
                    return scr[:, sm + a:sm + a + n]

                x, e, dt_, z, q = X(60), X(120), X(180), X(420), X(480)
                x5 = x.rearrange("p (c n) -> p c n", c=NCH)
                own(v.tensor_tensor(x5, dtr[:], row[:, 6:18].unsqueeze(1).broadcast_to([P, NCH, 12]), ALU.add))
                tr.sig(v.scalar_tensor_tensor(e, x, -1.0, x, ALU.mult, ALU.min), c_dtx)
                own(v.tensor_scalar(x, x, 0.0, None, ALU.max))
                dve.wait_ge(c_dte, l + 1)
                own(v.tensor_scalar(z, e, 2.0, None, ALU.add))
                own(v.reciprocal(z, z))
                own(v.tensor_tensor(e, e, z, ALU.mult))
                own(v.tensor_tensor(z, e, e, ALU.mult))
                own(v.tensor_scalar(q, z, 1.0 / 17, None, ALU.mult))
                for c in (15, 13, 11, 9, 7, 5, 3):
                    own(v.scalar_tensor_tensor(q, q, 1.0 / c, z, ALU.add, ALU.mult))
                own(v.scalar_tensor_tensor(q, q, 1.0, e, ALU.add, ALU.mult))
                own(v.scalar_tensor_tensor(dt_, q, 2.0, x, ALU.mult, ALU.add))
                d5 = dt_.rearrange("p (c n) -> p c n", c=NCH)
                for d in range(2):
                    ins = v.scalar_tensor_tensor(scr[:, sm + 30 * d:sm + 30 * d + 30].rearrange("p (c n) -> p c n", c=NCH),
                                                 d5[:, :, 6 * d:6 * d + 6], -1.0,
                                                 row[:, 18 + 6 * d:24 + 6 * d].unsqueeze(1).broadcast_to([P, NCH, 6]),
                                                 ALU.mult, ALU.mult)
                    if d == 0:
                        tr.own(ins)
                tr.sig(ins, c_a)
                dve.wait_ge(c_ecum, l + 1)
                for d in range(2):
                    ins = v.tensor_tensor(X(540 + 30 * d, 30).rearrange("p (c n) -> p c n", c=NCH),
                                          d5[:, :, 6 * d:6 * d + 6],
                                          X(300 + 30 * d, 30).rearrange("p (c n) -> p c n", c=NCH), ALU.mult)
                    if d == 0:
                        tr.own(ins)
                tr.sig(ins, c_dtend)
                for g in range(2):
                    own(v.tensor_copy(scr[HD * g:HD * g + HD, sm + 600:sm + 630].rearrange("p (a n) -> p a n", n=3),
                                      scr[HD * g:HD * g + HD, sm + 360:sm + 420]
                                      .rearrange("p (a n) -> p a n", n=6)[:, :, 3 * g:3 * g + 3]))
                dve.wait_ge(c_cs, 5 * l + 5)
                dve.wait_ge(s_init, 32 * (l + 1))
                for step in range(3):
                    for d in range(2):
                        c = 1 + step if d == 0 else 4 - step
                        nxt = c + 1 if d == 0 else c - 1
                        old = S(SS_, "sp", 192, 960 * d + 192 * c).rearrange("p (h n) -> p h n", h=3)
                        new = S(SS_, "sp", 192, 960 * d + 192 * nxt)
                        own(v.tensor_tensor(new.rearrange("p (h n) -> p h n", h=3), old,
                                            X(600 + 15 * d + 3 * c, 3).unsqueeze(2).broadcast_to([P, 3, HD]),
                                            ALU.mult))
                        own(v.tensor_tensor(new, new, S(SS_, "cs0", 192, 384 * c + 192 * d), ALU.add))
                tr.sig(v.tensor_copy(X(630, 1), X(600, 1)), c_sp)

                cbm = S(SS_, "cbm", 512).rearrange("p (g d n) -> p g d n", g=2, d=2)

                def masked(c):
                    dve.wait_ge(c_cb, 5 * l + c + 1)
                    for d, name in enumerate(("incf", "incb")):
                        ins = v.tensor_tensor(cbm[:, :, d], ps[:, 0:2, 0:P],
                                              C(name).unsqueeze(1).broadcast_to([P, 2, P]), ALU.mult)
                        if d == 0:
                            tr.own(ins)
                    tr.sig(ins, c_cbm)

                def finish(c):
                    dve.wait_ge(c_yt, 5 * l + c + 1)
                    for t in range(3):
                        ins = v.scalar_tensor_tensor(mix[:, 3 + t, P * c:P * c + P], ch(TX + t, c), V("d", t),
                                                     bank(7, P, P * t), ALU.mult, ALU.add)
                        if t < 2:
                            tr.own(ins)
                    tr.sig(ins, c_yf)

                masked(0)
                for c in range(NCH):
                    dve.wait_ge(c_cbm, 5 * l + c + 1)
                    dve.wait_ge(c_ea, 5 * l + c + 1)
                    if c:
                        dve.wait_ge(c_y, 5 * l + c)
                    for d in range(2):
                        for g in range(2):
                            ins = v.tensor_tensor(
                                S(SS_, "g", 384, 768 * d + 384 * g).rearrange("p (h n) -> p h n", h=3),
                                S(SS_, "ea", 384, 384 * g).rearrange("p (h n) -> p h n", h=3),
                                cbm[:, g, d].unsqueeze(1).broadcast_to([P, 3, P]), ALU.mult)
                            if d == 0 or g == 0:
                                tr.own(ins)
                    tr.sig(ins, c_g)
                    if c + 1 < NCH:
                        tr.hold()
                        masked(c + 1)
                    y = S(SS_, "y", 384)
                    if c:
                        finish(c - 1)
                        dve.wait_ge(c_off, 4 * l + c)
                        for d in range(2):
                            t1 = S(SS_, "t1", 384, 384 * d).rearrange("p (g h n) -> p g h n", g=2, h=3)
                            ec = X(240 + 30 * d + 6 * c, 6).rearrange("p (g h) -> p g h", g=2)
                            for g in range(2):
                                tr.own(v.tensor_tensor(t1[:, g], bank(5 + g, 192, 192 * d)
                                                       .rearrange("p (h n) -> p h n", h=3),
                                                       ec[:, g].unsqueeze(2).broadcast_to([P, 3, HD]), ALU.mult))
                        tr.hold()
                        own(v.tensor_tensor(y, S(SS_, "t1", 384), S(SS_, "t1", 384, 384), ALU.add))
                        dve.wait_ge(c_y, 5 * l + c + 1)
                        tr.sig(v.tensor_tensor(y, y, bank(4, 384), ALU.add), c_ytok)
                    else:
                        dve.wait_ge(c_y, 5 * l + c + 1)
                        tr.sig(v.tensor_copy(y, bank(4, 384)), c_ytok)
                finish(NCH - 1)
                tr.hold()
                for t in range(3):
                    tr.sig(v.tensor_tensor(mix[:, 3 + t], mix[:, 3 + t], T(TZ + t), ALU.mult), c_gate)
                dve.wait_ge(c_std, l + 1)
                own(v.reciprocal(rstd[:], rstd[:]))
                for t in range(3):
                    own(v.scalar_tensor_tensor(mix[:, 3 + t], mix[:, 3 + t], V("normw", t), rstd[:],
                                               ALU.mult, ALU.mult))

            def rwkv_features(l):
                tr.own(v.tensor_scalar(mus[:, 8:16], V("mu", 0, 8), 0.5, None, ALU.mult))
                tr.own(v.tensor_scalar(mus[:, 16:18], V("ka", 0, 2), -1.0, 1.0, ALU.mult, ALU.add))
                tr.sig(v.tensor_scalar(mus[:, 0:8], V("mu", 0, 8), -1.0, 1.0, ALU.mult, ALU.add), r_mu)
                tr.hold()
                kk = S(ST_, "kk", 1280).rearrange("p (a n) -> p a n", a=2)
                for m, t in enumerate(SHIFT_ORDER):
                    dve.wait_ge(r_sum, 8 * l + m + 1)
                    dve.wait_ge(r_scl, 8 * l + m + 1)
                    a = 642 * (m % 2)
                    for i, (o, n, f) in enumerate(((0, CTX, 0), (CTX, LAT, LAT0 - CTX0))):
                        ins = v.scalar_tensor_tensor(T(TR + t)[:, o:o + n], tail[:, a + f:a + f + n],
                                                     mus[:, 8 + t:9 + t], tail[:, 1284 + a + f:1284 + a + f + n],
                                                     ALU.mult, ALU.add)
                        if i == 0:
                            tr.own(ins)
                    tr.sig(ins, r_shift)
                    if m == 3:
                        tr.hold()
                        for hp in range(2):
                            own(v.tensor_scalar(kk[:, hp], T(TKK + hp), V("kk", hp), None, ALU.mult))
                            tr.sig(v.tensor_tensor(t2[:, hp], kk[:, hp], kk[:, hp], ALU.mult), r_ksq)
                tr.hold()
                for hp in range(2):
                    dve.wait_ge(r_kstd, 2 * l + hp + 1)
                    own(v.reciprocal(t2[:, hp], t2[:, hp]))
                    tr.sig(v.tensor_tensor(kk[:, hp], kk[:, hp], t2[:, hp], ALU.mult), r_kk)
                units = [(hp, d) for hp in range(2) for d in range(2)]

                def sums(u):
                    hp, d = units[u]
                    i = 2 * d + hp
                    dve.wait_ge(r_sig, 8 * l + 2 * i + 1)
                    L, t1, tt2 = sums_of(u)
                    sw = S(ST_, "sw", TOK, TOK * i)
                    if d == 0:
                        own(v.tensor_tensor_scan(L, C("reset", TOK), sw, 0.0, ALU.mult, ALU.add))
                    else:
                        own(v.tensor_tensor_scan(L[:, ::-1], C("reset", TOK), sw[:, ::-1], 0.0, ALU.mult, ALU.add))
                    L5, t15 = (x.rearrange("p (c n) -> p c n", c=NCH) for x in (L, t1))
                    own(v.tensor_tensor(t15, L5, L5[:, :, HD:HD + 1].broadcast_to([P, NCH, P]), ALU.subtract))
                    tr.sig(v.tensor_tensor(tt2, t1, sw, ALU.subtract), r_cum)

                sums(0)
                for u, (hp, d) in enumerate(units):
                    i = 2 * d + hp
                    if u + 1 < 4:
                        sums(u + 1)
                    dve.wait_ge(r_exp, 4 * l + u + 1)
                    dve.wait_ge(r_kd, 8 * l + 2 * u + 2)
                    al, rho = op_blocks(1, d, hp)[:, :, 0:P], op_blocks(1, d, hp)[:, :, P:2 * P]
                    be, ka = op_blocks(0, d, hp)[:, :, 0:P], op_blocks(0, d, hp)[:, :, P:2 * P]

                    def c5(x):
                        return x.rearrange("p (c n) -> p c n", c=NCH)

                    tr.own(v.tensor_tensor(rho, rho, c5(T(TR + hp)), ALU.mult))
                    tr.own(v.tensor_tensor(al, al, c5(kk[:, hp]), ALU.mult))
                    own(v.tensor_tensor(be, ka, c5(S(ST_, "sa", TOK, TOK * i)), ALU.mult))
                    own(v.tensor_tensor(ka, ka, c5(S(ST_, "kd", TOK, TOK * d)), ALU.mult))
                    if d == 1:
                        kd0, kd1 = S(ST_, "kd", TOK), S(ST_, "kd", TOK, TOK)
                        dve.wait_ge(r_wps, 8 * l + 8)
                        dve.wait_ge(r_gps, 2 * l + 2)
                        own(v.tensor_tensor(kd0, kd0, kd1, ALU.add))
                        tr.sig(v.scalar_tensor_tensor(T(TWA + hp), kd0, V("rk", hp), T(TR + hp),
                                                      ALU.mult, ALU.mult), r_bon)
                for hp in range(2):
                    dve.wait_ge(r_bps, 2 * l + hp + 1)
                    tr.sig(v.tensor_tensor(T(TWA + hp), pair(2 + hp), T(TVV + hp), ALU.mult), r_bv)

            def rwkv_scan(l):
                own(v.memset(OTOK, 0.0))
                sx, s0x = S(SR_, "s", 256), S(SR_, "s0", 256)

                def masked(i, d):
                    n = 10 * l + 2 * i + d
                    for w, of in enumerate((gb_of, gk_of)):
                        dve.wait_ge(r_gmat, 2 * n + w + 1)
                        tr.sig(v.tensor_tensor(
                            of(i, d).rearrange("p (q n) -> p q n", q=4),
                            ps[:, 2 * w:2 * w + 2, :].rearrange("p b (h n) -> p (b h) n", h=2),
                            C("gmf" if d == 0 else "gmb", 256).unsqueeze(1).broadcast_to([P, 4, 256]),
                            ALU.mult), r_gsb)

                def level(i, j):
                    for d in range(2):
                        dve.wait_ge(r_mps, x_count(l, i, d, j))
                        m = S(SR_, "m", 512, 512 * d) if j < 6 else mt_of(i, d)
                        tr.sig(v.tensor_tensor(m, m, bank(5 + 2 * d), ALU.subtract), r_msb)

                def scaled_state(c):
                    for d in range(2):
                        src = (init_rw[:] if c == 1 else sx)
                        ins = v.tensor_tensor(s0x[:, 128 * d:128 * d + 128].rearrange("p (h n) -> p h n", h=2),
                                              src[:, 128 * d:128 * d + 128].rearrange("p (h n) -> p h n", h=2),
                                              dec[:, 0, 2 * d:2 * d + 2, token_chunk(c, d)].unsqueeze(2)
                                              .broadcast_to([P, 2, HD]), ALU.mult)
                        if d == 0:
                            tr.own(ins)
                    tr.sig(ins, r_s0)

                def new_state(c):
                    dve.wait_ge(r_sps, 5 * l + c + 1)
                    if c:
                        own(v.tensor_tensor(sx, s0x, bank(1, 256), ALU.add))
                    else:
                        own(v.tensor_copy(sx, bank(1, 256)))
                    for d in range(2):
                        o = (fin_rw[:] if c == 0 else sx)[:, 128 * d:128 * d + 128]
                        ins = v.tensor_tensor(o.rearrange("p (h n) -> p h n", h=2),
                                              sx[:, 128 * d:128 * d + 128].rearrange("p (h n) -> p h n", h=2),
                                              dec[:, 1, 2 * d:2 * d + 2, token_chunk(c, d)].unsqueeze(2)
                                              .broadcast_to([P, 2, HD]), ALU.mult)
                        if d == 0:
                            tr.own(ins)
                    tr.sig(ins, r_st)

                def add_out(c):
                    dve.wait_ge(r_ops2, 5 * l + c + 1)
                    for d in range(2):
                        o = OTOK[:, token_chunk(c, d)].rearrange("p (h a n) -> p a h n", h=2, a=2)
                        for par in range(2):
                            ins = v.tensor_tensor(o[:, par], o[:, par],
                                                  bank(2 + par, P, P * d).rearrange("p (h n) -> p h n", h=2),
                                                  ALU.add)
                            if d == 0 or par == 0:
                                own(ins)
                    tr.sig(ins, r_osb)

                masked(0, 0)
                masked(0, 1)
                for i in range(NCH + 1):
                    inv, chain, ahead = i < NCH, i > 0, i + 1 < NCH
                    if inv:
                        for d in range(2):
                            dve.wait_ge(r_m0ps, 10 * l + 2 * i + d + 1)
                            tr.sig(v.tensor_copy(S(SR_, "m", 512, 512 * d), bank(5 + 2 * d)), r_m0)
                    if chain:
                        dve.wait_ge(r_ups, 5 * l + i)
                        tr.sig(v.tensor_scalar(xs(1, 512, 0), bank(0), -1.0, None, ALU.mult), r_nu)
                    if inv:
                        level(i, 1)
                    if chain:
                        new_state(i - 1)
                    if inv:
                        level(i, 2)
                        level(i, 3)
                        level(i, 4)
                    if chain:
                        add_out(i - 1)
                    if chain and inv:
                        scaled_state(i)
                    if ahead:
                        masked(i + 1, 0)
                    if inv:
                        level(i, 5)
                    if ahead:
                        masked(i + 1, 1)
                    if inv:
                        level(i, 6)
                tr.hold()
                o20 = OTOK.rearrange("p c (h n) -> p (c h) n", h=4)
                mu, var = S(SR_, "small", 20), S(SR_, "small", 20, 20)
                own(v.tensor_reduce(mu, o20, AX.X, ALU.add))
                own(v.tensor_scalar(mu, mu, 1.0 / HD, None, ALU.mult))
                tr.sig(v.tensor_tensor(o20, o20, mu.unsqueeze(2).broadcast_to([P, 20, HD]), ALU.subtract), r_osq)
                dve.wait_ge(r_ovar, l + 1)
                tr.sig(v.tensor_reduce(var, S(SR_, "gb", 1280).rearrange("p (a n) -> p a n", a=20), AX.X, ALU.add),
                       r_osq)
                dve.wait_ge(r_ostd, l + 1)
                own(v.reciprocal(var, var))
                tr.sig(v.tensor_tensor(o20, o20, var.unsqueeze(2).broadcast_to([P, 20, HD]), ALU.mult), r_on)
                dve.wait_ge(r_otps, l + 1)
                for hp in range(2):
                    y = S(SR_, "gb", TOK, TOK * hp)
                    own(v.tensor_scalar(y, chunks(hp), V("gnw", hp), V("gnb", hp), ALU.mult, ALU.add))
                    own(v.tensor_tensor(y, y, T(TWA + hp), ALU.add))
                    own(v.tensor_tensor(mix[:, 6 + hp], mix[:, 6 + hp], y, ALU.mult))

            dve.wait_ge(s_const, 48)
            modulation(0, 0, 16)
            for k in range(KT):
                input_low(k, k, rawh[:, k % 2])
            split_low(0)
            split_low(1)
            for l in range(DEPTH):
                q0 = PER_DENSE * l
                for i in range(2, IN_SLOTS):
                    split_low(q0 + i)
                bar()
                dve.wait_ge(s_small, 16 * N_SMALL * (l + 1))
                attention(l)
                bar()
                modulation(l, 2 * MOD_FIRST, MOD_T)
                ssd(l)
                bar()
                if l + 1 < DEPTH:
                    modulation(l + 1, 0, 2 * MOD_FIRST)
                rwkv_features(l)
                bar()
                rwkv_scan(l)
                bar()
                for k in range(KT):
                    input_low(k, (3 * l + 1) * KT + k, mix[:, k])
                q0 += IN_SLOTS
                split_low(q0)
                split_low(q0 + 1)
                for k in range(KT):
                    residual(2 * l, N_DENSE * l + D_OUT, k)
                    if k % 2 == 1 and k < KT - 1:
                        split_low(q0 + 2 + k // 2)
                norm(2 * l, "ln1w", "ln1b", (3 * l + 2) * KT, q0 + 1 + KT // 2)
                q0 += OUT_SLOTS
                for i in range(FFN_T):
                    n = N_DENSE * l + D_UP + 2 * i
                    dve.wait_ge(s_dense, done(n + 1))
                    dve.wait_ge(s_free[0], n // 2 + 1)
                    tr.sig(v.tensor_tensor(T(i), T(i), pair(1), ALU.mult), s_free[2])
                    split_low(q0 + 2 + i)
                q0 += UP_SLOTS
                for i in range(DOWN_PAIRS):
                    for k in range(FFN_T):
                        e = (DOWN_PAIRS * l + i) * FFN_T + k
                        dve.wait_ge(s_hid_high, e + 1)
                        tr.sig(v.tensor_tensor(xl[:, hid_at(i, k)], T(k), xh[:, hid_at(i, k)], ALU.subtract),
                               s_hid)
                        if i and k == KT:
                            residual(2 * l + 1, N_DENSE * l + D_DOWN, 2 * i - 2)
                            residual(2 * l + 1, N_DENSE * l + D_DOWN, 2 * i - 1)
                        if k in split_after and (i or split_after[k] > 1):
                            split_low(q0 + DOWN_PARTS * i + split_after[k])
                q0 += DOWN_PAIRS * DOWN_PARTS
                residual(2 * l + 1, N_DENSE * l + D_DOWN, 6)
                residual(2 * l + 1, N_DENSE * l + D_DOWN, 7)
                norm(2 * l + 1, "ln2w", "ln2b", (3 * l + 3) * KT if l + 1 < DEPTH else None, q0 + 1)
                bar()

        @block.gpsimd
        def _(pool):
            tr = Track(pool, s_pool)
            nbar = [0]
            g_ = nc.gpsimd

            def bar():
                barrier(pool, tr, nbar[0])
                nbar[0] += 1

            def own(ins):
                tr.own(ins)
                tr.hold()

            def small_loads(l):
                for dst, src in ((vc[:], vecs), (row[:, 0:NROW], rows), (kc[:], kctx), (vcx[:], vctx), (lo[:], lora),
                                 (gu[:], gup)):
                    pool.dma_start(dst, src[l]).then_inc(s_small, 16)
                pool.dma_start(init_rw[:], rwkv0[l]).then_inc(s_small, 16)

            def pads():
                for a in (0, CTX0 + CTX, LAT0 + LAT):
                    own(g_.memset(proj[:, TX:N_IN, a:a + 2], 0.0))

            def ssd(l):
                sm = SS_["small"]
                pool.dma_start(S(SS_, "sp", 192, 192 * 1), ssd0[l, :, 0]).then_inc(s_init, 16)
                pool.dma_start(S(SS_, "sp", 192, 960 + 192 * 4), ssd0[l, :, 1]).then_inc(s_init, 16)
                pool.wait_ge(c_dtend, l + 1)
                for c in range(NCH):
                    pool.wait_ge(c_xb, 5 * l + c + 1)
                    if c:
                        pool.wait_ge(c_st, 5 * l + c)
                    scaled_x(l, c, 540, c_xe)

                def decays(c):
                    if c == 0:
                        pool.wait_ge(c_sp, l + 1)
                    else:
                        pool.wait_ge(c_arg, 5 * l + c)
                    for d, name in enumerate(("incf", "incb")):
                        ins = g_.tensor_tensor(S(SS_, "cs", 768, 768 * d).rearrange("p (h n) -> p h n", h=6),
                                               C(name).unsqueeze(1).broadcast_to([P, 6, P]),
                                               scr[:, sm + 30 * d + 6 * c:sm + 30 * d + 6 * c + 6]
                                               .unsqueeze(2).broadcast_to([P, 6, P]), ALU.mult)
                        if d == 0:
                            tr.own(ins)
                    tr.sig(ins, c_rh)

                decays(0)
                for c in range(NCH):
                    if c + 1 < NCH:
                        decays(c + 1)
                    if c == 0:
                        pool.wait_ge(c_st, 5 * l + 5)
                    else:
                        pool.wait_ge(c_y, 5 * l + c)
                    scaled_x(l, c, None, c_xd)
                pool.wait_ge(c_cs, 5 * l + 1)
                pool.dma_start(ssd_out[l], S(SS_, "cs0", 384)).then_inc(s_out, 16)

            def scaled_x(l, c, at, sig):
                sm = SS_["small"]
                for d in range(2):
                    a = sm + (180 + 12 * c + 6 * d if at is None else at + 30 * d + 6 * c)
                    ins = g_.tensor_tensor(S(SS_, "xd", 384, 384 * d).rearrange("p (h n) -> p h n", h=6),
                                           S(SS_, "xb", 384, 512 * c).rearrange("p (h n) -> p h n", h=6),
                                           scr[:, a:a + 6].unsqueeze(2).broadcast_to([P, 6, HD]), ALU.mult)
                    if d == 0:
                        tr.own(ins)
                tr.sig(ins, sig)

            def rwkv_features(l):
                for n, t in enumerate(SHIFT_ORDER):
                    if n >= 2:
                        pool.wait_ge(r_shift, 8 * l + n - 1)
                    tr.sig(g_.tensor_tensor(tail[:, 642 * (n % 2):642 * (n % 2) + 642], proj[:, TR + t, 1:643],
                                            proj[:, TR + t, 3:645], ALU.add), r_sum)
                pool.wait_ge(r_kk, 2 * l + 2)
                for u, (hp, d) in enumerate((hp, d) for hp in range(2) for d in range(2)):
                    i = 2 * d + hp
                    kd, sa = S(ST_, "kd", TOK, TOK * d), S(ST_, "sa", TOK, TOK * i)
                    if u == 0:
                        pool.wait_ge(r_sig, 8 * l + 8)
                    if u >= 2:
                        pool.wait_ge(r_bon, 2 * l + 1)
                    own(g_.tensor_scalar(kd, sa, V("ka", hp), mus[:, 16 + hp:17 + hp], ALU.mult, ALU.add))
                    tr.sig(g_.tensor_tensor(kd, kd, T(TKK + hp), ALU.mult), r_kd)
                    tr.hold()
                    tr.sig(g_.tensor_tensor(sa, sa, S(ST_, "kk", TOK, TOK * hp), ALU.mult), r_kd)

            def rwkv_scan(l):
                for i in range(NCH):
                    for j in range(7):
                        for d in range(2):
                            if j == 0:
                                pool.wait_ge(r_gsb, 4 * (NCH * l + i) + 2 * d + 1)
                            if j == 0 and i:
                                pool.wait_ge(r_xps, x_count(l, i - 1, d, 6))
                            if j >= 2:
                                pool.wait_ge(r_xps, x_count(l, i, d, j - 1))
                            lv = lv_(d).rearrange("p (q n) -> p q n", q=4)
                            gb = gb_of(i, d).rearrange("p (q n) -> p q n", q=4)[:, :, 0:P]
                            tr.sig(g_.tensor_tensor(lv, gb, C("lvl", P, j).unsqueeze(1).broadcast_to([P, 4, P]),
                                                    ALU.mult), r_lvl)
                            if j == 0:
                                tr.hold()
                                tr.sig(g_.tensor_tensor(mt_of(i, d).rearrange("p (q n) -> p q n", q=4),
                                                        C("ident").unsqueeze(1).broadcast_to([P, 4, P]), lv,
                                                        ALU.subtract), r_mt0)
                                tr.hold()
                    if i == 1:
                        pool.wait_ge(r_st, 5 * l + 1)
                        pool.dma_start(rwkv_out[l], fin_rw[:]).then_inc(s_out, 16)

            def norm(group, w, b, modulated):
                for k in range(KT):
                    pool.wait_ge(s_hat, KT * group + k + 1)
                    if modulated:
                        pool.wait_ge(s_raw, KT * (group + 1) + k + 1)
                    tr.sig(g_.tensor_scalar(xt[:, k], xt[:, k], V(w, k), V(b, k), ALU.mult, ALU.add), s_ln)

            for l in range(DEPTH):
                small_loads(l)
                pads()
                pool.wait_ge(s_free[0], (N_DENSE * l + TV) // 2 + 1)
                pool.wait_ge(s_free[1], (N_DENSE // 2 - FFN_T) * l + TK_ // 2 + 1)
                pool.dma_start(k_out[l], proj[:, TK_, 0:CTX]).then_inc(s_out, 16)
                pool.dma_start(v_out[l], proj[:, TV, 0:CTX]).then_inc(s_out, 16)
                bar()
                bar()
                ssd(l)
                pool.wait_ge(s_out, 64 * l + 48)
                bar()
                rwkv_features(l)
                bar()
                rwkv_scan(l)
                bar()
                pool.wait_ge(s_out, 64 * l + 64)
                norm(2 * l, "ln1w", "ln1b", True)
                norm(2 * l + 1, "ln2w", "ln2b", l + 1 < DEPTH)
                bar()



def constants():
    c = np.zeros((P, NCON), np.float32)

    def put(name, m, j=0):
        c[:, CON[name] + j * m.shape[1]:CON[name] + (j + 1) * m.shape[1]] = m

    i = np.arange(P)
    row, col = i[:, None], i[None, :]
    put("ident", np.eye(P))
    put("ones", np.full((P, P), 1.0 / D))
    put("blk", (row // HD == col // HD).astype(np.float32))
    perm = np.zeros((P, P))
    for m in range(P):
        if m % 32 < 16:
            perm[m + 16, m] = -1.0
        else:
            perm[m - 16, m] = 1.0
    put("perm", perm)
    put("incf", row <= col)
    put("incb", row >= col)
    put("strf", row < col)
    put("strb", row > col)
    for j in range(7):
        b = 2 ** j
        put("lvl", (row // (2 * b) == col // (2 * b)) & (row // b != col // b), j)
    put("gmf", np.concatenate([row < col, row <= col], 1))
    put("gmb", np.concatenate([row > col, row >= col], 1))
    put("bprev", np.where(col >= row, 0.0, NEG_BIG))
    put("bnext", np.where(col <= row, 0.0, NEG_BIG))
    half = HD // 2
    inv = (1.0 / (np.float32(ROPE_BASE) ** (np.arange(0, half, 2, dtype=np.float32) / np.float32(half)))).astype(np.float32)
    t = np.arange(LAT)
    pos = np.stack([t // GRID_W, t % GRID_W]).astype(np.float32)
    dd = i % HD
    ang = (pos[dd // half] * inv[dd % (half // 2)][:, None]).astype(np.float32)
    put("cos", np.cos(ang))
    put("sin", np.sin(ang))
    put("reset", np.broadcast_to((np.arange(TOK) % P != 0), (P, TOK)))
    put("eps", np.broadcast_to(np.array([LN_EPS, 1e-12, GN_EPS, 0.0], np.float32), (P, 4)))
    return c


def kernel(**inputs):
    import concourse.bacc as bacc
    from concourse.bass_utils import run_bass_kernel_spmd

    x = {k: np.asarray(v) for k, v in inputs.items()}
    L = DEPTH

    def cat(parts, axis):
        return np.concatenate(parts, axis=axis)

    def head_pairs(a, axis):
        s = np.split(a, ATT_H, axis=axis)
        return cat([s[t + 3 * j] for t in range(3) for j in range(2)], axis)

    def slots(w):
        k, n = w.shape
        return w.reshape(k // P, P, n // 256, 256).transpose(2, 1, 0, 3)

    def columns(a):
        return a.reshape(-1, P).T

    packed = {}
    for l in range(L):
        wi = x["w_in"][l]
        wi = cat([head_pairs(wi[:, :384], 1), wi[:, 384:1664], wi[:, 1676:2700], wi[:, 1664:1676],
                  np.zeros((D, 2816 - 2700), np.float32)], 1)
        packed["in", l] = slots(wi)
        packed["mod", l] = slots(x["w_mod"][l])
        packed["out", l] = slots(cat([head_pairs(x["w_out"][l][:384], 0), x["w_out"][l][384:]], 0))
        fi = x["ffn_w_in"][l]
        n = FFN_T * P
        packed["up", l] = slots(np.stack([fi[:, :n].reshape(D, FFN_T, P), fi[:, n:].reshape(D, FFN_T, P)], 2)
                                .reshape(D, 2 * n))
        fo = cat([x["ffn_w_out"][l], np.zeros((2 * P, D), np.float32)], 0)
        packed["down", l] = fo.reshape(3, 8, P, 4, 256).transpose(3, 0, 2, 1, 4).reshape(12, P, 8, 256)
    order = stream_order()
    stream = np.stack([packed[kind, l][i].reshape(P, SLOT) for kind, l, i in order])

    tok = cat([x["x_prompt"][0], x["x_sample"][0]], 0)
    xin = tok.T.reshape(KT, P, TOK).transpose(1, 0, 2)
    conds = np.stack([x["c_ctx"].reshape(KT, P).T, x["c"][0].reshape(KT, P).T], 2)
    bmods = np.stack([columns(x["b_mod"][l]) for l in range(L)], 1)
    vecs = np.stack([cat([columns(x["ssd_conv_w"][l]), columns(x["ssd_conv_b"][l]),
                          columns(np.repeat(x["ssd_d"][l], HD)), columns(x["ssd_norm_w"][l]),
                          columns(x["rwkv_mu"][l]), columns(x["rwkv_w0"][l]), columns(x["rwkv_a0"][l]),
                          columns(x["rwkv_k_k"][l]), columns(x["rwkv_k_a"][l]), columns(x["rwkv_r_k"][l]),
                          columns(x["rwkv_gn_w"][l]), columns(x["rwkv_gn_b"][l]),
                          columns(x["ln1_w"][l]), columns(x["ln1_b"][l]), columns(x["ln2_w"][l]),
                          columns(x["ln2_b"][l])], 1) for l in range(L)])
    rows = np.stack([np.broadcast_to(cat([head_pairs(x["attn_sink"][l], 0), x["ssd_dt_bias"][l].ravel(),
                                          x["ssd_a_log"][l].ravel()], 0), (P, NROW)) for l in range(L)])
    kctx = x["cache_k"][0].transpose(0, 2, 3, 1).reshape(L, P, CTX)
    vctx = x["cache_v"][0].reshape(L, CTX, P)
    lora = cat([x["rwkv_w_up"].transpose(0, 2, 1, 3), x["rwkv_a_up"].transpose(0, 2, 1, 3)], 1)
    gup = x["rwkv_g_up"]
    ssd0 = x["state_ssd"][0].reshape(L, 2, 2, 3, HD, HD).transpose(0, 2, 5, 1, 3, 4).reshape(L, P, 2, 192)
    rwkv0 = x["state_rwkv"][0].reshape(L, 2, 2, 2, HD, HD).transpose(0, 3, 5, 1, 2, 4).reshape(L, P, 256)

    arrays = {"stream": stream, "xin": xin, "consts": constants(), "conds": conds, "bmods": bmods, "vecs": vecs,
              "rows": rows, "kctx": kctx, "vctx": vctx, "lora": lora, "gup": gup, "ssd0": ssd0, "rwkv0": rwkv0}
    arrays = {k: np.ascontiguousarray(v) for k, v in arrays.items()}
    outs = {"y_out": (P, KT, TOK), "k_out": (L, P, CTX), "v_out": (L, P, CTX), "ssd_out": (L, P, 384),
            "rwkv_out": (L, P, 256)}

    nc = bacc.Bacc("TRN2", target_bir_lowering=False, num_devices=1)
    args = [nc.dram_tensor(k, v.shape, F32, kind="ExternalInput").ap() for k, v in arrays.items()]
    args += [nc.dram_tensor(k, s, F32, kind="ExternalOutput").ap() for k, s in outs.items()]
    build(nc, *args)
    r = run_bass_kernel_spmd(nc, [arrays], core_ids=[0]).results[0]

    y = r["y_out"].transpose(2, 1, 0).reshape(TOK, D)
    new_k = r["k_out"].transpose(0, 2, 1).reshape(1, L, CTX, 2, HD)
    new_v = r["v_out"].transpose(0, 2, 1).reshape(1, L, CTX, 2, HD)
    new_ssd = r["ssd_out"].reshape(L, 2, HD, 2, 3, HD).transpose(0, 3, 1, 4, 5, 2).reshape(1, L, 2, 6, HD, HD)
    new_rwkv = r["rwkv_out"].reshape(L, 2, HD, 2, 2, HD).transpose(0, 3, 4, 1, 5, 2).reshape(1, L, 2, 4, HD, HD)
    return (y[None, :CTX], y[None, CTX:], new_k, new_v, new_ssd, new_rwkv)
```
